# Optimizing a Trainium2 kernel written in Bass

```python
import math
import jax
import jax.numpy as jnp
from jax import lax
import numpy as np

D_MODEL = 1024
BATCH = 1
SEQ = 256
DEPTH = 1

GRID_W = 64
CTX_LEN = 256
D_MIX = D_MODEL
D_GROUP = D_MIX // 4
N_MOD = 6

FOURIER_HEADS = 4
FOURIER_HD = D_GROUP // FOURIER_HEADS

S5_CH = 16
S5_GROUPS = D_GROUP // S5_CH
S5_STATE = 64

GLA_HEADS = 4
GLA_DK = D_GROUP // (2 * GLA_HEADS)
GLA_DV = D_GROUP // GLA_HEADS
GLA_RANK = 16
GLA_TAU = 16.0
GLA_CHUNK = 64

SSD_HEADS = 4
SSD_HD = D_GROUP // SSD_HEADS
SSD_GROUPS = 2
SSD_STATE = 64
SSD_CONV = 5
SSD_CHUNK = 64
SSD_XBC = D_GROUP + 2 * SSD_GROUPS * SSD_STATE

N_EXPERTS = 32
TOP_K = 4
D_EXPERT = D_MODEL
SWIGLU_LIMIT = 7.0
SWIGLU_ALPHA = 1.702
MOE_BLOCK = 256

EPS = 1e-6

IN_SPLIT = (D_GROUP, D_GROUP, GLA_HEADS * GLA_DK, GLA_HEADS * GLA_DK, D_GROUP, D_GROUP,
            2 * GLA_RANK, D_GROUP, SSD_XBC, 2 * SSD_HEADS)
D_IN_PROJ = (2 * D_GROUP + 2 * GLA_HEADS * GLA_DK + 2 * D_GROUP + 2 * GLA_RANK
             + D_GROUP + SSD_XBC + 2 * SSD_HEADS)

kernel_name = 'hybrid_flow_backbone_fourier_s5_gla_ssd_moe'

def _rmsnorm(x, g):
    xf = x.astype(jnp.float32)
    y = xf * lax.rsqrt(jnp.mean(xf * xf, axis=-1, keepdims=True) + EPS)
    return (y * g.astype(jnp.float32)).astype(x.dtype)

def _modulate(h, shift, scale):
    return h * (1.0 + scale) + shift

def _ada(cond, w, b):
    m = cond @ w + b
    return [t[:, None, :] for t in jnp.split(m, N_MOD, axis=-1)]

def _split_in(p):
    return jnp.split(p, np.cumsum(IN_SPLIT)[:-1].tolist(), axis=-1)

def _flip(t, rev):
    return jnp.flip(t, axis=1) if rev else t

def _tril(n):
    return jnp.tril(jnp.ones((n, n), dtype=bool))

def fourier_mixer(u, w):
    bsz, seq_len, _ = u.shape
    uh = u.astype(jnp.float32).reshape(bsz, seq_len, FOURIER_HEADS, FOURIER_HD)
    f = jnp.fft.fft2(uh, axes=(1, 3), norm='ortho').real
    return (f.reshape(bsz, seq_len, D_GROUP) @ w.astype(jnp.float32)).astype(u.dtype)

def _s5_combine(left, right):
    a_l, b_l = left
    a_r, b_r = right
    return a_r * a_l, a_r * b_l + b_r

def _s5_scan(a_bar, lam_dt, bu, h0):
    seq_len = bu.shape[1]
    a = jnp.broadcast_to(a_bar, bu.shape)
    _, h = lax.associative_scan(_s5_combine, (a, bu), axis=1)
    if h0 is None:
        return h
    steps = jnp.arange(1, seq_len + 1, dtype=jnp.float32)[:, None, None]
    return h + jnp.exp(lam_dt * steps)[None] * h0[:, None]

def s5_mixer(u_c, u_l, lam_re, lam_im, log_dt, b_re, b_im, c_re, c_im, d_skip, w_glu, ctx_out):
    f32 = jnp.float32

    def groups(u):
        return u.astype(f32).reshape(u.shape[0], u.shape[1], S5_GROUPS, S5_CH)

    uc, ul = groups(u_c), groups(u_l)
    y_c, y_l = [], []
    for r in range(2):
        rev = r == 1
        lam = lax.complex(lam_re[r].astype(f32), lam_im[r].astype(f32))
        lam_dt = lam * jnp.exp(log_dt[r].astype(f32))[:, None]
        a_bar = jnp.exp(lam_dt)
        b_bar = ((a_bar - 1.0) / lam)[..., None] * lax.complex(b_re[r].astype(f32), b_im[r].astype(f32))
        c_mat = lax.complex(c_re[r].astype(f32), c_im[r].astype(f32))
        h_c = _s5_scan(a_bar, lam_dt, jnp.einsum('blgh,gph->blgp', _flip(uc, rev), b_bar), None)
        h_l = _s5_scan(a_bar, lam_dt, jnp.einsum('blgh,gph->blgp', _flip(ul, rev), b_bar), h_c[:, -1])
        y_l.append(_flip(jnp.einsum('blgp,ghp->blgh', h_l, c_mat).real, rev))
        if ctx_out:
            y_c.append(_flip(jnp.einsum('blgp,ghp->blgh', h_c, c_mat).real, rev))

    def finish(u, u_g, ys):
        y = (ys[0] + ys[1] + d_skip.astype(f32).reshape(S5_GROUPS, S5_CH) * u_g).reshape(u.shape)
        act = jax.nn.gelu(y)
        return (act * jax.nn.sigmoid(act @ w_glu.astype(f32))).astype(u.dtype)

    return (finish(u_c, uc, y_c) if ctx_out else None), finish(u_l, ul, y_l)

def _chunk_states(k_dec, v, chunk_decay, s0):
    ds = jnp.einsum('bnchk,bnchv->bnhkv', k_dec, v)

    def step(s, inp):
        dec, d = inp
        return dec[..., None] * s + d, s

    s_final, s_enter = lax.scan(step, s0, (jnp.moveaxis(chunk_decay, 1, 0), jnp.moveaxis(ds, 1, 0)))
    return jnp.moveaxis(s_enter, 0, 1), s_final

def _gla_direction(q, k, v, log_a, s0, with_out):
    bsz, seq_len, nh, dk = q.shape
    csz = min(GLA_CHUNK, seq_len)
    nc = seq_len // csz
    q, k, v, log_a = (t.reshape(bsz, nc, csz, nh, t.shape[-1]) for t in (q, k, v, log_a))
    b = jnp.cumsum(log_a, axis=2)
    b_last = b[:, :, -1]
    s_enter, s_final = _chunk_states(k * jnp.exp(b_last[:, :, None] - b), v, jnp.exp(b_last), s0)
    if not with_out:
        return None, s_final
    q_in = q * jnp.exp(b)
    k_in = k * jnp.exp(-b)
    att = jnp.where(_tril(csz), jnp.einsum('bnthk,bnshk->bnhts', q_in, k_in), 0.0)
    o = (jnp.einsum('bnhts,bnshv->bnthv', att, v)
         + jnp.einsum('bnthk,bnhkv->bnthv', q_in, s_enter))
    return o.reshape(bsz, seq_len, nh, v.shape[-1]), s_final

def gla_mixer(pc, pl, a2, a_b, norm_g, ctx_out):
    f32 = jnp.float32

    def prep(p):
        q, k, v, r, a1 = p
        bsz, seq_len, _ = q.shape
        z = jnp.einsum('blzr,zrk->blzk', a1.astype(f32).reshape(bsz, seq_len, 2, GLA_RANK),
                       a2.astype(f32)) + a_b.astype(f32)
        log_a = (jax.nn.log_sigmoid(z) / GLA_TAU).reshape(bsz, seq_len, 2, GLA_HEADS, GLA_DK)
        qh = q.astype(f32).reshape(bsz, seq_len, GLA_HEADS, GLA_DK) * GLA_DK ** -0.5
        kh = k.astype(f32).reshape(bsz, seq_len, GLA_HEADS, GLA_DK)
        vh = v.astype(f32).reshape(bsz, seq_len, GLA_HEADS, GLA_DV)
        return qh, kh, vh, log_a, r

    qc, kc, vc, lac, rc = prep(pc)
    ql, kl, vl, lal, rl = prep(pl)
    s0 = jnp.zeros((qc.shape[0], GLA_HEADS, GLA_DK, GLA_DV), f32)
    o_c, o_l = [], []
    for r in range(2):
        rev = r == 1
        oc, s_c = _gla_direction(_flip(qc, rev), _flip(kc, rev), _flip(vc, rev), _flip(lac[:, :, r], rev), s0, ctx_out)
        ol, _ = _gla_direction(_flip(ql, rev), _flip(kl, rev), _flip(vl, rev), _flip(lal[:, :, r], rev), s_c, True)
        o_l.append(_flip(ol, rev))
        if ctx_out:
            o_c.append(_flip(oc, rev))

    def finish(os_, r):
        o = _rmsnorm(os_[0] + os_[1], norm_g)
        return (o.reshape(r.shape) * jax.nn.silu(r.astype(f32))).astype(r.dtype)

    return (finish(o_c, rc) if ctx_out else None), finish(o_l, rl)

def _dwconv(x, w, b):
    y = lax.conv_general_dilated(x, w[:, None, :], window_strides=(1,),
                                 padding=[(SSD_CONV // 2, SSD_CONV // 2)],
                                 dimension_numbers=('NWC', 'WIO', 'NWC'),
                                 feature_group_count=x.shape[-1])
    return y + b

def _ssd_direction(x, bm, cm, dt, a, s0, with_out):
    bsz, seq_len, nh, hd = x.shape
    csz = min(SSD_CHUNK, seq_len)
    nc = seq_len // csz
    x, bm, cm = (t.reshape(bsz, nc, csz, nh, t.shape[-1]) for t in (x, bm, cm))
    dt = dt.reshape(bsz, nc, csz, nh)
    cum = jnp.cumsum(dt * a, axis=2)
    xdt = x * dt[..., None]
    s_enter, s_final = _chunk_states(bm * jnp.exp(cum[:, :, -1:] - cum)[..., None], xdt,
                                     jnp.exp(cum[:, :, -1])[..., None], s0)
    if not with_out:
        return None, s_final
    seg = cum[:, :, :, None, :] - cum[:, :, None, :, :]
    decay = jnp.exp(jnp.where(_tril(csz)[..., None], seg, -jnp.inf))
    scores = jnp.einsum('bnthd,bnshd->bntsh', cm, bm) * decay
    y = (jnp.einsum('bntsh,bnshp->bnthp', scores, xdt)
         + jnp.einsum('bnthd,bnhdp->bnthp', cm * jnp.exp(cum)[..., None], s_enter))
    return y.reshape(bsz, seq_len, nh, hd), s_final

def ssd_mixer(pc, pl, conv_w, conv_b, a_log, dt_bias, d_skip, norm_g, ctx_out):
    f32 = jnp.float32
    w, bconv = conv_w.astype(f32), conv_b.astype(f32)

    def conv_ctx(t):
        return _dwconv(t, w, bconv)

    def conv_lat(t):
        bsz, seq_len, ch = t.shape
        rows = seq_len // GRID_W
        return _dwconv(t.reshape(bsz * rows, GRID_W, ch), w, bconv).reshape(bsz, seq_len, ch)

    def prep(p, conv):
        z, xbc, dt_raw = p
        bsz, seq_len, _ = z.shape
        xbc = jax.nn.silu(conv(xbc.astype(f32)))
        xs, bm, cm = jnp.split(xbc, [D_GROUP, D_GROUP + SSD_GROUPS * SSD_STATE], axis=-1)
        rep = SSD_HEADS // SSD_GROUPS

        def grp(t):
            return jnp.repeat(t.reshape(bsz, seq_len, SSD_GROUPS, SSD_STATE), rep, axis=2)

        dt = jax.nn.softplus(dt_raw.astype(f32).reshape(bsz, seq_len, 2, SSD_HEADS) + dt_bias.astype(f32))
        return xs.reshape(bsz, seq_len, SSD_HEADS, SSD_HD), grp(bm), grp(cm), dt, z

    xc, bc, cc, dtc, zc = prep(pc, conv_ctx)
    xl, bl, cl, dtl, zl = prep(pl, conv_lat)
    a = -jnp.exp(a_log.astype(f32))
    s0 = jnp.zeros((xc.shape[0], SSD_HEADS, SSD_STATE, SSD_HD), f32)
    y_c, y_l = [], []
    for r in range(2):
        rev = r == 1
        yc, s_c = _ssd_direction(_flip(xc, rev), _flip(bc, rev), _flip(cc, rev), _flip(dtc[:, :, r], rev), a[r], s0, ctx_out)
        yl, _ = _ssd_direction(_flip(xl, rev), _flip(bl, rev), _flip(cl, rev), _flip(dtl[:, :, r], rev), a[r], s_c, True)
        y_l.append(_flip(yl, rev))
        if ctx_out:
            y_c.append(_flip(yc, rev))
    dsk = d_skip.astype(f32)

    def finish(x_h, ys, z):
        y = (ys[0] + ys[1] + dsk[:, None] * x_h).reshape(z.shape)
        return _rmsnorm(y * jax.nn.silu(z.astype(f32)), norm_g).astype(z.dtype)

    return (finish(xc, y_c, zc) if ctx_out else None), finish(xl, y_l, zl)

def moe_ffn(h, router_w, router_b, w_gu, b_gu, w_dn, b_dn):
    n_tok, dm = h.shape
    logits = (h @ router_w + router_b).astype(jnp.float32)
    top_logit, top_idx = lax.top_k(logits, TOP_K)
    gates = jax.nn.softmax(top_logit, axis=-1)
    e_flat = top_idx.reshape(-1)
    order = jnp.argsort(e_flat)
    e_sorted = e_flat[order]
    tok_sorted = order // TOP_K
    counts = jnp.bincount(e_flat, length=N_EXPERTS)
    padded = (counts + MOE_BLOCK - 1) // MOE_BLOCK * MOE_BLOCK
    seg_start = jnp.cumsum(counts) - counts
    pad_end = jnp.cumsum(padded)
    dest = (pad_end - padded)[e_sorted] + jnp.arange(n_tok * TOP_K) - seg_start[e_sorted]
    n_blocks = -(-(n_tok * TOP_K) // MOE_BLOCK) + N_EXPERTS
    buf = jnp.zeros((n_blocks * MOE_BLOCK, dm), h.dtype).at[dest].set(h[tok_sorted])
    block_expert = jnp.minimum(jnp.searchsorted(pad_end, jnp.arange(n_blocks) * MOE_BLOCK, side='right'),
                               N_EXPERTS - 1)

    def run_block(args):
        xb, e = args
        gu = xb @ w_gu[e] + b_gu[e]
        gate = jnp.minimum(gu[:, 0::2], SWIGLU_LIMIT)
        up = jnp.clip(gu[:, 1::2], -SWIGLU_LIMIT, SWIGLU_LIMIT)
        act = (up + 1.0) * gate * jax.nn.sigmoid(SWIGLU_ALPHA * gate)
        return act @ w_dn[e] + b_dn[e]

    y_buf = lax.map(run_block, (buf.reshape(n_blocks, MOE_BLOCK, dm), block_expert)).reshape(-1, dm)
    y_pairs = y_buf[dest] * gates.reshape(-1)[order][:, None].astype(h.dtype)
    return jnp.zeros((n_tok, dm), h.dtype).at[tok_sorted].add(y_pairs)

def setup_inputs(seed: int = 0) -> dict:
    key = jax.random.key(seed)
    ks = jax.random.split(key, 36)
    f32 = jnp.float32
    nl = DEPTH

    def nrm(k, shape, scale):
        return jax.random.normal(k, shape, f32) * scale

    def gain(k, shape):
        return 1.0 + nrm(k, shape, 0.05)

    s5_n = jnp.arange(S5_STATE, dtype=f32)
    ssd_dt = jnp.exp(jax.random.uniform(ks[26], (nl, 2, SSD_HEADS), f32, math.log(1e-3), math.log(1e-1)))
    return {
        'x': nrm(ks[0], (BATCH, SEQ, D_MODEL), 1.0),
        'c': nrm(ks[1], (BATCH, D_MODEL), 1.0),
        'ctx': nrm(ks[2], (BATCH, CTX_LEN, D_MODEL), 1.0),
        'c_ctx': nrm(ks[3], (D_MODEL,), 1.0),
        'ada_w': nrm(ks[4], (nl, D_MODEL, N_MOD * D_MODEL), 0.5 * D_MODEL ** -0.5),
        'ada_b': nrm(ks[5], (nl, N_MOD * D_MODEL), 0.02),
        'norm_mix_g': gain(ks[6], (nl, D_MODEL)),
        'norm_ffn_g': gain(ks[7], (nl, D_MODEL)),
        'w_in': nrm(ks[8], (nl, D_MODEL, D_IN_PROJ), D_MODEL ** -0.5),
        'w_out': nrm(ks[9], (nl, D_MIX, D_MODEL), D_MIX ** -0.5),
        'four_w': nrm(ks[10], (nl, D_GROUP, D_GROUP), D_GROUP ** -0.5),
        's5_lam_re': -0.5 + nrm(ks[11], (nl, 2, S5_GROUPS, S5_STATE), 0.01),
        's5_lam_im': math.pi * s5_n + nrm(ks[12], (nl, 2, S5_GROUPS, S5_STATE), 0.01),
        's5_log_dt': jax.random.uniform(ks[13], (nl, 2, S5_GROUPS), f32, math.log(1e-3), math.log(1e-1)),
        's5_b_re': nrm(ks[14], (nl, 2, S5_GROUPS, S5_STATE, S5_CH), (2 * S5_CH) ** -0.5),
        's5_b_im': nrm(ks[15], (nl, 2, S5_GROUPS, S5_STATE, S5_CH), (2 * S5_CH) ** -0.5),
        's5_c_re': nrm(ks[16], (nl, 2, S5_GROUPS, S5_CH, S5_STATE), S5_STATE ** -0.5),
        's5_c_im': nrm(ks[17], (nl, 2, S5_GROUPS, S5_CH, S5_STATE), S5_STATE ** -0.5),
        's5_d': nrm(ks[18], (nl, D_GROUP), 1.0),
        's5_w_glu': nrm(ks[19], (nl, D_GROUP, D_GROUP), D_GROUP ** -0.5),
        'gla_a2': nrm(ks[20], (nl, 2, GLA_RANK, GLA_HEADS * GLA_DK), GLA_RANK ** -0.5),
        'gla_a_b': nrm(ks[21], (nl, 2, GLA_HEADS * GLA_DK), 0.1),
        'gla_norm_g': gain(ks[22], (nl, GLA_DV)),
        'ssd_conv_w': nrm(ks[23], (nl, SSD_CONV, SSD_XBC), SSD_CONV ** -0.5),
        'ssd_conv_b': nrm(ks[24], (nl, SSD_XBC), 0.02),
        'ssd_a_log': jnp.log(jax.random.uniform(ks[25], (nl, 2, SSD_HEADS), f32, 1.0, 16.0)),
        'ssd_dt_bias': ssd_dt + jnp.log(-jnp.expm1(-ssd_dt)),
        'ssd_d': 1.0 + nrm(ks[27], (nl, SSD_HEADS), 0.1),
        'ssd_norm_g': gain(ks[28], (nl, D_GROUP)),
        'router_w': nrm(ks[29], (nl, D_MODEL, N_EXPERTS), D_MODEL ** -0.5),
        'router_b': nrm(ks[30], (nl, N_EXPERTS), 0.01),
        'exp_w_gu': nrm(ks[31], (nl, N_EXPERTS, D_MODEL, 2 * D_EXPERT), D_MODEL ** -0.5),
        'exp_b_gu': nrm(ks[32], (nl, N_EXPERTS, 2 * D_EXPERT), 0.02),
        'exp_w_dn': nrm(ks[33], (nl, N_EXPERTS, D_EXPERT, D_MODEL), D_EXPERT ** -0.5),
        'exp_b_dn': nrm(ks[34], (nl, N_EXPERTS, D_MODEL), 0.02),
        'final_g': gain(ks[35], (D_MODEL,)),
    }

def reference(x, c, ctx, c_ctx, ada_w, ada_b, norm_mix_g, norm_ffn_g, w_in, w_out, four_w,
              s5_lam_re, s5_lam_im, s5_log_dt, s5_b_re, s5_b_im, s5_c_re, s5_c_im, s5_d, s5_w_glu,
              gla_a2, gla_a_b, gla_norm_g, ssd_conv_w, ssd_conv_b, ssd_a_log, ssd_dt_bias, ssd_d,
              ssd_norm_g, router_w, router_b, exp_w_gu, exp_b_gu, exp_w_dn, exp_b_dn, final_g):
    x_lat, x_ctx = x, ctx
    cond_lat = jax.nn.silu(c)
    cond_ctx = jax.nn.silu(c_ctx)[None, :]
    for i in range(DEPTH):
        ctx_out = i < DEPTH - 1
        m_l = _ada(cond_lat, ada_w[i], ada_b[i])
        m_c = _ada(cond_ctx, ada_w[i], ada_b[i])
        pl = _split_in(_modulate(_rmsnorm(x_lat, norm_mix_g[i]), m_l[0], m_l[1]) @ w_in[i])
        pc = _split_in(_modulate(_rmsnorm(x_ctx, norm_mix_g[i]), m_c[0], m_c[1]) @ w_in[i])
        s5_c, s5_l = s5_mixer(pc[1], pl[1], s5_lam_re[i], s5_lam_im[i], s5_log_dt[i], s5_b_re[i], s5_b_im[i],
                              s5_c_re[i], s5_c_im[i], s5_d[i], s5_w_glu[i], ctx_out)
        gla_c, gla_l = gla_mixer(pc[2:7], pl[2:7], gla_a2[i], gla_a_b[i], gla_norm_g[i], ctx_out)
        ssd_c, ssd_l = ssd_mixer(pc[7:], pl[7:], ssd_conv_w[i], ssd_conv_b[i], ssd_a_log[i], ssd_dt_bias[i],
                                 ssd_d[i], ssd_norm_g[i], ctx_out)
        mix_l = jnp.concatenate([fourier_mixer(pl[0], four_w[i]), s5_l, gla_l, ssd_l], axis=-1)
        x_lat = x_lat + m_l[2] * (mix_l @ w_out[i])
        h_l = _modulate(_rmsnorm(x_lat, norm_ffn_g[i]), m_l[3], m_l[4])
        if ctx_out:
            mix_c = jnp.concatenate([fourier_mixer(pc[0], four_w[i]), s5_c, gla_c, ssd_c], axis=-1)
            x_ctx = x_ctx + m_c[2] * (mix_c @ w_out[i])
            h_c = _modulate(_rmsnorm(x_ctx, norm_ffn_g[i]), m_c[3], m_c[4])
            n_c = h_c.shape[0] * h_c.shape[1]
            f = moe_ffn(jnp.concatenate([h_c.reshape(n_c, D_MODEL), h_l.reshape(-1, D_MODEL)], axis=0),
                        router_w[i], router_b[i], exp_w_gu[i], exp_b_gu[i], exp_w_dn[i], exp_b_dn[i])
            x_ctx = x_ctx + m_c[5] * f[:n_c].reshape(x_ctx.shape)
            f_l = f[n_c:].reshape(x_lat.shape)
        else:
            f_l = moe_ffn(h_l.reshape(-1, D_MODEL), router_w[i], router_b[i], exp_w_gu[i], exp_b_gu[i],
                          exp_w_dn[i], exp_b_dn[i]).reshape(x_lat.shape)
        x_lat = x_lat + m_l[5] * f_l
    return _rmsnorm(x_lat, final_g)


_drawn_inputs = setup_inputs


def setup_inputs(seed=0):
    import zlib

    import numpy as np

    out = dict(_drawn_inputs(seed))
    spreads = {}
    factors = {'c_ctx': 2.928,
     'norm_mix_g': 2.721,
     's5_lam_re': 64.0,
     's5_lam_im': 29.272,
     's5_log_dt': 37.344,
     's5_b_re': 38.696,
     's5_b_im': 40.808,
     's5_c_re': 35.616,
     's5_c_im': 36.704,
     'gla_a_b': 6.047,
     'gla_norm_g': 8.0,
     'ssd_conv_b': 22.021,
     'ssd_d': 39.296,
     'ssd_norm_g': 17.896,
     'router_b': 27.407,
     'exp_b_gu': 34.4,
     'exp_b_dn': 41.699,
     'norm_ffn_g': 4.637}
    for name, (base, spread) in spreads.items():
        noise = np.random.default_rng([zlib.crc32(name.encode()), seed]).standard_normal(out[name].shape)
        drawn = base * np.exp(spread * noise) if base else spread * noise
        out[name] = jnp.asarray(drawn.astype(out[name].dtype))
    for name, factor in factors.items():
        out[name] = (out[name] * factor).astype(out[name].dtype)
    return out
```

```python
from contextlib import ExitStack

import numpy as np

import concourse.bass as bass
from concourse import mybir

F32 = mybir.dt.float32
I32 = mybir.dt.int32
ALU = mybir.AluOpType
ACT = mybir.ActivationFunctionType
AX = mybir.AxisListType

P = 128
D = 1024
KT = D // P
NCTX = 256
NLAT = 256
NTOK = NCTX + NLAT
EPS = 1e-6
NMOD = 6
NE = 32
TOPK = 4
CAP = 64
NI = 50
LIMIT = 7.0
ALPHA = 1.702

CH = 16
NG = 16
Q = 8
NCH = NTOK // Q
LCH = NLAT // Q
CSZ = 64
NCK = NTOK // CSZ
GATE_TAU = 16.0
GLA_DK = 32

SLOT = 2048
NSLOT = 12
FR = 5
MIX = (NSLOT - FR) * SLOT

_C = {}


def _layout():
    at = 0
    for name, n in (("ident", 128), ("ones", 128), ("blk64", 128), ("cbd", 256), ("cseq", 512), ("sseq", 512),
                    ("sel", 8 * 240), ("tri", 2 * 128), ("neg", 2 * 128), ("scan", 512), ("iota", 2 * CAP),
                    ("rows", 8 * 128), ("incl", 128), ("headm", 4), ("halfm", 2), ("items", NI), ("evec", 1),
                    ("first", 1), ("strict", 32)):
        _C[name] = (at, n)
        at += n
    return at


NCONST = _layout()
ROW0 = 64


def shape_constants():
    c = np.zeros((P, NCONST), np.float32)

    def put(name, a):
        at, n = _C[name]
        a = np.asarray(a, np.float64).reshape(a.shape[0], -1)
        c[:a.shape[0], at:at + n] = a

    i = np.arange(P)
    put("ident", np.eye(P))
    put("ones", np.ones((P, P)))
    put("blk64", (i[:, None] // 64 == i[None, :] // 64) * 1.0)
    same = i[:, None] // 64 == i[None, :] // 64
    ang = 2 * np.pi * ((i[:, None] % 64) * (i[None, :] % 64) % 64) / 64
    put("cbd", np.concatenate([np.cos(ang) * same, np.sin(ang) * same], 1) / 128.0)
    t = np.arange(NLAT)
    angs = 2 * np.pi * (t[:, None] * t[None, :] % NLAT) / NLAT
    put("cseq", np.cos(angs).reshape(2, P, NLAT).transpose(1, 0, 2))
    put("sseq", -np.sin(angs).reshape(2, P, NLAT).transpose(1, 0, 2))
    sel = np.zeros((P, 8, 240))
    for b in range(8):
        for k in range(CH):
            sel[CH * b + k, b, 112 + k] = 1
    put("sel", sel)
    fwd = same & (i[:, None] <= i[None, :])
    rev = same & (i[:, None] >= i[None, :])
    put("tri", np.stack([fwd, rev], 1) * 1.0)
    put("neg", (1.0 - np.stack([fwd, rev], 1)) * -1e30)
    put("scan", np.broadcast_to((np.arange(NTOK) % CSZ != 0) * 1.0, (P, NTOK)))
    put("iota", np.broadcast_to(np.arange(2 * CAP) % CAP + 1, (P, 2 * CAP)))
    rows = np.zeros((P, 8, P))
    for r in range(8):
        rows[ROW0 + 32 * (r // 4) + r % 4, r] = 1
    put("rows", rows)
    put("incl", (i[:, None] <= i[None, :]) * 1.0)
    put("headm", (i[:, None] // 32 == np.arange(4)[None]) * 1.0)
    put("halfm", (i[:, None] // 64 == np.arange(2)[None]) * 1.0)
    put("items", np.broadcast_to(np.arange(-1, NI - 1), (P, NI)))
    put("evec", i[:, None] * 1.0)
    put("first", (i[:, None] == 0) * 1.0)
    e = np.arange(NE)
    put("strict", (e[:, None] < e[None, :]) * 1.0)
    return c


R_C, R_CCTX, R_GMIX, R_GFFN, R_ADAB, R_S5D, R_SSDG, R_CONVB, R_CONVW, R_GLAB, R_GLAG, R_DTB, R_ALOG = (
    0, 8, 16, 24, 32, 80, 82, 84, 88, 108, 110, 111, 112)
NPAR = 113
PAIR_D = 64
NPAR2 = PAIR_D + 2

W_FOUR, W_U, W_QK, W_V, W_R, W_MISC, W_Z, W_X, W_BC = range(9)
STREAM = ([("ada", b) for b in range(8)] + [("win", b) for b in range(9)] + [("ada", b) for b in range(8, 24)]
          + [("wout", b) for b in range(4)])
AT = {s: n for n, s in enumerate(STREAM)}

BANKED = (
    [("par", "dve"), ("s5par", "dve"), ("cpar0", "act"), ("cpar1", "act")] + [(f"xraw{i}", "act") for i in range(4)]
    + [("ada0", "dve"), ("VT0", "act"), ("VT1", "act"), ("VT2", "act"), ("VT3", "act"), ("VT4", "act"),
       ("VT5", "act"), ("VT6", "act"), ("VT7", "act"), ("Kq", "act")]
    + [(f"xn{k}", "dve") for k in range(KT)]
    + [("four", "act"), ("u0", "act"), ("u1", "act"), ("q", "act"), ("k", "act"), ("v0", "act"), ("v1", "act"),
       ("r", "act"), ("misc", "act"), ("z", "act"), ("x0", "act"), ("x1", "act"), ("B", "act"), ("C", "act")]
    + [("fA0", "act"), ("fA1", "act"), ("fB", "act"), ("fW", "act")]
    + [("U0", "act"), ("U1", "act")] + [(f"D{i}", "act") for i in range(4)]
    + [("zg0", "act"), ("zg1", "act"), ("ada1", "dve")]
    + [("Y", "act"), ("ysel", "dve"), ("glu", "act")]
    + [("kd0", "dve"), ("kd1", "dve")] + [(f"att{i}", "dve") for i in range(4)]
    + [(f"ds{n}", "dve") for n in range(NCK - 1)] + [("og", "dve"), ("gss", "act")]
    + [(f"rT{i}", "dve") for i in range(3)] + [(f"xt{i}", "dve") for i in range(4)]
    + [("decl", "act")] + [(f"rb{i}", "dve") for i in range(4)] + [(f"bc{i}", "dve") for i in range(2)]
    + [(f"sds{n}", "dve") for n in range(NCK - 1)] + [("oy", "dve"), ("yss", "act")]
    + [(f"wo{i}", "dve") for i in range(4)] + [("ss2", "act")] + [(f"h2{i}", "act") for i in range(4)]
    + [("lg", "dve"), ("pos", "dve"), ("pgT", "dve"), ("cnt", "dve"), ("start", "dve"), ("it0", "dve"),
       ("ids", "dve")]
)


class BankRing:

    def __init__(self, psum, filled, emptied):
        self.psum, self.filled, self.emptied = psum, filled, emptied
        self.number, self.count = {}, {}
        seen = {"act": 0, "dve": 0}
        for n, (name, by) in enumerate(BANKED):
            seen[by] += 1
            self.number[name] = n
            self.count[name] = (by, seen[by])
        self.names = [name for name, _ in BANKED]
        self.done = {"pe": 0, "act": 0, "dve": 0}

    def bank(self, name):
        return self.psum[:, self.number[name] % 8, :]

    def wait_free(self, pe, name):
        n = self.number[name]
        assert n == self.done["pe"], name
        self.done["pe"] += 1
        if n >= 8:
            by, count = self.count[self.names[n - 8]]
            pe.wait_ge(self.emptied[by], count)

    def wait_filled(self, eng, name):
        eng.wait_ge(self.filled, self.number[name] + 1)

    def wait_emptied(self, eng, name):
        by, count = self.count[name]
        eng.wait_ge(self.emptied[by], count)

    def mark_filled(self, ins):
        ins.then_inc(self.filled, 1)

    def mark_emptied(self, ins, name, by):
        self.done[by] += 1
        assert self.count[name] == (by, self.done[by]), name
        ins.then_inc(self.emptied[by], 1)


def backbone(nc, t, out):
    ctx = ExitStack()
    with ctx:
        def sb(name, n, dt=F32):
            return ctx.enter_context(nc.sbuf_tensor(name, [P, n], dt))

        def sem(name):
            return ctx.enter_context(nc.semaphore(name))

        psum = ctx.enter_context(nc.psum_tensor("psum", [P, 8, 512], F32))
        arena = sb("arena", NSLOT * SLOT)

        def slot(n):
            return arena[:, n * SLOT:(n + 1) * SLOT]

        def mix(at, n, parts=P):
            assert at + n <= MIX
            return arena[0:parts, FR * SLOT + at:FR * SLOT + at + n]

        const = sb("const", NCONST)

        def con(name, parts=P):
            at, n = _C[name]
            return const[0:parts, at:at + n]

        ident = con("ident")
        xT = sb("xT", KT * NLAT)[:, :].rearrange("p (k t) -> p k t", k=KT)
        mixT = sb("mixT", KT * NLAT)[:, :].rearrange("p (k t) -> p k t", k=KT)
        prm = sb("prm", NPAR)
        s5p = sb("s5p", NPAR2)
        pairs = sb("pairs", 2)
        mod = sb("mod", 96)[:, :].rearrange("p (t c) -> p t c", c=2)
        cond = sb("cond", 16)[:, :].rearrange("p (k c) -> p k c", c=2)
        tiny = sb("tiny", 160)
        hbuf = sb("hbuf", KT * NTOK)
        hT = hbuf[:, :].rearrange("p (k t) -> p k t", k=KT)
        proj = sb("proj", 6992)
        small = sb("small", 4600)
        neghalf = sb("neghalf", 1)
        ids = ctx.enter_context(nc.sbuf_tensor("ids", [1, NI + 1], I32))
        a2 = sb("a2", 256)

        at = [0]

        def part(n):
            at[0] += n
            return proj[:, at[0] - n:at[0]]

        fourT = part(512).rearrange("p (a t) -> p a t", a=2)
        uT = part(1024).rearrange("p (a t) -> p a t", a=2)
        qT = part(256)
        kTt = part(512)
        vTM = part(1024).rearrange("p (a t) -> p a t", a=4)
        rT = part(512).rearrange("p (a t) -> p a t", a=2)
        miscT = part(512)
        zT = part(512).rearrange("p (a t) -> p a t", a=2)
        PADW = NCTX + 4 + 4 * (CSZ + 4)
        xbc = part(4 * PADW).rearrange("p (a t) -> p a t", a=4)
        staging = proj[:, 0:4096].rearrange("p (a t) -> p a t", a=4)
        square = hbuf[:, 0:1024]

        at2 = [0]

        def spart(n):
            at2[0] += n
            return small[:, at2[0] - n:at2[0]]

        bre = spart(256).rearrange("p (g c) -> p g c", g=16)
        bim = spart(256).rearrange("p (g c) -> p g c", g=16)
        bbr = spart(256).rearrange("p (g c) -> p g c", g=16)
        bbi = spart(256).rearrange("p (g c) -> p g c", g=16)
        cT = spart(512).rearrange("p (r g c) -> p r g c", r=2, g=16)
        c0 = spart(1024).rearrange("p (h g r c) -> p h g r c", h=2, g=16, r=2)
        pwr = spart(9 * 16).rearrange("p (j g) -> p j g", j=9)
        pwi = spart(9 * 16).rearrange("p (j g) -> p j g", j=9)
        pV = spart(256).rearrange("p (r g m) -> p r g m", r=2, g=16)
        pC = spart(256).rearrange("p (r g m) -> p r g m", r=2, g=16)
        co = spart(64).rearrange("p (o g t) -> p o g t", o=2, g=16)
        sc5 = spart(24 * 16).rearrange("p (j g) -> p j g", g=16)
        par1 = spart(128)
        par2 = spart(128)

        VT = mix(0, 4096).rearrange("p (g r n) -> p g r n", g=16, r=2)
        crow = mix(11264, 1024).rearrange("p (r b n) -> p r b n", r=2, b=4)
        V = mix(4096, 4096).rearrange("p (g r m) -> p g r m", g=16, r=2)
        vtmp = mix(8192, 2048)
        W = mix(4096, 6144).rearrange("p (c o g t) -> p c o g t", c=NCH, o=2, g=16)
        T5 = mix(4096, 4096).rearrange("p (g d m) -> p g d m", g=NG, d=2)
        SHm = mix(8192, 2048).rearrange("p (h c g r) -> p h c g r", h=2, c=LCH, g=16)
        U = mix(10240, 1024).rearrange("p (g c) -> p g c", g=NG)
        SH = mix(11264, 2048).rearrange("p (c g r) -> p c g r", c=NCH, g=16)
        kqsb = mix(13312, 512).rearrange("p (d g c) -> p d g c", d=2, g=NG)
        zero5 = mix(13824, 112)
        YS = mix(13312, 512).rearrange("p (g c) -> p g c", g=NG)
        Cc = hbuf[:, :].rearrange("p (g r m) -> p g r m", g=16, r=2)
        cctmp = mix(0, 2048)

        fA = mix(0, 1024)

        filled, ev_act, ev_dve = sem("bank_filled"), sem("bank_emptied_act"), sem("bank_emptied_dve")
        ring = BankRing(psum, filled, {"act": ev_act, "dve": ev_dve})
        bank = ring.bank
        loaded = [sem(f"slot{i}_loaded") for i in range(NSLOT)]
        slot_read = sem("slot_read")
        const_in, par_in, s5b_in, x_in, a2_in, fw_in, glu_in = (
            sem(n) for n in ("const_in", "par_in", "s5b_in", "x_in", "a2_in", "fw_in", "glu_in"))
        par_zeroed, cond_ready = sem("par_zeroed"), sem("cond_ready")
        dve_chain, act_chain, pool_chain = sem("dve_chain"), sem("act_chain"), sem("pool_chain")
        ssq_ready, rstd_ready, xn_ready = sem("ssq_ready"), sem("rstd_ready"), sem("xn_ready")
        cexp_ready = sem("cexp_ready")
        V_ready, C0_ready = sem("V_ready"), sem("C0_ready")
        hT_ready = sem("hT_ready")
        kq_stored, T_in, scratch_zeroed = sem("kq_stored"), sem("T_in"), sem("scratch_zeroed")
        s5_scan, SH_ready = sem("s5_scan"), sem("SH_ready")
        Cc_ready = sem("Cc_ready")
        T_free = sem("T_free")
        s = {}

        def S(name):
            if name not in s:
                s[name] = sem(name)
            return s[name]

        scratch = nc.dram_tensor("s5_lags", (2, CH, NG, 15, CH), F32).ap()
        gz = mix(0, 1024).rearrange("p (d t) -> p d t", d=2)
        gln = mix(1024, 1024).rearrange("p (d t) -> p d t", d=2)
        gb = mix(2048, 1024).rearrange("p (d t) -> p d t", d=2)
        gluw = mix(3072, 512).rearrange("p (k n) -> p k n", k=2)
        gdec = mix(3584, 16).rearrange("p (d n) -> p d n", d=2)
        fourw = mix(9216, 512).rearrange("p (k n) -> p k n", k=2)
        fA = mix(8192, 1024).rearrange("p (a f n) -> p a f n", a=2, f=2)
        qm = mix(4096, 2048).rearrange("p (d h t) -> p d h t", d=2, h=4)
        qin = mix(6144, 512).rearrange("p (d t) -> p d t", d=2)
        kin = mix(6656, 512).rearrange("p (d t) -> p d t", d=2)
        kdM = mix(7168, 2048).rearrange("p (d a h n) -> p d a h n", d=2, a=4, h=2)
        att = mix(9216, 2048).rearrange("p (d a h t) -> p d a h t", d=2, a=2, h=4)
        SM = mix(11264, 2048).rearrange("p (d j n) -> p d j n", d=2, j=4)
        Srun = mix(13312, 512).rearrange("p (d n) -> p d n", d=2)
        go, gsq, grs, gsl = (mix(4096 + 512 * i, 512).rearrange("p (a t) -> p a t", a=2) for i in range(4))
        fin5 = [hbuf[:, 2048 + 512 * i:2560 + 512 * i].rearrange("p (a t) -> p a t", a=2) for i in range(4)]

        dtR, cumR, wR, tR = (mix(512 * i, 512) for i in range(4))
        cv = mix(2048, 4 * PADW).rearrange("p (a t) -> p a t", a=4)
        ce = mix(4176, 4 * PADW).rearrange("p (a t) -> p a t", a=4)
        XC = hbuf[:, 0:2048].rearrange("p (a t) -> p a t", a=4)
        cols = mix(6304, 96).rearrange("p (w a d h) -> p w a d h", w=3, a=4, d=2)
        xdt = mix(6400, 1024).rearrange("p (a d n) -> p a d n", a=2, d=2)
        xdec = mix(7424, 2048).rearrange("p (a d n) -> p a d n", a=4, d=2)
        BTM = mix(9472, 1024).rearrange("p (a h n) -> p a h n", a=4, h=2)
        ECR = mix(10496, 2048).rearrange("p (r t) -> p r t", r=8)
        SEG = mix(2048, 2048).rearrange("p (r a t) -> p r a t", r=8, a=2)
        SE = mix(4096, 2048).rearrange("p (d j n) -> p d j n", d=2, j=4)
        SSrun = mix(12544, 512).rearrange("p (d n) -> p d n", d=2)
        Cg = mix(13056, 512).rearrange("p (g t) -> p g t", g=2)
        DEC = mix(13568, 64).rearrange("p (r n) -> p r n", r=8)
        anegc = mix(13632, 1)

        h2T = proj[:, 0:2048].rearrange("p (k t) -> p k t", k=KT)
        h2TM = proj[:, 2048:4096].rearrange("p (a n) -> p a n", a=2)
        xsq = proj[:, 4096:6144].rearrange("p (k t) -> p k t", k=KT)
        bgu = hbuf[:, 0:2048]
        bdn = hbuf[0:NE, 2048:3072]
        gfin = hbuf[:, 3072:4096]
        rw = small[:, 0:256].rearrange("p (k e) -> p k e", k=KT)
        eg, eu, es, hg, aT, ey = (small[:, 256 + 512 * i:768 + 512 * i] for i in range(6))
        hg = hg.rearrange("p (k c) -> p k c", k=KT)
        aT = aT.rearrange("p (i h c) -> p i h c", h=2, c=CAP)
        GT = small[:, 3328:3584]
        facc = psum[:, 4:8, :].rearrange("p b (o t) -> p (b o) t", o=2)
        ext = sb("ext", 1900)
        at3 = [0]

        def epart(n):
            at3[0] += n
            assert at3[0] <= 1900
            return ext[:, at3[0] - n:at3[0]]

        Ssel = epart(2 * CAP).rearrange("p (a c) -> p a c", a=2)
        Sgat = epart(4 * CAP).rearrange("p (a c) -> p a c", a=2)
        posI = epart(2 * NI).rearrange("p (a i) -> p a i", a=2)
        gatI = epart(2 * NI).rearrange("p (a i) -> p a i", a=2)
        lg = epart(64).rearrange("p (a e) -> p a e", a=2)
        gt = epart(64).rearrange("p (a e) -> p a e", a=2)
        eq = epart(64).rearrange("p (a e) -> p a e", a=2)
        rank = epart(64).rearrange("p (a e) -> p a e", a=2)
        sel = epart(64).rearrange("p (a e) -> p a e", a=2)
        gate = epart(64).rearrange("p (a e) -> p a e", a=2)
        posm = epart(64).rearrange("p (a e) -> p a e", a=2)
        top = epart(16).rearrange("p (a e) -> p a e", a=2)
        need = epart(8).rearrange("p (a e) -> p a e", a=2)
        nmax = epart(2)
        zsum = epart(2)
        rbias = epart(32)
        posT = epart(256)
        gatT = epart(256)
        Em, Eb, Et = epart(NI), epart(NI), epart(NI)
        Ecol = epart(CAP)
        nb = epart(4)
        idf = epart(NI + 1)
        eps_half = epart(1)

        cw = D // P
        win = t["w_in"][0].rearrange("(k p) c -> p k c", p=P)
        ada = t["ada_w"][0].rearrange("(k p) c -> p k c", p=P)
        wout = t["w_out"][0].rearrange("(k p) c -> p k c", p=P)
        wgu = t["exp_w_gu"][0]
        wdn = t["exp_w_dn"][0]
        WCOL = {W_FOUR: 0, W_U: 256, W_QK: 512, W_V: 768, W_R: 1024, W_Z: 1312, W_X: 1568, W_BC: 1824}
        A1_COL, DT_COL = 1280, 2080
        uses = [len([n for n in range(len(STREAM)) if n % FR == i]) if i < FR else 0 for i in range(NSLOT)]
        NSTREAM = len(STREAM)

        def sview(n):
            return slot(n % FR).rearrange("p (k c) -> p k c", k=KT)

        block = ctx.enter_context(nc.Block())

        @block.sync
        def _(sp):
            for i in range(2):
                sp.dma_start(staging[:, i, :], t["ctx"][0, P * i:P * (i + 1), :]).then_inc(x_in, 16)
                sp.dma_start(staging[:, 2 + i, :], t["x"][0, P * i:P * (i + 1), :]).then_inc(x_in, 16)
            for n, (kind, b) in enumerate(STREAM):
                if n >= FR:
                    sp.wait_ge(slot_read, n - FR + 1)
                dst = sview(n)
                done = loaded[n % FR]
                if kind == "win" and b == W_MISC:
                    sp.wait_ge(S("misc_zeroed"), 1)
                    sp.dma_start(dst[:, :, 0:32], win[:, :, A1_COL:A1_COL + 32]).then_inc(S("misc_in"), 16)
                    sp.dma_start(dst[:, :, 64:68], win[:, :, DT_COL:DT_COL + 4]).then_inc(S("misc_in"), 16)
                    sp.dma_start(dst[:, :, 96:100], win[:, :, DT_COL + 4:DT_COL + 8]).then_inc(done, 16)
                else:
                    src = {"ada": ada, "win": win, "wout": wout}[kind]
                    c0 = WCOL[b] if kind == "win" else 256 * b
                    sp.dma_start(dst, src[:, :, c0:c0 + 256]).then_inc(done, 16)

            def chunk(e, c):
                if c < 8:
                    src = wgu[e, P * c:P * (c + 1), :]
                    return slot(c), src.rearrange("a p c -> p (a c)") if len(src.shape) == 3 else src
                j = c - 8
                src = wdn[e, 2 * P * j:2 * P * (j + 1), :]
                if len(src.shape) == 3:
                    src = src.rearrange("e k c -> (e k) c")
                return slot(c).rearrange("p (a n) -> p a n", a=2), src.rearrange("(a p) n -> p a n", p=P)

            for c in range(NSLOT):
                if c < FR:
                    sp.wait_ge(slot_read, max(n for n in range(NSTREAM) if n % FR == c) + 1)
                elif c == FR:
                    sp.wait_ge(S("mixers_done"), 1)
                dst, src = chunk(0, c)
                sp.dma_start(dst, src).then_inc(loaded[c], 16)
            sp.wait_ge(S("ids_ready"), 1)
            n_items = sp.value_load(ids[0:1, NI:NI + 1], min_val=2, max_val=NI - 2)
            with sp.Fori(1, n_items) as it:
                e = sp.value_load(ids[0:1, bass.ds(it + 1, 1)], min_val=0, max_val=NE - 1)
                for c in range(NSLOT):
                    if c == KT - 1:
                        sp.wait_ge(S("gu_full"), it)
                    elif c == NSLOT - 1:
                        sp.wait_ge(S("d_full"), it)
                    else:
                        sp.wait_ge(slot_read, (NSLOT - 2) * (it - 1) + (NSTREAM + c + 1 - c // KT))
                    dst, src = chunk(bass.ds(e, 1), c)
                    sp.dma_start(dst, src).then_inc(loaded[c], 16)
            for a in range(2):
                sp.wait_ge(S("out_ready"), a + 1)
                sp.dma_start(out[0, P * a:P * (a + 1), :], h2TM[:, a, :]).then_inc(S("out_stored"), 16)
            sp.wait_ge(S("out_stored"), 32)

        @block.gpsimd
        def _(pool):
            chain = [0]

            def link(ins):
                chain[0] += 1
                ins.then_inc(pool_chain, 1)
                pool.wait_ge(pool_chain, chain[0])

            pool.memset(proj[:, 4864:6992], 0.0).then_inc(S("xbc_zeroed"), 1)
            link(pool.memset(neghalf[:, :], -0.5))
            link(pool.memset(zero5[0:CH, :], 0.0))
            for d in range(2):
                x0 = 0 if d == 0 else Q
                pool.dma_start(scratch[d, :, :, x0:x0 + 7, :].rearrange("c g x k -> c g (x k)"),
                               zero5[0:CH, :].unsqueeze(1).to_broadcast([CH, NG, 7 * CH])
                               ).then_inc(scratch_zeroed, 16)

            def power(dst, src, scale, n):
                link(pool.tensor_scalar(dst, src, scale, EPS, ALU.mult, ALU.add))
                return pool.tensor_tensor(dst, dst, neghalf[:, 0:1].to_broadcast([P, n]), ALU.pow)

            pool.wait_ge(ssq_ready, 4)
            power(tiny[:, 4:8], tiny[:, 0:4], 1.0 / D, 4).then_inc(rstd_ready, 1)

            n = AT[("win", W_MISC)]
            pool.wait_ge(slot_read, n - FR + 1)
            pool.memset(sview(n)[:, :, 0:P], 0.0).then_inc(S("misc_zeroed"), 1)

            ring.wait_emptied(pool, "Kq")
            for d in range(2):
                for m in range(Q):
                    x = 14 - m if d == 0 else 7 - m
                    pool.dma_start(scratch[d, :, :, x, :], kqsb[CH * m:CH * (m + 1), d, :, :]).then_inc(kq_stored, 16)
            pool.wait_ge(kq_stored, 16 * 2 * Q)
            pool.wait_ge(scratch_zeroed, 32)
            pool.wait_ge(T_free, 1)
            for d in range(2):
                for j in range(Q):
                    pool.dma_start(T5[CH * j:CH * (j + 1), :, d, :],
                                   scratch[d, :, :, 7 - j:15 - j, :].rearrange("c g x k -> c g (x k)")
                                   ).then_inc(T_in, 16)

            for name, buf, scale in (("gss", grs, 1.0 / 64), ("yss", fin5[2], 1.0 / 256)):
                ring.wait_emptied(pool, name)
                w = buf if name == "gss" else buf[:, 0, :]
                link(pool.tensor_scalar(w, w, scale, EPS, ALU.mult, ALU.add))
                nh = neghalf[:, 0:1].unsqueeze(2).to_broadcast([P, 2, 256]) if name == "gss" else \
                    neghalf[:, 0:1].to_broadcast([P, 256])
                pool.tensor_tensor(w, w, nh, ALU.pow).then_inc(S(name + "_root"), 1)
            ring.wait_emptied(pool, "ss2")
            power(mixT[:, 0, :], mixT[:, 0, :], 1.0 / D, 256).then_inc(S("ss2_root"), 1)
            pool.wait_ge(S("last_ssq"), 2)
            power(tiny[:, 52:54], tiny[:, 50:52], 1.0 / D, 2).then_inc(S("last_root"), 1)

        @block.scalar
        def _(act):
            chain = [0]
            counts = {}

            def link(ins, done=None):
                if done is None:
                    chain[0] += 1
                    ins.then_inc(act_chain, 1)
                    act.wait_ge(act_chain, chain[0])
                    return
                counts[done] = counts.get(done, 0) + 1
                ins.then_inc(S(done), 1)
                act.wait_ge(S(done), counts[done])

            def copy_out(name, dst, src):
                ring.wait_filled(act, name)
                ring.mark_emptied(nc.scalar.copy(dst, src), name, "act")

            act.dma_start(const[:, :], t["const"]).then_inc(const_in, 16)
            act.wait_ge(par_zeroed, 1)

            def rows(at, n, src):
                act.dma_start(par1[at:at + n, :], src).then_inc(par_in, 16)

            rows(R_C, 8, t["c"][0].rearrange("(k p) -> k p", p=P))
            rows(R_CCTX, 8, t["c_ctx"].rearrange("(k p) -> k p", p=P))
            rows(R_GMIX, 8, t["norm_mix_g"][0].rearrange("(k p) -> k p", p=P))
            rows(R_GFFN, 8, t["norm_ffn_g"][0].rearrange("(k p) -> k p", p=P))
            rows(R_ADAB, 48, t["ada_b"][0].rearrange("(k p) -> k p", p=P))
            rows(R_S5D, 2, t["s5_d"][0].rearrange("(k p) -> k p", p=P))
            rows(R_SSDG, 2, t["ssd_norm_g"][0].rearrange("(k p) -> k p", p=P))
            rows(R_CONVB, 4, t["ssd_conv_b"][0].rearrange("(k p) -> k p", p=P))
            rows(R_CONVW, 20, t["ssd_conv_w"][0].rearrange("j (k p) -> (j k) p", p=P))
            rows(R_GLAB, 2, t["gla_a_b"][0])
            for i in range(2):
                act.dma_start(par1[R_GLAG:R_GLAG + 1, 64 * i:64 * (i + 1)], t["gla_norm_g"]).then_inc(par_in, 16)
                at_ = ROW0 + 32 * i
                act.dma_start(par1[R_DTB:R_DTB + 1, at_:at_ + 4], t["ssd_dt_bias"][0, i:i + 1, :]).then_inc(par_in, 16)
                act.dma_start(par1[R_ALOG:R_ALOG + 1, at_:at_ + 4], t["ssd_a_log"][0, i:i + 1, :]).then_inc(par_in, 16)
            for i, name in enumerate(("s5_lam_re", "s5_lam_im")):
                act.dma_start(par2[16 * i:16 * i + 16, :],
                              t[name][0].rearrange("d (g h) n -> (d g) (h n)", h=2)).then_inc(par_in, 16)
            act.dma_start(pairs[32:48, :], t["s5_log_dt"][0].rearrange("d (g h) -> (d g) h", h=2)
                          ).then_inc(S("pairs_in"), 16)
            act.dma_start(pairs[PAIR_D:PAIR_D + 2, :], t["ssd_d"][0].rearrange("(a h) -> a h", h=2)
                          ).then_inc(S("pairs_in"), 16)
            for name, dst in (("s5_b_re", bre), ("s5_b_im", bim)):
                for d in range(2):
                    act.dma_start(dst[:, 8 * d:8 * d + 8, :],
                                  t[name][0, d].rearrange("(g h) n c -> (h n) g c", h=2)).then_inc(s5b_in, 16)
            for r, name in enumerate(("s5_c_re", "s5_c_im")):
                for h in range(2):
                    act.dma_start(crow[:, r, :, 64 * h:64 * h + 64],
                                  t[name][0].rearrange("d (b g) c n -> (g c) (d b) n", b=2)).then_inc(S("s5c_in"), 16)
            for d in range(2):
                act.dma_start(a2[16 * d:16 * d + 16, 128 * d:128 * d + 128], t["gla_a2"][0, d]).then_inc(a2_in, 16)

            act.wait_ge(S("pairs_in"), 32)
            for h in range(2):
                for q in (slice(32, 48), slice(PAIR_D, PAIR_D + 2)):
                    nc.scalar.copy(par2[q, 64 * h:64 * h + 64], pairs[q, h:h + 1].to_broadcast(
                        [q.stop - q.start, 64])).then_inc(S("pairs_spread"), 1)
            ring.wait_emptied(act, "par")
            nc.scalar.activation(tiny[:, 16:32], prm[:, 0:16], ACT.Sigmoid).then_inc(cexp_ready, 1)
            act.wait_ge(x_in, 64)
            for i in range(4):
                nc.scalar.activation(square, staging[:, i, :], ACT.Square,
                                     accum_out=tiny[:, i:i + 1]).then_inc(ssq_ready, 1)
                act.wait_ge(ssq_ready, i + 1)
            for r in range(2):
                ring.wait_filled(act, f"cpar{r}")
                for h in range(2):
                    q = slice(64 * h, 64 * h + 64)
                    ins = nc.scalar.copy(cT[q, r], bank(f"cpar{r}")[q, :].rearrange("p (g h c) -> p g h c", h=2,
                                                                                    c=CH)[:, :, h, :])
                ring.mark_emptied(ins, f"cpar{r}", "act")
            for i in range(4):
                copy_out(f"xraw{i}", xT[:, 2 * i:2 * i + 2, :].rearrange("p k t -> p (k t)"), bank(f"xraw{i}"))
            VTf = VT.rearrange("p g r n -> p (g r n)")
            for i in range(8):
                copy_out(f"VT{i}", VTf[:, 512 * i:512 * (i + 1)], bank(f"VT{i}"))
            copy_out("Kq", kqsb.rearrange("p d g c -> p (d g c)"), bank("Kq"))
            act.wait_ge(V_ready, 1)
            act.dma_start(fourw, t["four_w"][0].rearrange("(k p) n -> p k n", p=P)).then_inc(fw_in, 16)

            copy_out("four", fourT.rearrange("p a t -> p (a t)"), bank("four"))
            copy_out("u0", uT[:, 0, :], bank("u0"))
            copy_out("u1", uT[:, 1, :], bank("u1"))
            ring.wait_filled(act, "q")
            ring.mark_emptied(nc.scalar.mul(qT, bank("q")[:, 0:256], float(GLA_DK) ** -0.5), "q", "act")
            copy_out("k", kTt, bank("k"))
            copy_out("v0", vTM[:, 0:2, :].rearrange("p a t -> p (a t)"), bank("v0"))
            copy_out("v1", vTM[:, 2:4, :].rearrange("p a t -> p (a t)"), bank("v1"))
            copy_out("r", rT.rearrange("p a t -> p (a t)"), bank("r"))
            copy_out("misc", miscT, bank("misc"))
            copy_out("z", zT.rearrange("p a t -> p (a t)"), bank("z"))
            act.wait_ge(S("xbc_zeroed"), 1)

            def lat_rows(tile):
                return tile[:, NCTX + 4:].rearrange("p (r w) -> p r w", w=CSZ + 4)[:, :, 2:2 + CSZ]

            for i, name in enumerate(("x0", "x1", "B", "C")):
                ring.wait_filled(act, name)
                if name != "C":
                    nc.scalar.copy(xbc[:, i, 2:2 + NCTX], bank(name)[:, 0:NCTX])
                lat = bank(name)[:, NCTX:] if name != "C" else bank(name)[:, 0:NLAT]
                ring.mark_emptied(nc.scalar.copy(lat_rows(xbc[:, i, :]), lat.rearrange("p (r w) -> p r w", w=CSZ)),
                                  name, "act")

            for i in range(2):
                copy_out(f"fA{i}", fA[:, i].rearrange("p f n -> p (f n)"), bank(f"fA{i}"))
            copy_out("fB", fourT.rearrange("p a t -> p (a t)"), bank("fB"))
            copy_out("fW", mixT[:, 0:2, :].rearrange("p a t -> p (a t)"), bank("fW"))

            for i in range(2):
                copy_out(f"U{i}", U[:, 8 * i:8 * i + 8, :].rearrange("p g c -> p (g c)"), bank(f"U{i}"))
            for i in range(4):
                ring.wait_filled(act, f"D{i}")
                b4 = bank(f"D{i}").rearrange("p (o g c) -> p o g c", o=2, g=4)
                w4 = W[:, :, :, 4 * i:4 * i + 4, 2].rearrange("p c o g -> p o g c")
                if i < 2:
                    ring.mark_emptied(nc.scalar.copy(w4, b4), f"D{i}", "act")
                else:
                    nc.scalar.copy(w4[:, :, :, 31::-1], b4[:, :, :, 0:32])
                    ring.mark_emptied(nc.scalar.copy(w4[:, :, :, 63:31:-1], b4[:, :, :, 32:64]), f"D{i}", "act")
            act.dma_start(gluw, t["s5_w_glu"][0].rearrange("(k p) n -> p k n", p=P)).then_inc(glu_in, 16)
            for d in range(2):
                ring.wait_filled(act, f"zg{d}")
                ring.mark_emptied(nc.scalar.activation(gz[:, d, :], bank(f"zg{d}"), ACT.Identity,
                                                       bias=prm[:, R_GLAB + d:R_GLAB + d + 1]), f"zg{d}", "act")
            act.wait_ge(S("gabs"), 1)
            link(nc.scalar.activation(gln, gln, ACT.Exp, scale=-1.0))
            link(nc.scalar.activation(gln, gln, ACT.Ln, bias=1.0), "glog")
            copy_out("Y", YS.rearrange("p g c -> p (g c)"), bank("Y"))
            act.wait_ge(S("gelu_in"), 1)
            link(nc.scalar.activation(fin5[1], fin5[1], ACT.Sigmoid, scale=2.0 * float(np.sqrt(2 / np.pi))), "gelu_exp")
            ring.wait_filled(act, "glu")
            ring.mark_emptied(nc.scalar.activation(fin5[2], bank("glu").rearrange("p (a t) -> p a t", a=2),
                                                   ACT.Sigmoid), "glu", "act")
            act.wait_ge(S("gscan"), 1)
            nc.scalar.activation(qin, gb[:, :, NCTX:], ACT.Exp)
            nc.scalar.activation(kin, gb[:, :, NCTX:], ACT.Exp, scale=-1.0)
            nc.scalar.activation(gln, gln, ACT.Exp)
            for d in range(2):
                last = CSZ - 1 if d == 0 else 0
                ins = nc.scalar.activation(gdec[:, d, :], gb[:, d, last::CSZ], ACT.Exp)
            link(ins, "gexp")
            act.wait_ge(S("go_ready"), 1)
            link(nc.scalar.activation(gsq, go, ACT.Square), "gsq_ready")
            link(nc.scalar.activation(gsl, rT, ACT.Sigmoid), "gsl_ready")
            copy_out("gss", grs.rearrange("p a t -> p (a t)"), bank("gss"))

            act.wait_ge(S("dt_abs"), 1)
            link(nc.scalar.activation(tR[ROW0:, :], tR[ROW0:, :], ACT.Exp, scale=-1.0))
            nc.scalar.activation(anegc[ROW0:, :], prm[ROW0:, R_ALOG:R_ALOG + 1], ACT.Exp)
            link(nc.scalar.activation(tR[ROW0:, :], tR[ROW0:, :], ACT.Ln, bias=1.0), "dt_log")
            act.wait_ge(S("cum_ready"), 1)
            link(nc.scalar.activation(wR[ROW0:, :], wR[ROW0:, :], ACT.Exp), "w_exp")
            act.wait_ge(S("conv_ready"), 1)
            link(nc.scalar.activation(ce, cv, ACT.Sigmoid), "conv_exp")
            ring.wait_filled(act, "decl")
            ring.mark_emptied(nc.scalar.activation(DEC.rearrange("p r n -> p (r n)"), bank("decl")[:, 0:64], ACT.Exp),
                              "decl", "act")
            for i in range(4):
                ring.wait_filled(act, f"rb{i}")
                nc.scalar.activation(ECR[:, 2 * i:2 * i + 2, :].rearrange("p r t -> p (r t)"), bank(f"rb{i}"),
                                     ACT.Exp).then_inc(S("ecr_ready"), 1)
            act.wait_ge(S("seg_ready"), 1)
            link(nc.scalar.activation(SEG, SEG, ACT.Exp), "seg_exp")
            link(nc.scalar.activation(fin5[3], zT, ACT.Sigmoid), "sz_exp")
            act.wait_ge(S("yz_ready"), 1)
            link(nc.scalar.activation(fin5[1], fin5[0], ACT.Square), "ysq_ready")
            copy_out("yss", fin5[2][:, 0, :], bank("yss")[:, 0:256])

            act.wait_ge(S("mixers_done"), 1)
            act.wait_ge(S("bgu_zeroed"), 1)
            act.dma_start(bgu[0:NE, :], t["exp_b_gu"][0]).then_inc(S("bias_in"), 16)
            act.dma_start(bdn, t["exp_b_dn"][0]).then_inc(S("bias_in"), 16)
            act.dma_start(gfin, t["final_g"].unsqueeze(0).to_broadcast([P, D])).then_inc(S("gfin_in"), 16)
            act.dma_start(rw, t["router_w"][0].rearrange("(k p) e -> p k e", p=P)).then_inc(S("router_in"), 16)
            act.dma_start(rbias, t["router_b"].to_broadcast([P, NE])).then_inc(S("router_in"), 16)
            act.wait_ge(S("x2_ready"), KT)
            link(nc.scalar.activation(xsq, xT, ACT.Square), "xsq_ready")
            copy_out("ss2", mixT[:, 0, :], bank("ss2")[:, 0:256])
            for i in range(4):
                copy_out(f"h2{i}", h2TM[:, :, 256 * i:256 * (i + 1)], bank(f"h2{i}").rearrange("p (a n) -> p a n", a=2))
            act.wait_ge(S("lmax_ready"), 1)
            for a in range(2):
                ins = nc.scalar.activation(gate[:, a, :], lg[:, a, :], ACT.Exp, bias=nmax[:, a:a + 1])
            link(ins, "gate_exp")

            def gathered(n):
                act.wait_ge(S("g_full"), n)
                nc.scalar.copy(hg.rearrange("p k c -> p (k c)"), psum[:, 3, :]).then_inc(S("hg_ready"), 1)

            gathered(1)
            act.wait_ge(S("ids_ready"), 1)
            n_items = act.value_load(ids[0:1, NI:NI + 1], min_val=2, max_val=NI - 2)
            with act.Fori(0, n_items) as it:
                act.wait_ge(S("gclip_ready"), it + 1)
                nc.scalar.activation(es, eg, ACT.Sigmoid, scale=ALPHA).then_inc(S("sig_ready"), 1)
                gathered(it + 2)
                act.wait_ge(S("at_full"), it + 1)
                nc.scalar.copy(aT.rearrange("p i h c -> p (i h c)"), psum[:, 2, :]).then_inc(S("aT_ready"), 1)
                act.wait_ge(S("d_full"), it + 1)
                act.wait_ge(S("sc_full"), it + 2)
                nc.scalar.copy(ey, psum[:, 3, :]).then_inc(S("y_ready"), 1)
            for a in range(2):
                act.wait_ge(S("fin_full"), a + 1)
                nc.scalar.activation(h2TM[:, a, :].rearrange("p (b n) -> p b n", b=2), psum[:, 2 * a:2 * a + 2, :],
                                     ACT.Square, accum_out=tiny[:, 50 + a:51 + a]).then_inc(S("last_ssq"), 1)

        @block.vector
        def _(dve):
            v = nc.vector
            chain = [0]
            counts = {}

            def link(ins, done=None):
                if done is None:
                    chain[0] += 1
                    ins.then_inc(dve_chain, 1)
                    dve.wait_ge(dve_chain, chain[0])
                    return
                counts[done] = counts.get(done, 0) + 1
                ins.then_inc(S(done), 1)
                dve.wait_ge(S(done), counts[done])

            def emptied(ins, name):
                ring.mark_emptied(ins, name, "dve")
                ring.wait_emptied(dve, name)

            def add(o, a, b):
                return v.tensor_tensor(o, a, b, ALU.add)

            def sub(o, a, b):
                return v.tensor_tensor(o, a, b, ALU.subtract)

            def mul(o, a, b):
                return v.tensor_tensor(o, a, b, ALU.mult)

            v.memset(par2[:, :], 0.0)
            v.memset(a2[:, :], 0.0)
            link(v.memset(par1[:, :], 0.0))
            v.tensor_copy(tiny[:, 159:160], par1[:, 0:1]).then_inc(par_zeroed, 1)

            ring.wait_filled(dve, "par")
            emptied(v.tensor_copy(prm[:, :], bank("par")[:, 0:NPAR]), "par")
            ring.wait_filled(dve, "s5par")
            emptied(v.tensor_copy(s5p[:, :], bank("s5par")[:, 0:NPAR2]), "s5par")
            ce_ = tiny[:, 16:32]
            dve.wait_ge(cexp_ready, 1)
            link(mul(cond.rearrange("p k c -> p c k"), prm[:, 0:16].rearrange("p (c k) -> p c k", c=2),
                     ce_.rearrange("p (c k) -> p c k", c=2)), "cond_silu")

            LN2_HI, LN2_LO = 0.693145751953125, 1.42860682030941723212e-6
            PI2_A, PI2_B, PI2_C = 6.28125, 1.93500518798828125e-3, 3.0199159819567014e-7
            MAGIC = 1.5 * 2.0 ** 23
            (dt_, zr, zi, t0, t1, t2, ex, sn, cs, ar, ai, am, den, wr_, wi_, t3) = (sc5[:, j, :] for j in range(16))
            lre, lim_, ldt = s5p[:, 0:16], s5p[:, 16:32], s5p[:, 32:48]

            def nearest(o, a, scale):
                link(v.tensor_scalar(o, a, scale, MAGIC, ALU.mult, ALU.add))
                link(v.tensor_scalar(o, o, -MAGIC, None, ALU.add))

            def exponential(o, a):
                link(v.tensor_scalar(t0, a, -87.0, 88.0, ALU.max, ALU.min))
                nearest(t1, t0, 1.0 / float(np.log(2.0)))
                link(v.scalar_tensor_tensor(t0, t1, -LN2_HI, t0, ALU.mult, ALU.add))
                link(v.scalar_tensor_tensor(t0, t1, -LN2_LO, t0, ALU.mult, ALU.add))
                link(v.tensor_scalar(t2, t0, 1.0 / 5040, None, ALU.mult))
                for c in (720, 120, 24, 6, 2, 1):
                    link(v.scalar_tensor_tensor(t2, t2, 1.0 / c, t0, ALU.add, ALU.mult))
                link(v.tensor_scalar(t1.bitcast(I32), t1, 127.0, 2.0 ** 23, ALU.add, ALU.mult))
                link(v.scalar_tensor_tensor(o, t2, 1.0, t1, ALU.add, ALU.mult))

            exponential(dt_, ldt)
            link(mul(zr, lre, dt_))
            link(mul(zi, lim_, dt_))
            exponential(ex, zr)
            nearest(t1, zi, 1.0 / (2 * float(np.pi)))
            for c in (PI2_A, PI2_B, PI2_C):
                link(v.scalar_tensor_tensor(zi, t1, -c, zi, ALU.mult, ALU.add))
            link(v.tensor_scalar(t0, zi, 0.25, None, ALU.mult))
            link(mul(t1, t0, t0))
            link(v.tensor_scalar(sn, t1, 1.0 / 362880, None, ALU.mult))
            for c in (-5040.0, 120.0, -6.0):
                link(v.scalar_tensor_tensor(sn, sn, 1.0 / c, t1, ALU.add, ALU.mult))
            link(v.scalar_tensor_tensor(sn, sn, 1.0, t0, ALU.add, ALU.mult))
            link(v.tensor_scalar(cs, t1, -1.0 / 3628800, None, ALU.mult))
            for c in (40320.0, -720.0, 24.0, -2.0):
                link(v.scalar_tensor_tensor(cs, cs, 1.0 / c, t1, ALU.add, ALU.mult))
            link(v.tensor_scalar(cs, cs, 1.0, None, ALU.add))
            for _ in range(2):
                link(mul(t2, sn, sn))
                link(v.scalar_tensor_tensor(sn, sn, 2.0, cs, ALU.mult, ALU.mult))
                link(v.tensor_scalar(cs, t2, -2.0, 1.0, ALU.mult, ALU.add))
            link(mul(ar, ex, cs))
            link(mul(ai, ex, sn))
            link(v.tensor_scalar(am, ar, -1.0, None, ALU.add))
            link(mul(den, lre, lre))
            link(mul(t0, lim_, lim_))
            link(add(den, den, t0))
            link(v.reciprocal(den, den))
            link(mul(t0, am, lre))
            link(mul(t1, ai, lim_))
            link(add(t0, t0, t1))
            link(mul(wr_, t0, den))
            link(mul(t0, ai, lre))
            link(mul(t1, am, lim_))
            link(sub(t0, t0, t1))
            link(mul(wi_, t0, den))

            def cmul(orr, oi, xr, xi, yr, yi, tr):
                link(mul(orr, xr, yr))
                link(mul(tr, xi, yi))
                link(sub(orr, orr, tr))
                link(mul(oi, xr, yi))
                link(mul(tr, xi, yr))
                link(add(oi, oi, tr))

            dve.wait_ge(s5b_in, 64)

            def over(x, n):
                return x.unsqueeze(2).to_broadcast([P, 16, n])

            tb = vtmp[:, 0:256].rearrange("p (g c) -> p g c", g=16)
            cmul(bbr, bbi, over(wr_, CH), over(wi_, CH), bre, bim, tb)
            v.memset(pwr[:, 0, :], 1.0)
            v.memset(pwi[:, 0, :], 0.0)
            v.tensor_copy(pwr[:, 1, :], ar)
            link(v.tensor_copy(pwi[:, 1, :], ai))
            for n in (1, 2, 4):
                a, b = slice(1, n + 1), slice(n + 1, 2 * n + 1)

                def times(x):
                    return x[:, n:n + 1, :].to_broadcast([P, n, 16])

                cmul(pwr[:, b, :], pwi[:, b, :], pwr[:, a, :], pwi[:, a, :], times(pwr), times(pwi),
                     vtmp[:, 0:16 * n].rearrange("p (j g) -> p j g", g=16))
            for r, pw in enumerate((pwr, pwi)):
                v.tensor_copy(pV[:, r, 0:8, :], pw[:, 7::-1, 0:8].rearrange("p j g -> p g j"))
                v.tensor_copy(pV[:, r, 8:16, :], pw[:, 0:8, 8:16].rearrange("p j g -> p g j"))
                v.tensor_copy(pC[:, r, 0:8, :], pw[:, 1:9, 0:8].rearrange("p j g -> p g j"))
                link(v.tensor_copy(pC[:, r, 8:16, :], pw[:, 8:0:-1, 8:16].rearrange("p j g -> p g j")))
            v.tensor_copy(co[:, 0, :, 0], pwr[:, 8, :])
            v.tensor_scalar(co[:, 0, :, 1], pwi[:, 8, :], -1.0, None, ALU.mult)
            v.tensor_copy(co[:, 1, :, 0], pwi[:, 8, :])
            link(v.tensor_copy(co[:, 1, :, 1], pwr[:, 8, :]))

            def power_of(x, r):
                return x[:, r].unsqueeze(3).to_broadcast([P, 16, Q, CH])

            def channel_of(x):
                return x.unsqueeze(2).to_broadcast([P, 16, Q, CH])

            Vr, Vi = (V[:, :, r, :].rearrange("p g (m c) -> p g m c", m=Q) for r in range(2))
            vt4 = vtmp.rearrange("p (g m c) -> p g m c", g=16, m=Q)
            link(mul(Vr, power_of(pV, 0), channel_of(bbr)))
            link(mul(vt4, power_of(pV, 1), channel_of(bbi)))
            link(sub(Vr, Vr, vt4))
            link(mul(Vi, power_of(pV, 0), channel_of(bbi)))
            link(mul(vt4, power_of(pV, 1), channel_of(bbr)))
            link(add(Vi, Vi, vt4), "V_done")
            v.tensor_copy(tiny[:, 158:159], prm[:, 0:1]).then_inc(V_ready, 1)
            dve.wait_ge(const_in, 16)
            ring.wait_emptied(dve, "cpar1")
            for h in range(2):
                hm = con("halfm")[:, h:h + 1]
                v.tensor_scalar(c0[:, h, :, 0, :], cT[:, 0], hm, None, ALU.mult)
                ins = v.tensor_scalar(c0[:, h, :, 1, :], cT[:, 1], hm, -1.0, ALU.mult, ALU.mult)
            link(ins, "C0_done")

            dve.wait_ge(rstd_ready, 1)
            ring.wait_filled(dve, "xraw3")
            for i in range(4):
                ins = v.tensor_scalar(staging[:, i, :], staging[:, i, :], tiny[:, 8 - 4 + i:8 - 4 + i + 1], None,
                                      ALU.mult)
            ins.then_inc(xn_ready, 1)

            def mod_out(name, a, b):
                ring.wait_filled(dve, name)
                emptied(v.tensor_tensor(mod[:, a:b, :], bank(name)[:, 0:2 * (b - a)].rearrange("p (t c) -> p t c", c=2),
                                        prm[:, R_ADAB + a:R_ADAB + b].unsqueeze(2).to_broadcast([P, b - a, 2]),
                                        ALU.add), name)

            def gain(dst, scale, g0):
                n = scale.shape[-1]
                link(v.scalar_tensor_tensor(dst, scale, 1.0, prm[:, g0:g0 + KT].unsqueeze(2).to_broadcast([P, KT, n]),
                                            ALU.add, ALU.mult))

            mod_out("ada0", 0, 16)
            gA = tiny[:, 32:48].rearrange("p (k c) -> p k c", c=2)
            gain(gA, mod[:, 8:16, :], R_GMIX)
            for k in range(KT):
                ring.wait_filled(dve, f"xn{k}")
                for c, (a, b) in ((1, (0, NCTX)), (0, (NCTX, NTOK))):
                    ins = v.tensor_scalar(hT[:, k, a:b], bank(f"xn{k}")[:, a:b], gA[:, k, c:c + 1], mod[:, k, c:c + 1],
                                          ALU.mult, ALU.add)
                ring.mark_emptied(ins, f"xn{k}", "dve")

            ring.wait_filled(dve, "C")
            Cr, Ci = (Cc[:, :, r, :].rearrange("p g (m c) -> p g m c", m=Q) for r in range(2))
            cct = mix(11264, 2048).rearrange("p (g m c) -> p g m c", g=16, m=Q)
            link(mul(Cr, power_of(pC, 0), channel_of(cT[:, 0])))
            link(mul(cct, power_of(pC, 1), channel_of(cT[:, 1])))
            link(sub(Cr, Cr, cct))
            link(mul(Ci, power_of(pC, 0), channel_of(cT[:, 1])))
            link(mul(cct, power_of(pC, 1), channel_of(cT[:, 0])))
            link(add(Ci, Ci, cct))
            link(v.tensor_scalar(Ci, Ci, -1.0, None, ALU.mult), "Cc_done")

            ring.wait_emptied(dve, "D3")
            v.memset(SH[:, 0], 0.0).then_inc(s5_scan, 1)
            with dve.Fori(0, NCH - 1) as c:
                dve.wait_ge(s5_scan, 2 * c + 1)
                v.tensor_tensor(W[:, bass.ds(c, 1), :, :, 0:2].rearrange("p c o g t -> p (c o) g t"),
                                co, SH[:, bass.ds(c, 1)].to_broadcast([P, 2, 16, 2]), ALU.mult).then_inc(s5_scan, 1)
                dve.wait_ge(s5_scan, 2 * c + 2)
                v.tensor_reduce(SH[:, bass.ds(c + 1, 1)].rearrange("p c g r -> p (c r) g"),
                                W[:, bass.ds(c, 1)].rearrange("p c o g t -> p (c o) g t"),
                                AX.X, ALU.add).then_inc(s5_scan, 1)
            dve.wait_ge(s5_scan, 2 * (NCH - 1) + 1)
            for h in range(2):
                hm = con("halfm")[:, h:h + 1]
                v.tensor_scalar(SHm[:, h, :, 0:8, :], SH[:, LCH:, 0:8, :], hm, None, ALU.mult)
                ins = v.tensor_scalar(SHm[:, h, :, 8:16, :], SH[:, NCH - 1:LCH - 1:-1, 8:16, :], hm, None, ALU.mult)
            link(ins, "SHm_done")
            v.tensor_copy(tiny[:, 157:158], prm[:, 0:1]).then_inc(T_free, 1)

            ring.wait_emptied(dve, "zg1")
            link(v.scalar_tensor_tensor(gln, gz, -1.0, gz, ALU.mult, ALU.max), "gabs")
            mod_out("ada1", 16, 48)
            dve.wait_ge(S("glog"), 1)
            link(v.scalar_tensor_tensor(gz, gz, 0.0, gln, ALU.min, ALU.subtract))
            link(v.tensor_scalar(gz, gz, 1.0 / GATE_TAU, None, ALU.mult))
            v.tensor_tensor_scan(gb[:, 0, :], con("scan"), gz[:, 0, :], 0.0, ALU.mult, ALU.add)
            link(v.tensor_tensor_scan(gb[:, 1, ::-1], con("scan"), gz[:, 1, ::-1], 0.0, ALU.mult, ALU.add))

            def chunks(x):
                return x.rearrange("p (n c) -> p n c", c=CSZ)

            ring.wait_filled(dve, "ysel")
            y5, e5, g5, _ = fin5
            for a in range(2):
                ins = v.scalar_tensor_tensor(y5[:, a, :], uT[:, a, NCTX:], prm[:, R_S5D + a:R_S5D + a + 1],
                                             bank("ysel")[:, NLAT * a:NLAT * (a + 1)], ALU.mult, ALU.add)
            emptied(ins, "ysel")
            link(mul(e5, y5, y5))
            link(v.tensor_scalar(e5, e5, 0.044715, 1.0, ALU.mult, ALU.add))
            link(mul(e5, e5, y5), "gelu_in")
            for d in range(2):
                last = CSZ - 1 if d == 0 else 0
                ins = sub(chunks(gln[:, d, :]),
                          chunks(gb[:, d, :])[:, :, last:last + 1].to_broadcast([P, NCK, CSZ]), chunks(gb[:, d, :]))
            link(ins, "gscan")
            dve.wait_ge(S("gelu_exp"), 1)
            link(mul(y5, y5, e5), "gelu_ready")
            ring.wait_emptied(dve, "glu")
            link(mul(mixT[:, 2:4, :], y5, g5))

            dve.wait_ge(S("gexp"), 1)
            for d in range(2):
                for h in range(4):
                    ins = v.scalar_tensor_tensor(qm[:, d, h, :], qT, con("headm")[:, h:h + 1], qin[:, d, :], ALU.mult,
                                                 ALU.mult)
            link(ins)
            link(mul(qin, qin, qT.unsqueeze(1).to_broadcast([P, 2, NLAT])))
            mul(kin, kin, kTt[:, NCTX:].unsqueeze(1).to_broadcast([P, 2, NLAT]))
            link(mul(gln, gln, kTt.unsqueeze(1).to_broadcast([P, 2, NTOK])), "gla_ready")
            for d in range(2):
                ring.wait_filled(dve, f"kd{d}")
                for h in range(2):
                    ins = v.tensor_scalar(kdM[:, d, :, h, :], bank(f"kd{d}").rearrange("p (a n) -> p a n", a=4),
                                          con("halfm")[:, h:h + 1], None, ALU.mult)
                ring.mark_emptied(ins, f"kd{d}", "dve")
            for i in range(4):
                d, a = divmod(i, 2)
                ring.wait_filled(dve, f"att{i}")
                ring.mark_emptied(v.tensor_tensor(
                    att[:, d, a], bank(f"att{i}").rearrange("p (h t) -> p h t", h=4),
                    con("tri")[:, P * d:P * (d + 1)].unsqueeze(1).to_broadcast([P, 4, P]), ALU.mult), f"att{i}", "dve")
            hmask = con("headm").unsqueeze(2).to_broadcast([P, 4, 64])
            for n in range(NCK - 1):
                ring.wait_filled(dve, f"ds{n}")
                for d in range(2):
                    b_ = bank(f"ds{n}")[:, 256 * d:256 * (d + 1)]
                    chunk_ = n if d == 0 else (3 - n if n < 4 else 11 - n)
                    if n == 0:
                        ins = v.tensor_copy(Srun[:, d, :], b_)
                    else:
                        ins = v.scalar_tensor_tensor(Srun[:, d, :], Srun[:, d, :], gdec[:, d, chunk_:chunk_ + 1], b_,
                                                     ALU.mult, ALU.add)
                emptied(ins, f"ds{n}")
                if n >= 3:
                    for d in range(2):
                        ins = mul(SM[:, d, n - 3, :].rearrange("p (h n) -> p h n", h=4),
                                  Srun[:, d, :].rearrange("p (h n) -> p h n", h=4), hmask)
                    link(ins)
            v.tensor_copy(tiny[:, 156:157], prm[:, 0:1]).then_inc(S("SM_ready"), 1)
            ring.wait_filled(dve, "og")
            emptied(v.tensor_copy(go.rearrange("p a t -> p (a t)"), bank("og")), "og")
            v.tensor_copy(tiny[:, 155:156], prm[:, 0:1]).then_inc(S("go_ready"), 1)
            dve.wait_ge(S("gsl_ready"), 1)
            link(mul(gsl, gsl, rT))
            dve.wait_ge(S("gss_root"), 1)
            link(mul(go, go, grs))
            link(v.scalar_tensor_tensor(mixT[:, 4:6, :], go, prm[:, R_GLAG:R_GLAG + 1], gsl, ALU.mult, ALU.mult))

            for x in (dtR, cumR, wR):
                v.memset(x[0:ROW0, :], 0.0)
            link(v.tensor_scalar(dtR[ROW0:, :], miscT[ROW0:, :], prm[ROW0:, R_DTB:R_DTB + 1], None, ALU.add))
            link(v.scalar_tensor_tensor(tR[ROW0:, :], dtR[ROW0:, :], -1.0, dtR[ROW0:, :], ALU.mult, ALU.max), "dt_abs")
            n_ = PADW - 4
            for k in range(5):
                for a in range(4):
                    wc = prm[:, R_CONVW + 4 * k + a:R_CONVW + 4 * k + a + 1]
                    if k == 0:
                        ins = v.tensor_scalar(cv[:, a, 2:2 + n_], xbc[:, a, 0:n_], wc,
                                              prm[:, R_CONVB + a:R_CONVB + a + 1], ALU.mult, ALU.add)
                    else:
                        ins = v.scalar_tensor_tensor(cv[:, a, 2:2 + n_], xbc[:, a, k:k + n_], wc, cv[:, a, 2:2 + n_],
                                                     ALU.mult, ALU.add)
                if k == 0:
                    v.memset(cv[:, :, 0:2], 0.0)
                    ins = v.memset(cv[:, :, 2 + n_:], 0.0)
                link(ins)
            v.tensor_copy(tiny[:, 154:155], prm[:, 0:1]).then_inc(S("conv_ready"), 1)
            dve.wait_ge(S("dt_log"), 1)
            link(v.scalar_tensor_tensor(dtR[ROW0:, :], dtR[ROW0:, :], 0.0, tR[ROW0:, :], ALU.max, ALU.add))
            link(v.tensor_scalar(tR[ROW0:, :], dtR[ROW0:, :], anegc[ROW0:, :], -1.0, ALU.mult, ALU.mult))
            v.tensor_tensor_scan(cumR[64:96, :], con("scan")[64:96, :], tR[64:96, :], 0.0, ALU.mult, ALU.add)
            link(v.tensor_tensor_scan(cumR[96:128, ::-1], con("scan")[96:128, :], tR[96:128, ::-1], 0.0, ALU.mult,
                                      ALU.add))
            for d in range(2):
                last = CSZ - 1 if d == 0 else 0
                a, b = ROW0 + 32 * d, ROW0 + 32 * d + 32
                ins = sub(chunks(wR[a:b, :]), chunks(cumR[a:b, :])[:, :, last:last + 1].to_broadcast([32, NCK, CSZ]),
                          chunks(cumR[a:b, :]))
            link(ins, "cum_ready")
            dve.wait_ge(S("w_exp"), 1)
            link(mul(wR[ROW0:, :], wR[ROW0:, :], dtR[ROW0:, :]), "rows_ready")
            dve.wait_ge(S("conv_exp"), 1)
            mul(XC[:, :, 0:NCTX], cv[:, :, 2:2 + NCTX], ce[:, :, 2:2 + NCTX])

            def lat_rows(tile, a):
                return tile[:, a, NCTX + 4:].rearrange("p (r w) -> p r w", w=CSZ + 4)[:, :, 2:2 + CSZ]

            for a in range(4):
                ins = mul(XC[:, a, NCTX:].rearrange("p (r w) -> p r w", w=CSZ), lat_rows(cv, a), lat_rows(ce, a))
            link(ins, "XC_ready")
            for g in range(2):
                ins = v.tensor_scalar(Cg[:, g, :], XC[:, 3, NCTX:], con("halfm")[:, g:g + 1], None, ALU.mult)
            link(ins, "Cg_ready")
            for i in range(3):
                ring.wait_filled(dve, f"rT{i}")
                src = bank(f"rT{i}").rearrange("p (a m x) -> p a m x", a=4, m=4)[:, :, 2:4, 0:4]
                emptied(v.tensor_copy(cols[:, i], src), f"rT{i}")

            def heads(x):
                return x.rearrange("p (h n) -> p h n", h=4)

            for a in range(4):
                ring.wait_filled(dve, f"xt{a}")
                xb = heads(bank(f"xt{a}")[:, 0:256])
                for d in range(2):
                    mul(heads(xdec[:, a, d, :]), xb, cols[:, 2, a, d, :].unsqueeze(2).to_broadcast([P, 4, 64]))
                    if a >= 2:
                        mul(heads(xdt[:, a - 2, d, :]), xb, cols[:, 0, a, d, :].unsqueeze(2).to_broadcast([P, 4, 64]))
                for h in range(2):
                    ins = v.tensor_scalar(BTM[:, a, h, :], bank(f"xt{a}")[:, 256:384], con("halfm")[:, h:h + 1], None,
                                          ALU.mult)
                ring.mark_emptied(ins, f"xt{a}", "dve")
            for i in range(4):
                dve.wait_ge(S("ecr_ready"), i + 1)
                for r in (2 * i, 2 * i + 1):
                    d, h = divmod(r, 4)
                    for a in range(2):
                        o = NLAT * (r % 2) + P * a
                        ins = v.scalar_tensor_tensor(SEG[:, r, a, :], bank(f"rb{i}")[:, o:o + P],
                                                     cols[:, 1, 2 + a, d, h:h + 1], con("neg")[:, P * d:P * (d + 1)],
                                                     ALU.subtract, ALU.add)
                ring.mark_emptied(ins, f"rb{i}", "dve")
            v.tensor_copy(tiny[:, 152:153], prm[:, 0:1]).then_inc(S("seg_ready"), 1)
            for d in range(2):
                e4 = ECR[:, 4 * d:4 * d + 4, :].rearrange("p (g h) t -> p g h t", g=2)
                ins = mul(e4, e4, Cg.unsqueeze(2).to_broadcast([P, 2, 2, NLAT]))
            link(ins)
            dve.wait_ge(S("seg_exp"), 1)
            for a in range(2):
                ring.wait_filled(dve, f"bc{a}")
                bc_ = bank(f"bc{a}")[:, 0:256].rearrange("p (g t) -> p g t", g=2).unsqueeze(2).to_broadcast([P, 2, 2, P])
                for d in range(2):
                    s4 = SEG[:, 4 * d:4 * d + 4, a, :].rearrange("p (g h) t -> p g h t", g=2)
                    ins = mul(s4, s4, bc_)
                ring.mark_emptied(ins, f"bc{a}", "dve")
            for n in range(NCK - 1):
                ring.wait_filled(dve, f"sds{n}")
                for d in range(2):
                    b_ = bank(f"sds{n}")[:, 256 * d:256 * (d + 1)]
                    chunk_ = n if d == 0 else (3 - n if n < 4 else 11 - n)
                    dst = SSrun[:, d, :] if n < 3 else SE[:, d, n - 3, :]
                    if n == 0:
                        ins = v.tensor_copy(dst, b_)
                    else:
                        prev = SSrun[:, d, :] if n <= 3 else SE[:, d, n - 4, :]
                        link(mul(heads(dst), heads(prev),
                                 DEC[:, 4 * d:4 * d + 4, chunk_].unsqueeze(2).to_broadcast([P, 4, 64])))
                        ins = add(dst, dst, b_)
                emptied(ins, f"sds{n}")
            v.tensor_copy(tiny[:, 151:152], prm[:, 0:1]).then_inc(S("SE_ready"), 1)
            sy, ssq_, srt, ssl = fin5
            dve.wait_ge(S("sz_exp"), 1)
            link(mul(ssl, ssl, zT))
            ring.wait_filled(dve, "oy")
            for a in range(2):
                ins = v.scalar_tensor_tensor(sy[:, a, :], XC[:, a, NCTX:], s5p[:, PAIR_D + a:PAIR_D + a + 1],
                                             bank("oy")[:, NLAT * a:NLAT * (a + 1)], ALU.mult, ALU.add)
            emptied(ins, "oy")
            link(mul(sy, sy, ssl), "yz_ready")
            dve.wait_ge(S("yss_root"), 1)
            for a in range(2):
                ins = v.scalar_tensor_tensor(mixT[:, 6 + a, :], sy[:, a, :], prm[:, R_SSDG + a:R_SSDG + a + 1],
                                             srt[:, 0, :], ALU.mult, ALU.mult)
            link(ins, "mixers_done")
            v.memset(bgu, 0.0).then_inc(S("bgu_zeroed"), 1)

            for i in range(4):
                ring.wait_filled(dve, f"wo{i}")
                for o in (2 * i, 2 * i + 1):
                    ins = v.scalar_tensor_tensor(xT[:, o, :], bank(f"wo{i}")[:, NLAT * (o % 2):NLAT * (o % 2) + NLAT],
                                                 mod[:, 16 + o, 0:1], xT[:, o, :], ALU.mult, ALU.add)
                    if o % 2 == 0:
                        link(ins, "x2_ready")
                emptied(ins, f"wo{i}")
                v.tensor_copy(tiny[:, 150:151], prm[:, 0:1]).then_inc(S("x2_ready"), 1)
                counts["x2_ready"] += 1
            g2 = tiny[:, 60:68].unsqueeze(2)
            gain(g2, mod[:, 32:40, 0:1], R_GFFN)
            dve.wait_ge(S("ss2_root"), 1)
            link(mul(h2T, xT, mixT[:, 0:1, :].to_broadcast([P, KT, NLAT])))
            for k in range(KT):
                ins = v.tensor_scalar(h2T[:, k, :], h2T[:, k, :], g2[:, k, :], mod[:, 24 + k, 0:1], ALU.mult, ALU.add)
            link(ins, "h2T_ready")
            v.memset(Em, 0.0)
            v.memset(ey, 0.0).then_inc(S("y_ready"), 1)

            ring.wait_filled(dve, "lg")
            dve.wait_ge(S("router_in"), 32)
            emptied(v.tensor_tensor(lg, bank("lg")[:, 0:64].rearrange("p (a e) -> p a e", a=2),
                                    rbias.unsqueeze(1).to_broadcast([P, 2, NE]), ALU.add), "lg")
            for a in range(2):
                ins = v.max(top[:, a, :], lg[:, a, :])
            link(ins)
            link(v.tensor_scalar(nmax, top[:, :, 0], -1.0, None, ALU.mult), "lmax_ready")
            for a in range(2):
                th = top[:, a, TOPK - 1:TOPK]
                v.tensor_scalar(gt[:, a, :], lg[:, a, :], th, None, ALU.is_gt)
                ins = v.tensor_scalar(eq[:, a, :], lg[:, a, :], th, None, ALU.is_equal)
            link(ins)
            link(v.tensor_reduce(need[:, :, 0], gt, AX.X, ALU.add))
            link(v.tensor_scalar(need[:, :, 0], need[:, :, 0], -1.0, float(TOPK), ALU.mult, ALU.add))
            for a in range(2):
                ins = v.tensor_tensor_scan(rank[:, a, :], con("ones")[:, 0:NE], eq[:, a, :], 0.0, ALU.mult, ALU.add)
            link(ins)
            for a in range(2):
                ins = v.scalar_tensor_tensor(eq[:, a, :], rank[:, a, :], need[:, a, 0:1], eq[:, a, :], ALU.is_le,
                                             ALU.mult)
            link(ins)
            link(add(sel, gt, eq), "sel_ready")
            dve.wait_ge(S("gate_exp"), 1)
            link(mul(gate, gate, sel))
            link(v.tensor_reduce(zsum, gate, AX.X, ALU.add))
            link(v.reciprocal(zsum, zsum))
            link(mul(gate, gate, zsum.unsqueeze(2).to_broadcast([P, 2, NE])))
            ring.wait_filled(dve, "pos")
            emptied(v.tensor_tensor(posm, bank("pos")[:, 0:64].rearrange("p (a e) -> p a e", a=2), sel, ALU.mult),
                    "pos")
            v.tensor_copy(tiny[:, 149:150], prm[:, 0:1]).then_inc(S("posm_ready"), 1)
            ring.wait_filled(dve, "pgT")
            v.tensor_copy(posT[0:NE, :], bank("pgT")[0:NE, 0:256])
            emptied(v.tensor_copy(gatT[0:NE, :], bank("pgT")[0:NE, 256:512]), "pgT")
            ring.wait_filled(dve, "cnt")
            ne = slice(0, NE)
            emptied(v.tensor_copy(nb[ne, 1:2], bank("cnt")[ne, 0:1]), "cnt")
            link(v.tensor_scalar(nb[ne, 0:1], nb[ne, 1:2], 0.0, con("first", NE), ALU.is_gt, ALU.max))
            for b_ in range(1, -(-NLAT // CAP)):
                link(v.scalar_tensor_tensor(nb[ne, 0:1], nb[ne, 1:2], float(CAP * b_), nb[ne, 0:1], ALU.is_gt, ALU.add))
            v.tensor_copy(tiny[:, 148:149], prm[:, 0:1]).then_inc(S("nb_ready"), 1)
            ring.wait_filled(dve, "start")
            emptied(v.tensor_copy(nb[ne, 2:3], bank("start")[ne, 0:1]), "start")
            link(v.tensor_scalar(Et[ne, :], con("items", NE), nb[ne, 2:3], None, ALU.subtract))
            link(v.tensor_scalar(Em[ne, :], Et[ne, :], 0.0, None, ALU.is_ge))
            link(v.scalar_tensor_tensor(Em[ne, :], Et[ne, :], nb[ne, 0:1], Em[ne, :], ALU.is_lt, ALU.mult))
            link(v.tensor_scalar(Et[ne, :], Et[ne, :], -float(CAP), None, ALU.mult))
            link(mul(Eb[ne, :], Et[ne, :], Em[ne, :]), "E_ready")
            ring.wait_filled(dve, "it0")
            i4 = bank("it0")[:, 0:4 * NI].rearrange("p (w i) -> p w i", w=4)
            v.tensor_copy(posI, i4[:, 0:2, :])
            emptied(v.tensor_copy(gatI, i4[:, 2:4, :]), "it0")
            ring.wait_filled(dve, "ids")
            emptied(v.tensor_copy(ids[0:1, :], bank("ids")[0:1, 0:NI + 1]), "ids")
            v.tensor_copy(tiny[:, 147:148], prm[:, 0:1]).then_inc(S("ids_ready"), 1)

            def select(col):
                for a in range(2):
                    ins = v.tensor_tensor(Ssel[:, a, :], con("iota")[:, 0:CAP],
                                          posI[:, a, bass.ds(col, 1)].to_broadcast([P, CAP]), ALU.is_equal)
                return ins

            def gates(col):
                for a in range(2):
                    ins = v.tensor_tensor(Sgat[:, a, :], con("iota"),
                                          posI[:, a, bass.ds(col, 1)].to_broadcast([P, 2 * CAP]), ALU.is_equal)
                ins.then_inc(S("sgat_chain"), 1)

            def scale_gates(col):
                v.tensor_tensor(Sgat, Sgat, gatI[:, :, bass.ds(col, 1)].to_broadcast([P, 2, 2 * CAP]),
                                ALU.mult).then_inc(S("sgat_ready"), 1)

            def gt_out(n):
                dve.wait_ge(S("gt_full"), n)
                dve.wait_ge(S("sc_full"), n)
                v.tensor_copy(GT, psum[:, 2, 0:NLAT]).then_inc(S("gt_ready"), 1)

            select(1).then_inc(S("s_ready"), 1)
            n_items = dve.value_load(ids[0:1, NI:NI + 1], min_val=2, max_val=NI - 2)

            dve.sem_inc(S("gu_emptied"), 1)
            gates(0)
            dve.wait_ge(S("sgat_chain"), 1)
            scale_gates(0)
            with dve.Fori(0, n_items) as it:
                dve.wait_ge(S("g_full"), it + 1)
                v.tensor_copy(Ecol, Em[:, bass.ds(it + 1, 1)].to_broadcast([P, CAP])).then_inc(S("Ecol_ready"), 1)
                select(it + 2).then_inc(S("s_ready"), 1)
                gt_out(it + 1)
                gates(it + 1)
                dve.wait_ge(S("sgat_chain"), it + 2)
                scale_gates(it + 1)
                dve.wait_ge(S("gu_full"), it + 1)
                gu = psum[:, 0:2, :].rearrange("p b (f w) -> p b f w", w=2)
                eg2, eu2 = (x.rearrange("p (b f) -> p b f", b=2) for x in (eg, eu))
                v.tensor_scalar(eg2, gu[:, :, :, 0], LIMIT, None, ALU.min).then_inc(S("gclip_ready"), 1)
                v.tensor_scalar(eu2, gu[:, :, :, 1], LIMIT, -LIMIT, ALU.min, ALU.max).then_inc(S("gu_emptied"), 1)
                dve.wait_ge(S("gclip_ready"), it + 1)
                dve.wait_ge(S("gu_emptied"), it + 2)
                v.scalar_tensor_tensor(eu, eu, 1.0, eg, ALU.add, ALU.mult).then_inc(S("ug_ready"), 1)
                dve.wait_ge(S("ug_ready"), it + 1)
                dve.wait_ge(S("sig_ready"), it + 1)
                v.tensor_tensor(eu, eu, es, ALU.mult).then_inc(S("act_ready"), 1)
                dve.wait_ge(S("at_full"), it + 1)
            gt_out(n_items + 1)
            dve.wait_ge(S("sc_full"), n_items + 2)
            for k in range(KT):
                ins = v.scalar_tensor_tensor(xT[:, k, :], facc[:, k, :], mod[:, 40 + k, 0:1], xT[:, k, :], ALU.mult,
                                             ALU.add)
            link(ins, "x3_ready")
            dve.wait_ge(S("last_root"), 1)
            dve.wait_ge(S("gfin_in"), 16)
            for a in range(2):
                v.scalar_tensor_tensor(h2TM[:, a, :].rearrange("p (b n) -> p b n", b=2), psum[:, 2 * a:2 * a + 2, :],
                                       tiny[:, 52 + a:53 + a], gfin.rearrange("p (b n) -> p b n", b=2),
                                       ALU.mult, ALU.mult).then_inc(S("out_ready"), 1)

        @block.tensor
        def _(pe):
            mm = nc.tensor.matmul

            def start(name):
                ring.wait_free(pe, name)
                return bank(name)

            def transposed(o, x):
                n = x.shape[0]
                return nc.tensor.transpose(o, x, ident[0:n, 0:n])

            pe.wait_ge(const_in, 16)
            pe.wait_ge(par_in, 16 * (10 + 2 * 3 + 2))
            ring.mark_filled(transposed(start("par")[:, 0:NPAR], par1[0:NPAR, :]))
            pe.wait_ge(S("pairs_spread"), 4)
            ring.mark_filled(transposed(start("s5par")[:, 0:NPAR2], par2[0:NPAR2, :]))
            pe.wait_ge(S("s5c_in"), 16 * 4)
            for r in range(2):
                b = start(f"cpar{r}")
                for i in range(4):
                    ins = transposed(b[:, P * i:P * (i + 1)], crow[:, r, i, :])
                ring.mark_filled(ins)
            pe.wait_ge(x_in, 64)
            for i in range(4):
                b = start(f"xraw{i}")
                for j in range(4):
                    k = 2 * i + j // 2
                    ins = transposed(b[:, P * j:P * (j + 1)], staging[:, 2 + j % 2, P * k:P * (k + 1)])
                ring.mark_filled(ins)

            def wait_slot(n):
                pe.wait_ge(loaded[n % FR], 16 * (n // FR + 1))

            def ada_blocks(name, first, last):
                bk = start(name)
                for blk in range(first, last):
                    n = AT[("ada", blk)]
                    wait_slot(n)
                    for o in range(2):
                        at_ = 2 * (2 * (blk - first) + o)
                        for k in range(KT):
                            ins = mm(bk[:, at_:at_ + 2], sview(n)[:, k, P * o:P * (o + 1)], cond[:, k, :],
                                     start=(k == 0), stop=(k == KT - 1))
                    if blk < last - 1:
                        ins.then_inc(slot_read, 1)
                return ins

            def both(ins):
                ring.mark_filled(ins)
                pe.wait_ge(filled, ring.done["pe"])
                pe.sem_inc(slot_read, 1)

            pe.wait_ge(S("cond_silu"), 1)
            both(ada_blocks("ada0", 0, 8))

            pe.wait_ge(V_ready, 1)
            for i in range(8):
                b = start(f"VT{i}")
                for j in range(4):
                    g, r = divmod(4 * i + j, 2)
                    ins = transposed(b[:, P * j:P * (j + 1)], V[:, g, r, :])
                ring.mark_filled(ins)
            pe.wait_ge(S("C0_done"), 1)
            b = start("Kq")
            for d in range(2):
                for g in range(NG):
                    dg, o = 8 * d + g // 2, CH * (NG * d + g)
                    for r in range(2):
                        ins = mm(b[:, o:o + CH], V[:, dg, r, :], c0[:, g % 2, dg, r, :], start=(r == 0), stop=(r == 1))
            ring.mark_filled(ins)

            pe.wait_ge(xn_ready, 1)
            for k in range(KT):
                b = start(f"xn{k}")
                for i in range(4):
                    ins = transposed(b[:, P * i:P * (i + 1)], staging[:, i, P * k:P * (k + 1)])
                ring.mark_filled(ins)

            ring.wait_emptied(pe, f"xn{KT - 1}")

            def feature_major(o, n, c0_, toks):
                for k in range(KT):
                    ins = mm(o, sview(n)[:, k, c0_:c0_ + P], hT[:, k, toks], start=(k == 0), stop=(k == KT - 1))
                return ins

            every, lat = slice(0, NTOK), slice(NCTX, NTOK)

            def two_lat(name, blk):
                n = AT[("win", blk)]
                wait_slot(n)
                b = start(name)
                for o in range(2):
                    ins = feature_major(b[:, NLAT * o:NLAT * (o + 1)], n, P * o, lat)
                return ins

            both(two_lat("four", W_FOUR))
            n = AT[("win", W_U)]
            wait_slot(n)
            ring.mark_filled(feature_major(start("u0"), n, 0, every))
            both(feature_major(start("u1"), n, P, every))
            n = AT[("win", W_QK)]
            wait_slot(n)
            ring.mark_filled(feature_major(start("q")[:, 0:NLAT], n, 0, lat))
            both(feature_major(start("k"), n, P, every))
            n = AT[("win", W_V)]
            wait_slot(n)
            for i in range(2):
                b = start(f"v{i}")
                for a in (2 * i, 2 * i + 1):
                    for k in range(KT):
                        ins = mm(b[:, 256 * (a % 2):256 * (a % 2 + 1)], hT[:, k, P * a:P * (a + 1)], sview(n)[:, k, :],
                                 start=(k == 0), stop=(k == KT - 1))
                if i == 0:
                    ring.mark_filled(ins)
            both(ins)
            both(two_lat("r", W_R))
            n = AT[("win", W_MISC)]
            pe.wait_ge(S("misc_in"), 32)
            wait_slot(n)
            both(feature_major(start("misc"), n, 0, every))
            both(two_lat("z", W_Z))
            n = AT[("win", W_X)]
            wait_slot(n)
            ring.mark_filled(feature_major(start("x0"), n, 0, every))
            both(feature_major(start("x1"), n, P, every))
            n = AT[("win", W_BC)]
            wait_slot(n)
            ring.mark_filled(feature_major(start("B"), n, 0, every))
            both(feature_major(start("C")[:, 0:NLAT], n, P, lat))

            ring.wait_emptied(pe, "four")
            for i in range(2):
                b = start(f"fA{i}")
                for f in range(2):
                    ins = mm(b[:, 256 * f:256 * (f + 1)], fourT[:, f, P * i:P * (i + 1)], con("cbd"), start=True,
                             stop=True)
                ring.mark_filled(ins)
            ring.wait_emptied(pe, "fA1")
            b = start("fB")
            for f in range(2):
                for i in range(2):
                    for w, tab in enumerate(("cseq", "sseq")):
                        ins = mm(b[:, NLAT * f:NLAT * (f + 1)], fA[:, i, f, P * w:P * (w + 1)],
                                 con(tab)[:, NLAT * i:NLAT * (i + 1)], start=(i + w == 0), stop=(i + w == 2))
            ring.mark_filled(ins)
            pe.wait_ge(fw_in, 16)
            ring.wait_emptied(pe, "fB")
            b = start("fW")
            for o in range(2):
                for k in range(2):
                    ins = mm(b[:, NLAT * o:NLAT * (o + 1)], fourw[:, k, P * o:P * (o + 1)], fourT[:, k, :],
                             start=(k == 0), stop=(k == 1))
            ring.mark_filled(ins)

            selw = con("sel").rearrange("p (b x) -> p b x", b=8)

            def window(b_, place):
                return selw[:, b_, 16 * (7 - place):16 * (7 - place) + P]

            for i in range(2):
                b = start(f"U{i}")
                for g in range(8):
                    for j in range(Q):
                        ins = mm(b[:, NCH * g:NCH * (g + 1)], window(g, j), uT[:, i, j::Q], start=(j == 0),
                                 stop=(j == Q - 1))
                ring.mark_filled(ins)
            ring.wait_emptied(pe, "U1")
            for i in range(4):
                b = start(f"D{i}")
                for r in range(2):
                    for j in range(4):
                        dg = 4 * i + j
                        for h in range(2):
                            o = NCH * (4 * r + j)
                            ins = mm(b[64 * h:64 * h + 64, o:o + NCH], VT[:, dg, r, 64 * h:64 * h + 64],
                                     U[:, 2 * (dg % 8) + h, :], start=True, stop=True)
                ring.mark_filled(ins)

            pe.wait_ge(a2_in, 32)
            for d in range(2):
                ring.mark_filled(mm(start(f"zg{d}"), a2[0:32, P * d:P * (d + 1)], miscT[0:32, :], start=True, stop=True))
            both(ada_blocks("ada1", 8, 24))

            pe.wait_ge(T_in, 16 * 2 * Q)
            pe.wait_ge(S("SHm_done"), 1)
            b = start("Y")
            for g in range(NG):
                o = b[:, LCH * g:LCH * (g + 1)]
                for d in range(2):
                    mm(o, T5[:, g, d, :], U[:, g, LCH:], start=(d == 0), stop=False)
                for d in range(2):
                    for r in range(2):
                        dg = 8 * d + g // 2
                        ins = mm(o, Cc[:, dg, r, :], SHm[:, g % 2, :, dg, r], start=False, stop=(d + r == 2))
            ring.mark_filled(ins)
            ring.wait_emptied(pe, "Y")
            b = start("ysel")
            for a in range(2):
                for i in range(Q):
                    for g in range(8):
                        ins = mm(b[:, NLAT * a + i:NLAT * (a + 1):Q], window(i, g), YS[:, 8 * a + g, :],
                                 start=(g == 0), stop=(g == 7))
            ring.mark_filled(ins)
            pe.wait_ge(glu_in, 16)
            pe.wait_ge(S("gelu_ready"), 1)
            b = start("glu")
            for o in range(2):
                for k in range(2):
                    ins = mm(b[:, NLAT * o:NLAT * (o + 1)], gluw[:, k, P * o:P * (o + 1)], fin5[0][:, k, :],
                             start=(k == 0), stop=(k == 1))
            ring.mark_filled(ins)

            pe.wait_ge(S("gla_ready"), 1)
            for d in range(2):
                b = start(f"kd{d}")
                for a in range(4):
                    ins = transposed(b[:, P * a:P * (a + 1)], gln[:, d, P * a:P * (a + 1)])
                ring.mark_filled(ins)
            for i in range(4):
                d, a = divmod(i, 2)
                ring.mark_filled(mm(start(f"att{i}").rearrange("p (h t) -> p h t", h=4), kin[:, d, P * a:P * (a + 1)],
                                    qm[:, d, :, P * a:P * (a + 1)], start=True, stop=True))

            def chunk_at(n, d):
                return divmod(n if d == 0 else (3 - n if n < 4 else 11 - n), 2)

            ring.wait_emptied(pe, "kd1")
            for n in range(NCK - 1):
                b = start(f"ds{n}")
                for d in range(2):
                    a, h = chunk_at(n, d)
                    ins = mm(b[:, 256 * d:256 * (d + 1)], kdM[:, d, a, h, :], vTM[:, a, :], start=True, stop=True)
                ring.mark_filled(ins)
            pe.wait_ge(S("SM_ready"), 1)
            ring.wait_emptied(pe, "att3")
            b = start("og")
            for vt in range(2):
                for a in range(2):
                    o = NLAT * vt + P * a
                    for d in range(2):
                        for h in (2 * vt, 2 * vt + 1):
                            q0 = 64 * (h % 2)
                            mm(b[q0:q0 + 64, o:o + P], vTM[:, 2 + a, 64 * h:64 * h + 64], att[:, d, a, h, :],
                               start=(d == 0), stop=False, skip_group_check=True)
                    for d in range(2):
                        for c in (2 * a, 2 * a + 1):
                            step = c if d == 0 else 3 - c
                            ins = mm(b[:, NLAT * vt + CSZ * c:NLAT * vt + CSZ * (c + 1)], SM[:, d, step, P * vt:P * (vt + 1)],
                                     qin[:, d, CSZ * c:CSZ * (c + 1)], start=False, stop=(d == 1),
                                     skip_group_check=True)
            ring.mark_filled(ins)
            pe.wait_ge(S("gsq_ready"), 1)
            ring.mark_filled(mm(start("gss"), con("blk64"), gsq.rearrange("p a t -> p (a t)"), start=True, stop=True))

            pe.wait_ge(S("rows_ready"), 1)
            for i, x in enumerate((dtR, cumR, wR)):
                b = start(f"rT{i}")
                for a in range(4):
                    ins = transposed(b[:, P * a:P * (a + 1)], x[:, P * a:P * (a + 1)])
                ring.mark_filled(ins)
            pe.wait_ge(S("XC_ready"), 1)
            for a in range(4):
                b = start(f"xt{a}")
                for j in range(3):
                    ins = transposed(b[:, P * j:P * (j + 1)], XC[:, j, P * a:P * (a + 1)])
                ring.mark_filled(ins)
            rowsel = con("rows").rearrange("p (r n) -> p r n", r=8)
            b = start("decl")
            for r in range(8):
                last = CSZ - 1 if r < 4 else 0
                ins = mm(b[:, 8 * r:8 * r + 8], rowsel[:, r, :], cumR[:, last::CSZ], start=True, stop=True)
            ring.mark_filled(ins)
            for i in range(4):
                b = start(f"rb{i}")
                for r in (2 * i, 2 * i + 1):
                    ins = mm(b[:, NLAT * (r % 2):NLAT * (r % 2 + 1)], rowsel[:, r, :], cumR[:, NCTX:], start=True,
                             stop=True)
                ring.mark_filled(ins)
            pe.wait_ge(S("Cg_ready"), 1)
            for a in range(2):
                b = start(f"bc{a}")
                ring.mark_filled(mm(b[:, 0:256].rearrange("p (g t) -> p g t", g=2),
                                    XC[:, 2, NCTX + P * a:NCTX + P * (a + 1)], Cg[:, :, P * a:P * (a + 1)],
                                    start=True, stop=True))
            ring.wait_emptied(pe, "xt3")
            for n in range(NCK - 1):
                b = start(f"sds{n}")
                for d in range(2):
                    a, h = chunk_at(n, d)
                    ins = mm(b[:, 256 * d:256 * (d + 1)], BTM[:, a, h, :], xdec[:, a, d, :], start=True, stop=True)
                ring.mark_filled(ins)
            pe.wait_ge(S("SE_ready"), 1)
            b = start("oy")
            for h in range(4):
                q0, o0 = 64 * (h % 2), NLAT * (h // 2)
                hs = slice(64 * h, 64 * h + 64)
                for a in range(2):
                    for d in range(2):
                        mm(b[q0:q0 + 64, o0 + P * a:o0 + P * (a + 1)], xdt[:, a, d, hs], SEG[:, 4 * d + h, a, :],
                           start=(d == 0), stop=False, skip_group_check=True)
                    for d in range(2):
                        for c in (2 * a, 2 * a + 1):
                            step = c if d == 0 else 3 - c
                            ins = mm(b[q0:q0 + 64, o0 + CSZ * c:o0 + CSZ * (c + 1)], SE[:, d, step, hs],
                                     ECR[:, 4 * d + h, CSZ * c:CSZ * (c + 1)], start=False, stop=(d == 1),
                                     skip_group_check=True)
            ring.mark_filled(ins)
            pe.wait_ge(S("ysq_ready"), 1)
            b = start("yss")
            for a in range(2):
                ins = mm(b[:, 0:NLAT], con("ones"), fin5[1][:, a, :], start=(a == 0), stop=(a == 1))
            ring.mark_filled(ins)

            pe.wait_ge(S("mixers_done"), 1)
            for i in range(4):
                n = AT[("wout", i)]
                wait_slot(n)
                b = start(f"wo{i}")
                for o in range(2):
                    for k in range(KT):
                        ins = mm(b[:, NLAT * o:NLAT * (o + 1)], sview(n)[:, k, P * o:P * (o + 1)], mixT[:, k, :],
                                 start=(k == 0), stop=(k == KT - 1))
                both(ins)
            pe.wait_ge(S("xsq_ready"), 1)
            b = start("ss2")
            for k in range(KT):
                ins = mm(b[:, 0:NLAT], con("ones"), xsq[:, k, :], start=(k == 0), stop=(k == KT - 1))
            ring.mark_filled(ins)
            pe.wait_ge(S("h2T_ready"), 1)
            for i in range(4):
                b = start(f"h2{i}")
                for j in range(4):
                    a, k = j // 2, 2 * i + j % 2
                    ins = transposed(b[:, P * j:P * (j + 1)], h2T[:, k, P * a:P * (a + 1)])
                ring.mark_filled(ins)

            pe.wait_ge(S("router_in"), 32)
            b = start("lg")
            for a in range(2):
                for k in range(KT):
                    ins = mm(b[:, NE * a:NE * (a + 1)], h2T[:, k, P * a:P * (a + 1)], rw[:, k, :], start=(k == 0),
                             stop=(k == KT - 1))
            ring.mark_filled(ins)
            pe.wait_ge(S("sel_ready"), 1)
            b = start("pos")
            mm(b[:, 0:NE], con("incl"), sel[:, 0, :], start=True, stop=True)
            mm(b[:, NE:2 * NE], con("incl"), sel[:, 1, :], start=True, stop=False)
            ring.mark_filled(mm(b[:, NE:2 * NE], con("ones"), sel[:, 0, :], start=False, stop=True))
            pe.wait_ge(S("posm_ready"), 1)
            b = start("pgT")
            for j, x in enumerate((posm, gate)):
                for a in range(2):
                    o = 256 * j + P * a
                    ins = transposed(b[0:NE, o:o + P], x[:, a, :])
            ring.mark_filled(ins)
            b = start("cnt")
            for a in range(2):
                ins = mm(b[0:NE, 0:1], sel[:, a, :], con("ones")[:, 0:1], start=(a == 0), stop=(a == 1))
            ring.mark_filled(ins)
            pe.wait_ge(S("nb_ready"), 1)
            ne = slice(0, NE)
            ring.mark_filled(mm(start("start")[0:NE, 0:1], con("strict", NE), nb[ne, 0:1], start=True, stop=True))
            pe.wait_ge(S("E_ready"), 1)
            b = start("it0")
            for a in range(2):
                mm(b[:, NI * a:NI * (a + 1)], posT[ne, P * a:P * (a + 1)], Em[ne, :], start=True, stop=False)
                mm(b[:, NI * a:NI * (a + 1)], con("ones", NE), Eb[ne, :], start=False, stop=True)
            for a in range(2):
                ins = mm(b[:, NI * (2 + a):NI * (3 + a)], gatT[ne, P * a:P * (a + 1)], Em[ne, :], start=True, stop=True)
            ring.mark_filled(ins)
            b = start("ids")
            mm(b[0:1, 0:NI], con("evec", NE), Em[ne, :], start=True, stop=True)
            ring.mark_filled(mm(b[0:1, NI:NI + 1], nb[ne, 0:1], con("ones", NE)[:, 0:1], start=True, stop=True))
            pe.wait_ge(S("bias_in"), 32)
            for name in ring.names[-8:]:
                ring.wait_emptied(pe, name)
            for k in range(KT):
                mm(facc[:, k, :], bdn[:, P * k:P * (k + 1)], gatT[ne, :], start=(k % 2 == 0), stop=False,
                   skip_group_check=True)

            n_items = pe.value_load(ids[0:1, NI:NI + 1], min_val=2, max_val=NI - 2)
            halves = [slice(CAP * h, CAP * (h + 1)) for h in range(2)]

            def gather(count):
                pe.wait_ge(S("s_ready"), count)
                for j in range(KT):
                    for a in range(2):
                        ins = mm(psum[:, 3, CAP * j:CAP * (j + 1)], h2TM[:, a, P * j:P * (j + 1)], Ssel[:, a, :],
                                 start=(a == 0), stop=(a == 1))
                ins.then_inc(S("g_full"), 1)

            def turn_gates(count):
                pe.wait_ge(S("sgat_ready"), count)
                for a in range(2):
                    ins = transposed(psum[:, 2, P * a:P * (a + 1)], Sgat[:, a, :])
                ins.then_inc(S("gt_full"), 1)

            def scatter(count):
                pe.wait_ge(S("y_ready"), count)
                pe.wait_ge(S("gt_ready"), count)
                for k in range(KT // 2):
                    for h, q in enumerate(halves):
                        ins = mm(facc[:, 4 * h + k, :], ey[q, P * k:P * (k + 1)], GT[q, :], start=False, stop=False,
                                 skip_group_check=True)
                ins.then_inc(S("sc_full"), 1)

            pe.sem_inc(S("sc_full"), 1)
            gather(1)
            with pe.Fori(0, n_items) as it:
                turn_gates(it + 1)
                pe.wait_ge(S("Ecol_ready"), it + 1)
                pe.wait_ge(S("hg_ready"), it + 1)
                pe.wait_ge(S("gu_emptied"), it + 1)
                for b_ in range(2):
                    for h, q in enumerate(halves):
                        mm(psum[q, b_, :], Ecol, bgu[:, 1024 * h + 512 * b_:1024 * h + 512 * (b_ + 1)], start=True, stop=False,
                           skip_group_check=True)
                for c in range(KT):
                    pe.wait_ge(loaded[c], 16 * it + 16 * (uses[c] + 1))
                    for b_ in range(2):
                        for h, q in enumerate(halves):
                            ins = mm(psum[q, b_, :], hg[:, c, :],
                                     slot(c)[:, 1024 * h + 512 * b_:1024 * h + 512 * (b_ + 1)], start=False,
                                     stop=(c == KT - 1), skip_group_check=True)
                    ins.then_inc(slot_read if c < KT - 1 else S("gu_full"), 1)
                pe.wait_ge(S("y_ready"), it + 1)
                gather(it + 2)
                scatter(it + 1)
                pe.wait_ge(S("act_ready"), it + 1)
                for i in range(4):
                    ins = transposed(psum[:, 2, P * i:P * (i + 1)], eu[:, P * i:P * (i + 1)])
                ins.then_inc(S("at_full"), 1)
                pe.wait_ge(S("aT_ready"), it + 1)
                pe.wait_ge(S("hg_ready"), it + 2)
                for c in range(4):
                    pe.wait_ge(loaded[8 + c], 16 * it + 16)
                    for a in range(2):
                        j = 2 * c + a
                        for h, q in enumerate(halves):
                            ins = mm(psum[q, 3, :], aT[:, j % 4, j // 4, :],
                                     slot(8 + c)[:, 1024 * a + 512 * h:1024 * a + 512 * (h + 1)], start=(j == 0),
                                     stop=(j == KT - 1), skip_group_check=True)
                    ins.then_inc(slot_read if c < 3 else S("d_full"), 1)
            turn_gates(n_items + 1)
            scatter(n_items + 1)

            pe.wait_ge(S("x3_ready"), 1)
            for a in range(2):
                for k in range(KT):
                    ins = transposed(psum[:, 2 * a + k // 4, P * (k % 4):P * (k % 4 + 1)], xT[:, k, P * a:P * (a + 1)])
                ins.then_inc(S("fin_full"), 1)


_INS = ['x', 'c', 'ctx', 'c_ctx', 'ada_w', 'ada_b', 'norm_mix_g', 'norm_ffn_g', 'w_in', 'w_out', 'four_w', 's5_lam_re',
        's5_lam_im', 's5_log_dt', 's5_b_re', 's5_b_im', 's5_c_re', 's5_c_im', 's5_d', 's5_w_glu', 'gla_a2', 'gla_a_b',
        'gla_norm_g', 'ssd_conv_w', 'ssd_conv_b', 'ssd_a_log', 'ssd_dt_bias', 'ssd_d', 'ssd_norm_g', 'router_w',
        'router_b', 'exp_w_gu', 'exp_b_gu', 'exp_w_dn', 'exp_b_dn', 'final_g']


def kernel(**inputs):
    import numpy as _np
    import concourse.bacc as _bacc
    from concourse import mybir as _mybir
    from concourse.bass_utils import run_bass_kernel_spmd as _run

    nc = _bacc.Bacc("TRN2", target_bir_lowering=False, num_devices=1)
    arrays, handles = {}, {}
    for name in _INS:
        a = _np.ascontiguousarray(inputs[name])
        arrays[f"in_{name}_dram"] = a
        handles[name] = nc.dram_tensor(f"in_{name}_dram", a.shape, _mybir.dt.from_np(a.dtype),
                                       kind="ExternalInput").ap()
    arrays["const_dram"] = shape_constants()
    handles["const"] = nc.dram_tensor("const_dram", (P, NCONST), F32, kind="ExternalInput").ap()
    out = nc.dram_tensor("out_dram", (1, NLAT, D), F32, kind="ExternalOutput").ap()
    backbone(nc, handles, out)
    r = _run(nc, [arrays], core_ids=[0])
    return r.results[0]["out_dram"]
```

```python
from contextlib import ExitStack

import numpy as np

import concourse.bass as bass
from concourse import mybir

F32 = mybir.dt.float32
I32 = mybir.dt.int32
ALU = mybir.AluOpType
ACT = mybir.ActivationFunctionType
AX = mybir.AxisListType

P = 128
D = 1024
KT = D // P
NCTX = 256
NLAT = 256
NTOK = NCTX + NLAT
EPS = 1e-6
NMOD = 6
NE = 32
TOPK = 4
CAP = 64
NI = 50
LIMIT = 7.0
ALPHA = 1.702

CH = 16
NG = 16
Q = 8
NCH = NTOK // Q
LCH = NLAT // Q
SG = 8
CSZ = 64
NCK = NTOK // CSZ
GATE_TAU = 16.0
GLA_DK = 32

SLOT = 2048
NSLOT = 12
FR = 5
MIX = (NSLOT - FR) * SLOT

_C = {}


def _layout():
    at = 0
    for name, n in (("ident", 128), ("ones", 128), ("blk64", 128), ("cbd", 256), ("cseq", 512), ("sseq", 512),
                    ("tri", 2 * 128), ("neg", 2 * 128), ("scan", 512), ("iota", 2 * CAP),
                    ("rows", 8 * 128), ("incl", 128), ("headm", 4), ("halfm", 2), ("items", NI), ("evec", 1),
                    ("first", 1), ("strict", 32)):
        _C[name] = (at, n)
        at += n
    return at


NCONST = _layout()
ROW0 = 64


def shape_constants():
    c = np.zeros((P, NCONST), np.float32)

    def put(name, a):
        at, n = _C[name]
        a = np.asarray(a, np.float64).reshape(a.shape[0], -1)
        c[:a.shape[0], at:at + n] = a

    i = np.arange(P)
    put("ident", np.eye(P))
    put("ones", np.ones((P, P)))
    put("blk64", (i[:, None] // 64 == i[None, :] // 64) * 1.0)
    same = i[:, None] // 64 == i[None, :] // 64
    ang = 2 * np.pi * ((i[:, None] % 64) * (i[None, :] % 64) % 64) / 64
    put("cbd", np.concatenate([np.cos(ang) * same, np.sin(ang) * same], 1) / 128.0)
    t = np.arange(NLAT)
    angs = 2 * np.pi * (t[:, None] * t[None, :] % NLAT) / NLAT
    put("cseq", np.cos(angs).reshape(2, P, NLAT).transpose(1, 0, 2))
    put("sseq", -np.sin(angs).reshape(2, P, NLAT).transpose(1, 0, 2))
    fwd = same & (i[:, None] <= i[None, :])
    rev = same & (i[:, None] >= i[None, :])
    put("tri", np.stack([fwd, rev], 1) * 1.0)
    put("neg", (1.0 - np.stack([fwd, rev], 1)) * -1e30)
    put("scan", np.broadcast_to((np.arange(NTOK) % CSZ != 0) * 1.0, (P, NTOK)))
    put("iota", np.broadcast_to(np.arange(2 * CAP) % CAP + 1, (P, 2 * CAP)))
    rows = np.zeros((P, 8, P))
    for r in range(8):
        rows[ROW0 + 32 * (r // 4) + r % 4, r] = 1
    put("rows", rows)
    put("incl", (i[:, None] <= i[None, :]) * 1.0)
    put("headm", (i[:, None] // 32 == np.arange(4)[None]) * 1.0)
    put("halfm", (i[:, None] // 64 == np.arange(2)[None]) * 1.0)
    put("items", np.broadcast_to(np.arange(-1, NI - 1), (P, NI)))
    put("evec", i[:, None] * 1.0)
    put("first", (i[:, None] == 0) * 1.0)
    e = np.arange(NE)
    put("strict", (e[:, None] < e[None, :]) * 1.0)
    return c


R_C, R_CCTX, R_GMIX, R_GFFN, R_ADAB, R_S5D, R_SSDG, R_CONVB, R_CONVW, R_GLAB, R_GLAG, R_DTB, R_ALOG = (
    0, 8, 16, 24, 32, 80, 82, 84, 88, 108, 110, 111, 112)
NPAR = 113
NPAR_IN = 10 + 2 * 3 + 2
PAIR_D = 64
NPAR2 = PAIR_D + 2

W_FOUR, W_U, W_QK, W_V, W_R, W_MISC, W_Z, W_X, W_BC = range(9)
WIN_ORDER = (W_FOUR, W_U, W_X, W_BC, W_QK, W_V, W_R, W_MISC, W_Z)
STREAM = ([("ada", b) for b in range(8)] + [("win", b) for b in WIN_ORDER] + [("ada", b) for b in range(8, 24)]
          + [("wout", b) for b in range(4)])
AT = {s: n for n, s in enumerate(STREAM)}

BANKED = (
    [("par", "dve"), ("s5par", "dve")] + [(f"xraw{i}", "act") for i in range(4)]
    + [("ar0", "act"), ("ar1", "act"), ("at0", "dve"), ("at1", "dve")]
    + [(f"xn{k}", "dve") for k in range(KT)]
    + [("cpar0", "act"), ("cpar1", "act"), ("four", "act"), ("u0", "act"), ("u1", "act"), ("x0", "act"),
       ("x1", "act"), ("B", "act"), ("C", "act"), ("q", "act"), ("k", "act"), ("v0", "act"), ("v1", "act"),
       ("r", "act")] + [(f"VT{i}", "act") for i in range(8)] + [
        ("Kr0", "act"), ("Kr1", "act"), ("Kq0", "act"), ("Kq1", "act"), ("misc", "act"), ("z", "act")]
    + [("fA0", "act"), ("fA1", "act"), ("fB", "act"), ("fW", "act")]
    + [(f"D{i}", "act") for i in range(4)]
    + [("zg0", "act"), ("zg1", "act"), ("ar2", "act"), ("ar3", "act"), ("at2", "dve"), ("at3", "dve")]
    + [("Yt", "act"), ("Y", "act"), ("ar4", "act"), ("ar5", "act"), ("glu", "act"), ("at4", "dve"), ("at5", "dve")]
    + [("kd0", "dve"), ("kd1", "dve")] + [(f"att{i}", "dve") for i in range(4)]
    + [(f"ds{n}", "dve") for n in range(NCK - 1)] + [("og", "dve"), ("gss", "act")]
    + [(f"rT{i}", "dve") for i in range(3)] + [(f"xt{i}", "dve") for i in range(4)]
    + [("decl", "act")] + [(f"rb{i}", "dve") for i in range(4)] + [(f"bc{i}", "dve") for i in range(2)]
    + [(f"sds{n}", "dve") for n in range(NCK - 1)] + [("oy", "dve"), ("yss", "act")]
    + [(f"wo{i}", "dve") for i in range(4)] + [("ss2", "act")] + [(f"h2{i}", "act") for i in range(4)]
    + [("lg", "dve"), ("pos", "dve"), ("pgT", "dve"), ("cnt", "dve"), ("start", "dve"), ("it0", "dve"),
       ("ids", "dve")]
)


class BankRing:

    def __init__(self, psum, filled, emptied):
        self.psum, self.filled, self.emptied = psum, filled, emptied
        self.number, self.count = {}, {}
        seen = {"act": 0, "dve": 0}
        for n, (name, by) in enumerate(BANKED):
            seen[by] += 1
            self.number[name] = n
            self.count[name] = (by, seen[by])
        self.names = [name for name, _ in BANKED]
        self.done = {"pe": 0, "act": 0, "dve": 0}

    def bank(self, name):
        return self.psum[:, self.number[name] % 8, :]

    def wait_free(self, pe, name):
        n = self.number[name]
        assert n == self.done["pe"], name
        self.done["pe"] += 1
        if n >= 8:
            by, count = self.count[self.names[n - 8]]
            pe.wait_ge(self.emptied[by], count)

    def wait_filled(self, eng, name):
        eng.wait_ge(self.filled, self.number[name] + 1)

    def wait_emptied(self, eng, name):
        by, count = self.count[name]
        eng.wait_ge(self.emptied[by], count)

    def mark_filled(self, ins):
        ins.then_inc(self.filled, 1)

    def mark_emptied(self, ins, name, by):
        self.done[by] += 1
        assert self.count[name] == (by, self.done[by]), name
        ins.then_inc(self.emptied[by], 1)


def backbone(nc, t, out):
    ctx = ExitStack()
    with ctx:
        def sb(name, n, dt=F32):
            return ctx.enter_context(nc.sbuf_tensor(name, [P, n], dt))

        def sem(name):
            return ctx.enter_context(nc.semaphore(name))

        psum = ctx.enter_context(nc.psum_tensor("psum", [P, 8, 512], F32))
        arena = sb("arena", NSLOT * SLOT)

        def slot(n):
            return arena[:, n * SLOT:(n + 1) * SLOT]

        def mix(at, n, parts=P):
            assert at + n <= MIX
            return arena[0:parts, FR * SLOT + at:FR * SLOT + at + n]

        const = sb("const", NCONST)

        def con(name, parts=P):
            at, n = _C[name]
            return const[0:parts, at:at + n]

        ident = con("ident")
        xT = sb("xT", KT * NLAT)[:, :].rearrange("p (k t) -> p k t", k=KT)
        mixT = sb("mixT", KT * NLAT)[:, :].rearrange("p (k t) -> p k t", k=KT)
        prm = sb("prm", NPAR)
        s5p = sb("s5p", NPAR2)
        pairs = sb("pairs", 2)
        mod = sb("mod", 96)[:, :].rearrange("p (t c) -> p t c", c=2)
        tiny = sb("tiny", 160)
        hbuf = sb("hbuf", KT * NTOK)
        hT = hbuf[:, :].rearrange("p (k t) -> p k t", k=KT)
        proj = sb("proj", 6992)
        small = sb("small", 4016)
        neghalf = sb("neghalf", 1)
        ids = ctx.enter_context(nc.sbuf_tensor("ids", [1, NI + 1], I32))
        a2 = sb("a2", 256)

        at = [0]

        def part(n):
            at[0] += n
            return proj[:, at[0] - n:at[0]]

        fourT = part(512).rearrange("p (a t) -> p a t", a=2)
        uT = part(1024).rearrange("p (a t) -> p a t", a=2)
        qT = part(256)
        kTt = part(512)
        vTM = part(1024).rearrange("p (a t) -> p a t", a=4)
        rT = part(512).rearrange("p (a t) -> p a t", a=2)
        miscT = part(512)
        zT = part(512).rearrange("p (a t) -> p a t", a=2)
        PADW = NCTX + 4 + 4 * (CSZ + 4)
        xbc = part(4 * PADW).rearrange("p (a t) -> p a t", a=4)
        staging = proj[:, 0:4096].rearrange("p (a t) -> p a t", a=4)
        square = hbuf[:, 0:1024]

        at2 = [0]

        def spart(n):
            at2[0] += n
            return small[:, at2[0] - n:at2[0]]

        bre = spart(256).rearrange("p (g c) -> p g c", g=16)
        bim = spart(256).rearrange("p (g c) -> p g c", g=16)
        bbr = spart(256).rearrange("p (g c) -> p g c", g=16)
        bbi = spart(256).rearrange("p (g c) -> p g c", g=16)
        cT = spart(512).rearrange("p (r g c) -> p r g c", r=2, g=16)
        c0 = spart(1024).rearrange("p (h g r c) -> p h g r c", h=2, g=16, r=2)
        c0f = small[:, at2[0] - 1024:at2[0] + CH]
        pwr = spart(9 * 16).rearrange("p (j g) -> p j g", j=9)
        pwi = spart(9 * 16).rearrange("p (j g) -> p j g", j=9)
        pV = spart(256).rearrange("p (r g m) -> p r g m", r=2, g=16)
        pC = spart(256).rearrange("p (r g m) -> p r g m", r=2, g=16)
        cA = small[:, 0:512].rearrange("p (s o g t) -> p s o g t", s=SG, o=2, g=16)
        pAr = small[:, 512:656].rearrange("p (j g) -> p j g", j=9)
        pAi = small[:, 656:800].rearrange("p (j g) -> p j g", j=9)
        cG = small[:, 800:864].rearrange("p (o g t) -> p o g t", o=2, g=16)
        ptmp = small[:, 864:928]
        WG = small[:, 1536:2304].rearrange("p (m o g t) -> p m o g t", m=SG, o=2, g=16)
        SB = small[:, 2304:2560].rearrange("p (m r g) -> p m r g", m=SG, r=2)
        carried = small[:, 2560:3584].rearrange("p (c x) -> p c x", c=LCH)
        sc5 = spart(24 * 16).rearrange("p (j g) -> p j g", g=16)
        par1 = spart(128)
        par2 = spart(128)

        VT = mix(0, 4096).rearrange("p (g r n) -> p g r n", g=16, r=2)
        crow = mix(11264, 1024).rearrange("p (r b n) -> p r b n", r=2, b=4)
        V = mix(4096, 4096).rearrange("p (g r m) -> p g r m", g=16, r=2)
        vtmp = mix(8192, 2048)
        W = mix(4096, 6144).rearrange("p (c o g t) -> p c o g t", c=NCH, o=2, g=16)
        T5 = mix(4096, 4096).rearrange("p (g d m) -> p g d m", g=NG, d=2)
        SHm = mix(8192, 2048).rearrange("p (h c g r) -> p h c g r", h=2, c=LCH, g=16)
        U = mix(10240, 1024).rearrange("p (g c) -> p g c", g=NG)
        SH = mix(11264, 2048).rearrange("p (c r g) -> p c r g", c=NCH, r=2)
        kqsb = mix(13312, 512).rearrange("p (d g c) -> p d g c", d=2, g=NG)
        kr = mix(8192, 1024).rearrange("p (d x) -> p d x", d=2)
        zero5 = mix(13824, 112)
        YT = mix(13824, 512)
        ychunks = mix(11264, 512).rearrange("p (a i c) -> p a i c", a=2, i=Q)
        YS = mix(13312, 512).rearrange("p (g c) -> p g c", g=NG)
        Cc = hbuf[:, :].rearrange("p (g r m) -> p g r m", g=16, r=2)


        filled, ev_act, ev_dve = sem("bank_filled"), sem("bank_emptied_act"), sem("bank_emptied_dve")
        ring = BankRing(psum, filled, {"act": ev_act, "dve": ev_dve})
        bank = ring.bank
        loaded = [sem(f"slot{i}_loaded") for i in range(NSLOT)]
        slot_read = sem("slot_read")
        const_in, par_in, s5b_in, x_in, a2_in, fw_in, glu_in = (
            sem(n) for n in ("const_in", "par_in", "s5b_in", "x_in", "a2_in", "fw_in", "glu_in"))
        par_zeroed, cond_ready = sem("par_zeroed"), sem("cond_ready")
        dve_chain, act_chain, pool_chain = sem("dve_chain"), sem("act_chain"), sem("pool_chain")
        ssq_ready, rstd_ready, xn_ready = sem("ssq_ready"), sem("rstd_ready"), sem("xn_ready")
        cexp_ready = sem("cexp_ready")
        V_ready = sem("V_ready")
        kq_stored, T_in, scratch_zeroed = sem("kq_stored"), sem("T_in"), sem("scratch_zeroed")
        T_free = sem("T_free")
        s = {}

        def S(name):
            if name not in s:
                s[name] = sem(name)
            return s[name]

        scratch = nc.dram_tensor("s5_lags", (2, CH, NG, 15, CH), F32).ap()
        u_dram = nc.dram_tensor("s5_inputs", (NG, CH, Q, NCH), F32).ap()
        y_dram = nc.dram_tensor("s5_outputs", (NG, CH, Q, LCH), F32).ap()
        gz = mix(0, 1024).rearrange("p (d t) -> p d t", d=2)
        gln = mix(1024, 1024).rearrange("p (d t) -> p d t", d=2)
        gb = mix(2048, 1024).rearrange("p (d t) -> p d t", d=2)
        gluw = mix(3072, 512).rearrange("p (k n) -> p k n", k=2)
        gdec = mix(3584, 16).rearrange("p (d n) -> p d n", d=2)
        fourw = mix(9216, 512).rearrange("p (k n) -> p k n", k=2)
        fA = mix(8192, 1024).rearrange("p (a f n) -> p a f n", a=2, f=2)
        qm = mix(4096, 2048).rearrange("p (d h t) -> p d h t", d=2, h=4)
        qin = mix(6144, 512).rearrange("p (d t) -> p d t", d=2)
        kin = mix(6656, 512).rearrange("p (d t) -> p d t", d=2)
        kdM = mix(7168, 2048).rearrange("p (d a h n) -> p d a h n", d=2, a=4, h=2)
        att = mix(9216, 2048).rearrange("p (d a h t) -> p d a h t", d=2, a=2, h=4)
        SM = mix(11264, 2048).rearrange("p (d j n) -> p d j n", d=2, j=4)
        Srun = mix(13312, 512).rearrange("p (d n) -> p d n", d=2)
        go, gsq, grs, gsl = (mix(4096 + 512 * i, 512).rearrange("p (a t) -> p a t", a=2) for i in range(4))
        fin5 = [hbuf[:, 2048 + 512 * i:2560 + 512 * i].rearrange("p (a t) -> p a t", a=2) for i in range(4)]

        dtR, cumR, wR, tR = (small[:, 512 * i:512 * (i + 1)] for i in range(4))
        cv = sb("conv", 4 * PADW)[:, :].rearrange("p (a t) -> p a t", a=4)
        ce = xbc
        XC = hbuf[:, 0:2048].rearrange("p (a t) -> p a t", a=4)
        cols = mix(6304, 96).rearrange("p (w a d h) -> p w a d h", w=3, a=4, d=2)
        xdt = mix(6400, 1024).rearrange("p (a d n) -> p a d n", a=2, d=2)
        xdec = mix(7424, 2048).rearrange("p (a d n) -> p a d n", a=4, d=2)
        BTM = mix(9472, 1024).rearrange("p (a h n) -> p a h n", a=4, h=2)
        ECR = mix(10496, 2048).rearrange("p (r t) -> p r t", r=8)
        SEG = mix(2048, 2048).rearrange("p (r a t) -> p r a t", r=8, a=2)
        SE = mix(4096, 2048).rearrange("p (d j n) -> p d j n", d=2, j=4)
        SSrun = mix(12544, 512).rearrange("p (d n) -> p d n", d=2)
        Cg = mix(13056, 512).rearrange("p (g t) -> p g t", g=2)
        DEC = mix(13568, 64).rearrange("p (r n) -> p r n", r=8)
        anegc = small[:, 2048:2049]

        ext = sb("ext", 1900)
        cond = ext[:, 0:256].rearrange("p (k x) -> p k x", k=KT)
        ada_sb = [hbuf[:, 1024 + 512 * i:1536 + 512 * i] for i in range(2)] + [
            mixT[:, 4 + 2 * (i % 2):6 + 2 * (i % 2), :].rearrange("p a t -> p (a t)") for i in range(4)]

        h2T = proj[:, 0:2048].rearrange("p (k t) -> p k t", k=KT)
        h2TM = proj[:, 2048:4096].rearrange("p (a n) -> p a n", a=2)
        xsq = proj[:, 4096:6144].rearrange("p (k t) -> p k t", k=KT)
        bgu = hbuf[:, 0:2048]
        bdn = hbuf[0:NE, 2048:3072]
        gfin = hbuf[:, 3072:4096]
        rw = small[:, 0:256].rearrange("p (k e) -> p k e", k=KT)
        eg, eu, es, hg, aT, ey = (small[:, 256 + 512 * i:768 + 512 * i] for i in range(6))
        hg = hg.rearrange("p (k c) -> p k c", k=KT)
        aT = aT.rearrange("p (i h c) -> p i h c", h=2, c=CAP)
        GT = small[:, 3328:3584]
        facc = psum[:, 4:8, :].rearrange("p b (o t) -> p (b o) t", o=2)
        at3 = [0]

        def epart(n):
            at3[0] += n
            assert at3[0] <= 1900
            return ext[:, at3[0] - n:at3[0]]

        Ssel = epart(2 * CAP).rearrange("p (a c) -> p a c", a=2)
        Sgat = epart(4 * CAP).rearrange("p (a c) -> p a c", a=2)
        posI = epart(2 * NI).rearrange("p (a i) -> p a i", a=2)
        gatI = epart(2 * NI).rearrange("p (a i) -> p a i", a=2)
        lg = epart(64).rearrange("p (a e) -> p a e", a=2)
        gt = epart(64).rearrange("p (a e) -> p a e", a=2)
        eq = epart(64).rearrange("p (a e) -> p a e", a=2)
        rank = epart(64).rearrange("p (a e) -> p a e", a=2)
        sel = epart(64).rearrange("p (a e) -> p a e", a=2)
        gate = epart(64).rearrange("p (a e) -> p a e", a=2)
        posm = epart(64).rearrange("p (a e) -> p a e", a=2)
        top = epart(16).rearrange("p (a e) -> p a e", a=2)
        need = epart(8).rearrange("p (a e) -> p a e", a=2)
        nmax = epart(2)
        zsum = epart(2)
        rbias = epart(32)
        posT = epart(256)
        gatT = epart(256)
        Em, Eb, Et = epart(NI), epart(NI), epart(NI)
        Ecol = epart(CAP)
        nb = epart(4)
        idf = epart(NI + 1)
        eps_col = epart(1)

        win = t["w_in"][0].rearrange("(k p) c -> p k c", p=P)
        ada = t["ada_w"][0].rearrange("(k p) c -> p k c", p=P)
        wout = t["w_out"][0].rearrange("(k p) c -> p k c", p=P)
        wgu = t["exp_w_gu"][0]
        wdn = t["exp_w_dn"][0]
        WCOL = {W_FOUR: 0, W_U: 256, W_QK: 512, W_V: 768, W_R: 1024, W_Z: 1312, W_X: 1568, W_BC: 1824}
        A1_COL, DT_COL = 1280, 2080
        uses = [len([n for n in range(len(STREAM)) if n % FR == i]) if i < FR else 0 for i in range(NSLOT)]
        NSTREAM = len(STREAM)

        def sview(n):
            return slot(n % FR).rearrange("p (k c) -> p k c", k=KT)

        block = ctx.enter_context(nc.Block())

        @block.sync
        def _(sp):
            for i in range(2):
                sp.dma_start(staging[:, i, :], t["ctx"][0, P * i:P * (i + 1), :]).then_inc(x_in, 16)
                sp.dma_start(staging[:, 2 + i, :], t["x"][0, P * i:P * (i + 1), :]).then_inc(x_in, 16)
            sp.wait_ge(par_in, 16 * NPAR_IN)
            sp.wait_ge(S("pairs_in"), 32)
            for n, (kind, b) in enumerate(STREAM):
                if n >= FR:
                    sp.wait_ge(slot_read, n - FR + 1)
                dst = sview(n)
                done = loaded[n % FR]
                if kind == "win" and b == W_MISC:
                    sp.wait_ge(S("misc_zeroed"), 1)
                    sp.dma_start(dst[:, :, 0:32], win[:, :, A1_COL:A1_COL + 32]).then_inc(S("misc_in"), 16)
                    sp.dma_start(dst[:, :, 64:68], win[:, :, DT_COL:DT_COL + 4]).then_inc(S("misc_in"), 16)
                    sp.dma_start(dst[:, :, 96:100], win[:, :, DT_COL + 4:DT_COL + 8]).then_inc(done, 16)
                else:
                    src = {"ada": ada, "win": win, "wout": wout}[kind]
                    c0 = WCOL[b] if kind == "win" else 256 * b
                    sp.dma_start(dst, src[:, :, c0:c0 + 256]).then_inc(done, 16)

            def chunk(e, c):
                if c < 8:
                    src = wgu[e, P * c:P * (c + 1), :]
                    return slot(c), src.rearrange("a p c -> p (a c)") if len(src.shape) == 3 else src
                j = c - 8
                src = wdn[e, 2 * P * j:2 * P * (j + 1), :]
                if len(src.shape) == 3:
                    src = src.rearrange("e k c -> (e k) c")
                return slot(c).rearrange("p (a n) -> p a n", a=2), src.rearrange("(a p) n -> p a n", p=P)

            for c in range(NSLOT):
                if c < FR:
                    sp.wait_ge(slot_read, max(n for n in range(NSTREAM) if n % FR == c) + 1)
                elif c == FR:
                    sp.wait_ge(S("mixers_done"), 1)
                dst, src = chunk(0, c)
                sp.dma_start(dst, src).then_inc(loaded[c], 16)
            sp.wait_ge(S("ids_ready"), 1)
            n_items = sp.value_load(ids[0:1, NI:NI + 1], min_val=2, max_val=NI - 2)
            with sp.Fori(1, n_items) as it:
                e = sp.value_load(ids[0:1, bass.ds(it + 1, 1)], min_val=0, max_val=NE - 1)
                for c in range(NSLOT):
                    if c == KT - 1:
                        sp.wait_ge(S("gu_full"), it)
                    elif c == NSLOT - 1:
                        sp.wait_ge(S("d_full"), it)
                    else:
                        sp.wait_ge(slot_read, (NSLOT - 2) * (it - 1) + (NSTREAM + c + 1 - c // KT))
                    dst, src = chunk(bass.ds(e, 1), c)
                    sp.dma_start(dst, src).then_inc(loaded[c], 16)
            for a in range(2):
                sp.wait_ge(S("out_ready"), a + 1)
                sp.dma_start(out[0, P * a:P * (a + 1), :], h2TM[:, a, :]).then_inc(S("out_stored"), 16)
            sp.wait_ge(S("out_stored"), 32)

        @block.gpsimd
        def _(pool):
            chain = [0]

            def link(ins):
                chain[0] += 1
                ins.then_inc(pool_chain, 1)
                pool.wait_ge(pool_chain, chain[0])

            pool.memset(proj[:, 4864:6992], 0.0).then_inc(S("xbc_zeroed"), 1)
            pool.memset(eps_col, EPS).then_inc(S("eps_ready"), 1)
            link(pool.memset(neghalf[:, :], -0.5))
            link(pool.memset(zero5[0:CH, :], 0.0))
            for d in range(2):
                x0 = 0 if d == 0 else Q
                pool.dma_start(scratch[d, :, :, x0:x0 + 7, :].rearrange("c g x k -> c g (x k)"),
                               zero5[0:CH, :].unsqueeze(1).to_broadcast([CH, NG, 7 * CH])
                               ).then_inc(scratch_zeroed, 16)

            def power(dst, src, scale, n):
                link(pool.tensor_scalar(dst, src, scale, EPS, ALU.mult, ALU.add))
                return pool.tensor_tensor(dst, dst, neghalf[:, 0:1].to_broadcast([P, n]), ALU.pow)

            pool.wait_ge(ssq_ready, 4)
            power(tiny[:, 4:8], tiny[:, 0:4], 1.0 / D, 4).then_inc(rstd_ready, 1)

            n = AT[("win", W_MISC)]
            pool.wait_ge(slot_read, n - FR + 1)
            pool.memset(sview(n)[:, :, 0:P], 0.0).then_inc(S("misc_zeroed"), 1)

            pool.wait_ge(S("u_stored"), 16)
            for j in range(Q):
                pool.dma_start(U[CH * j:CH * (j + 1), :, :], u_dram[:, :, j, :].rearrange("g h c -> h g c")
                               ).then_inc(S("U_in"), 16)
            ring.wait_emptied(pool, "Kq1")
            for d in range(2):
                for m in range(Q):
                    x = 14 - m if d == 0 else 7 - m
                    pool.dma_start(scratch[d, :, :, x, :], kqsb[CH * m:CH * (m + 1), d, :, :]).then_inc(kq_stored, 16)
            pool.wait_ge(kq_stored, 16 * 2 * Q)
            pool.wait_ge(scratch_zeroed, 32)
            pool.wait_ge(T_free, 1)
            for j in range(Q):
                pool.dma_start(T5[CH * j:CH * (j + 1), :, 0, :],
                               scratch[0, :, :, 7 - j:15 - j, :].rearrange("c g x k -> c g (x k)")).then_inc(T_in, 16)

            pool.wait_ge(S("last_ssq"), 2)
            power(tiny[:, 52:54], tiny[:, 50:52], 1.0 / D, 2).then_inc(S("last_root"), 1)

        @block.scalar
        def _(act):
            chain = [0]
            counts = {}

            def link(ins, done=None):
                if done is None:
                    chain[0] += 1
                    ins.then_inc(act_chain, 1)
                    act.wait_ge(act_chain, chain[0])
                    return
                counts[done] = counts.get(done, 0) + 1
                ins.then_inc(S(done), 1)
                act.wait_ge(S(done), counts[done])

            def copy_out(name, dst, src):
                ring.wait_filled(act, name)
                ring.mark_emptied(nc.scalar.copy(dst, src), name, "act")

            def root(name, dst, scale):
                act.wait_ge(S("eps_ready"), 1)
                ring.wait_filled(act, name)
                ring.mark_emptied(nc.scalar.activation(dst, bank(name)[:, 0:dst.shape[1]], ACT.Sqrt, scale=scale,
                                                       bias=eps_col[:, 0:1]), name, "act")

            act.dma_start(ident, t["const"][:, 0:P]).then_inc(S("ident_in"), 16)
            act.wait_ge(par_zeroed, 1)

            def rows(at, n, src):
                act.dma_start(par1[at:at + n, :], src).then_inc(par_in, 16)

            rows(R_C, 8, t["c"][0].rearrange("(k p) -> k p", p=P))
            rows(R_CCTX, 8, t["c_ctx"].rearrange("(k p) -> k p", p=P))
            rows(R_GMIX, 8, t["norm_mix_g"][0].rearrange("(k p) -> k p", p=P))
            rows(R_GFFN, 8, t["norm_ffn_g"][0].rearrange("(k p) -> k p", p=P))
            rows(R_ADAB, 48, t["ada_b"][0].rearrange("(k p) -> k p", p=P))
            rows(R_S5D, 2, t["s5_d"][0].rearrange("(k p) -> k p", p=P))
            rows(R_SSDG, 2, t["ssd_norm_g"][0].rearrange("(k p) -> k p", p=P))
            rows(R_CONVB, 4, t["ssd_conv_b"][0].rearrange("(k p) -> k p", p=P))
            rows(R_CONVW, 20, t["ssd_conv_w"][0].rearrange("j (k p) -> (j k) p", p=P))
            rows(R_GLAB, 2, t["gla_a_b"][0])
            for i in range(2):
                act.dma_start(par1[R_GLAG:R_GLAG + 1, 64 * i:64 * (i + 1)], t["gla_norm_g"]).then_inc(par_in, 16)
                at_ = ROW0 + 32 * i
                act.dma_start(par1[R_DTB:R_DTB + 1, at_:at_ + 4], t["ssd_dt_bias"][0, i:i + 1, :]).then_inc(par_in, 16)
                act.dma_start(par1[R_ALOG:R_ALOG + 1, at_:at_ + 4], t["ssd_a_log"][0, i:i + 1, :]).then_inc(par_in, 16)
            for i, name in enumerate(("s5_lam_re", "s5_lam_im")):
                act.dma_start(par2[16 * i:16 * i + 16, :],
                              t[name][0].rearrange("d (g h) n -> (d g) (h n)", h=2)).then_inc(par_in, 16)
            act.dma_start(pairs[32:48, :], t["s5_log_dt"][0].rearrange("d (g h) -> (d g) h", h=2)
                          ).then_inc(S("pairs_in"), 16)
            act.dma_start(pairs[PAIR_D:PAIR_D + 2, :], t["ssd_d"][0].rearrange("(a h) -> a h", h=2)
                          ).then_inc(S("pairs_in"), 16)
            act.dma_start(const[:, P:], t["const"][:, P:]).then_inc(const_in, 16)
            for name, dst in (("s5_b_re", bre), ("s5_b_im", bim)):
                for d in range(2):
                    act.dma_start(dst[:, 8 * d:8 * d + 8, :],
                                  t[name][0, d].rearrange("(g h) n c -> (h n) g c", h=2)).then_inc(s5b_in, 16)
            for r, name in enumerate(("s5_c_re", "s5_c_im")):
                for h in range(2):
                    act.dma_start(crow[:, r, :, 64 * h:64 * h + 64],
                                  t[name][0].rearrange("d (b g) c n -> (g c) (d b) n", b=2)).then_inc(S("s5c_in"), 16)
            for d in range(2):
                act.dma_start(a2[16 * d:16 * d + 16, 128 * d:128 * d + 128], t["gla_a2"][0, d]).then_inc(a2_in, 16)

            act.wait_ge(S("pairs_in"), 32)
            for h in range(2):
                for q in (slice(32, 48), slice(PAIR_D, PAIR_D + 2)):
                    nc.scalar.copy(par2[q, 64 * h:64 * h + 64], pairs[q, h:h + 1].to_broadcast(
                        [q.stop - q.start, 64])).then_inc(S("pairs_spread"), 1)
            ring.wait_emptied(act, "par")
            nc.scalar.activation(tiny[:, 16:32], prm[:, 0:16], ACT.Sigmoid).then_inc(cexp_ready, 1)
            act.wait_ge(x_in, 64)
            for i in range(4):
                nc.scalar.activation(square, staging[:, i, :], ACT.Square,
                                     accum_out=tiny[:, i:i + 1]).then_inc(ssq_ready, 1)
                act.wait_ge(ssq_ready, i + 1)
            for i in range(4):
                copy_out(f"xraw{i}", xT[:, 2 * i:2 * i + 2, :].rearrange("p k t -> p (k t)"), bank(f"xraw{i}"))
            for i in range(2):
                copy_out(f"ar{i}", ada_sb[i], bank(f"ar{i}"))
            for r in range(2):
                ring.wait_filled(act, f"cpar{r}")
                for h in range(2):
                    q = slice(64 * h, 64 * h + 64)
                    ins = nc.scalar.copy(cT[q, r], bank(f"cpar{r}")[q, :].rearrange("p (g h c) -> p g h c", h=2,
                                                                                    c=CH)[:, :, h, :])
                ring.mark_emptied(ins, f"cpar{r}", "act")
            copy_out("four", fourT.rearrange("p a t -> p (a t)"), bank("four"))
            for i in range(2):
                copy_out(f"u{i}", uT[:, i, :].rearrange("p (j c) -> p c j", j=Q),
                         bank(f"u{i}").rearrange("p (c j) -> p c j", j=Q))
            ring.wait_emptied(act, "u1")
            act.dma_start(u_dram.rearrange("(a g) h j c -> (g h) a (j c)", a=2), uT).then_inc(S("u_stored"), 16)
            act.wait_ge(S("xbc_zeroed"), 1)

            def lat_rows(tile):
                return tile[:, NCTX + 4:].rearrange("p (r w) -> p r w", w=CSZ + 4)[:, :, 2:2 + CSZ]

            for i, name in enumerate(("x0", "x1", "B", "C")):
                ring.wait_filled(act, name)
                if name != "C":
                    nc.scalar.copy(xbc[:, i, 2:2 + NCTX], bank(name)[:, 0:NCTX])
                lat = bank(name)[:, NCTX:] if name != "C" else bank(name)[:, 0:NLAT]
                ring.mark_emptied(nc.scalar.copy(lat_rows(xbc[:, i, :]), lat.rearrange("p (r w) -> p r w", w=CSZ)),
                                  name, "act")

            ring.wait_filled(act, "q")
            ring.mark_emptied(nc.scalar.mul(qT, bank("q")[:, 0:256], float(GLA_DK) ** -0.5), "q", "act")
            copy_out("k", kTt, bank("k"))
            copy_out("v0", vTM[:, 0:2, :].rearrange("p a t -> p (a t)"), bank("v0"))
            copy_out("v1", vTM[:, 2:4, :].rearrange("p a t -> p (a t)"), bank("v1"))
            copy_out("r", rT.rearrange("p a t -> p (a t)"), bank("r"))
            VTf = VT.rearrange("p g r n -> p (g r n)")
            for i in range(8):
                copy_out(f"VT{i}", VTf[:, 512 * i:512 * (i + 1)], bank(f"VT{i}"))
            for d in range(2):
                copy_out(f"Kr{d}", kr[:, d, :], bank(f"Kr{d}"))
            for d in range(2):
                copy_out(f"Kq{d}", kqsb[:, d], bank(f"Kq{d}").rearrange("p (g x) -> p g x", x=2 * CH)[:, :, 0:CH])
            act.wait_ge(V_ready, 1)
            act.dma_start(fourw, t["four_w"][0].rearrange("(k p) n -> p k n", p=P)).then_inc(fw_in, 16)

            act.wait_ge(S("conv_ready"), 1)
            link(nc.scalar.activation(ce, cv, ACT.Sigmoid), "conv_exp")
            copy_out("misc", miscT, bank("misc"))
            copy_out("z", zT.rearrange("p a t -> p (a t)"), bank("z"))
            for i in range(2):
                copy_out(f"fA{i}", fA[:, i].rearrange("p f n -> p (f n)"), bank(f"fA{i}"))
            copy_out("fB", fourT.rearrange("p a t -> p (a t)"), bank("fB"))
            copy_out("fW", mixT[:, 0:2, :].rearrange("p a t -> p (a t)"), bank("fW"))

            for i in range(4):
                ring.wait_filled(act, f"D{i}")
                b4 = bank(f"D{i}").rearrange("p (o g c) -> p o g c", o=2, g=4)
                w4 = W[:, :, :, 4 * i:4 * i + 4, 2].rearrange("p c o g -> p o g c")
                if i < 2:
                    ring.mark_emptied(nc.scalar.copy(w4, b4), f"D{i}", "act")
                else:
                    nc.scalar.copy(w4[:, :, :, 31::-1], b4[:, :, :, 0:32])
                    ring.mark_emptied(nc.scalar.copy(w4[:, :, :, 63:31:-1], b4[:, :, :, 32:64]), f"D{i}", "act")
            act.dma_start(gluw, t["s5_w_glu"][0].rearrange("(k p) n -> p k n", p=P)).then_inc(glu_in, 16)
            for d in range(2):
                ring.wait_filled(act, f"zg{d}")
                ring.mark_emptied(nc.scalar.activation(gz[:, d, :], bank(f"zg{d}"), ACT.Identity,
                                                       bias=prm[:, R_GLAB + d:R_GLAB + d + 1]), f"zg{d}", "act")
            for i in (2, 3):
                copy_out(f"ar{i}", ada_sb[i], bank(f"ar{i}"))
            act.wait_ge(kq_stored, 16 * 2 * Q)
            act.wait_ge(scratch_zeroed, 32)
            act.wait_ge(T_free, 1)
            for j in range(Q):
                act.dma_start(T5[CH * j:CH * (j + 1), :, 1, :],
                              scratch[1, :, :, 7 - j:15 - j, :].rearrange("c g x k -> c g (x k)")).then_inc(S("T1_in"), 16)
            act.wait_ge(S("gabs"), 1)
            link(nc.scalar.activation(gln, gln, ACT.Exp, scale=-1.0))
            link(nc.scalar.activation(gln, gln, ACT.Ln, bias=1.0), "glog")
            act.wait_ge(S("dt_abs"), 1)
            link(nc.scalar.activation(tR[ROW0:, :], tR[ROW0:, :], ACT.Exp, scale=-1.0))
            nc.scalar.activation(anegc[ROW0:, :], prm[ROW0:, R_ALOG:R_ALOG + 1], ACT.Exp)
            link(nc.scalar.activation(tR[ROW0:, :], tR[ROW0:, :], ACT.Ln, bias=1.0), "dt_log")
            act.wait_ge(S("cum_ready"), 1)
            link(nc.scalar.activation(wR[ROW0:, :], wR[ROW0:, :], ACT.Exp), "w_exp")
            copy_out("Yt", YT, bank("Yt"))
            copy_out("Y", YS.rearrange("p g c -> p (g c)"), bank("Y"))
            ring.wait_emptied(act, "Y")
            for i in range(Q):
                act.dma_start(y_dram[:, :, i, :].rearrange("g h c -> h g c"), YS[CH * i:CH * (i + 1), :, :]
                              ).then_inc(S("y_stored"), 16)
            act.wait_ge(S("gscan"), 1)
            nc.scalar.activation(qin, gb[:, :, NCTX:], ACT.Exp)
            nc.scalar.activation(kin, gb[:, :, NCTX:], ACT.Exp, scale=-1.0)
            nc.scalar.activation(gln, gln, ACT.Exp)
            for d in range(2):
                last = CSZ - 1 if d == 0 else 0
                ins = nc.scalar.activation(gdec[:, d, :], gb[:, d, last::CSZ], ACT.Exp)
            link(ins, "gexp")
            act.wait_ge(S("y_stored"), 16 * Q)
            act.dma_start(ychunks.rearrange("p a i c -> p a (i c)"),
                          y_dram.rearrange("(a g) h i c -> (g h) a (i c)", a=2)).then_inc(S("y_in"), 16)
            act.wait_ge(S("gelu_in"), 1)
            link(nc.scalar.activation(fin5[1], fin5[1], ACT.Sigmoid, scale=2.0 * float(np.sqrt(2 / np.pi))), "gelu_exp")
            for i in (4, 5):
                copy_out(f"ar{i}", ada_sb[i], bank(f"ar{i}"))
            ring.wait_filled(act, "glu")
            ring.mark_emptied(nc.scalar.activation(fin5[2], bank("glu").rearrange("p (a t) -> p a t", a=2),
                                                   ACT.Sigmoid), "glu", "act")
            act.wait_ge(S("go_ready"), 1)
            link(nc.scalar.activation(gsq, go, ACT.Square), "gsq_ready")
            link(nc.scalar.activation(gsl, rT, ACT.Sigmoid), "gsl_ready")
            root("gss", grs.rearrange("p a t -> p (a t)"), 1.0 / 64)

            ring.wait_filled(act, "decl")
            ring.mark_emptied(nc.scalar.activation(DEC.rearrange("p r n -> p (r n)"), bank("decl")[:, 0:64], ACT.Exp),
                              "decl", "act")
            for i in range(4):
                ring.wait_filled(act, f"rb{i}")
                nc.scalar.activation(ECR[:, 2 * i:2 * i + 2, :].rearrange("p r t -> p (r t)"), bank(f"rb{i}"),
                                     ACT.Exp).then_inc(S("ecr_ready"), 1)
            act.wait_ge(S("seg_ready"), 1)
            link(nc.scalar.activation(SEG, SEG, ACT.Exp), "seg_exp")
            link(nc.scalar.activation(fin5[3], zT, ACT.Sigmoid), "sz_exp")
            act.wait_ge(S("yz_ready"), 1)
            link(nc.scalar.activation(fin5[1], fin5[0], ACT.Square), "ysq_ready")
            root("yss", fin5[2][:, 0, :], 1.0 / 256)

            act.wait_ge(S("mixers_done"), 1)
            act.wait_ge(S("bgu_zeroed"), 1)
            act.dma_start(bgu[0:NE, :], t["exp_b_gu"][0]).then_inc(S("bias_in"), 16)
            act.dma_start(bdn, t["exp_b_dn"][0]).then_inc(S("bias_in"), 16)
            act.dma_start(gfin, t["final_g"].unsqueeze(0).to_broadcast([P, D])).then_inc(S("gfin_in"), 16)
            act.dma_start(rw, t["router_w"][0].rearrange("(k p) e -> p k e", p=P)).then_inc(S("router_in"), 16)
            act.dma_start(rbias, t["router_b"].to_broadcast([P, NE])).then_inc(S("router_in"), 16)
            for i in range(4):
                act.wait_ge(S("x2_ready"), 2 * (i + 1))
                nc.scalar.activation(xsq[:, 2 * i:2 * i + 2, :], xT[:, 2 * i:2 * i + 2, :],
                                     ACT.Square).then_inc(S("xsq_ready"), 1)
            root("ss2", mixT[:, 0, :], 1.0 / D)
            for i in range(4):
                copy_out(f"h2{i}", h2TM[:, :, 256 * i:256 * (i + 1)], bank(f"h2{i}").rearrange("p (a n) -> p a n", a=2))
            act.wait_ge(S("lmax_ready"), 1)
            for a in range(2):
                ins = nc.scalar.activation(gate[:, a, :], lg[:, a, :], ACT.Exp, bias=nmax[:, a:a + 1])
            link(ins, "gate_exp")

            def gathered(n):
                act.wait_ge(S("g_full"), n)
                nc.scalar.copy(hg.rearrange("p k c -> p (k c)"), psum[:, 3, :]).then_inc(S("hg_ready"), 1)

            gathered(1)
            act.wait_ge(S("ids_ready"), 1)
            n_items = act.value_load(ids[0:1, NI:NI + 1], min_val=2, max_val=NI - 2)
            with act.Fori(0, n_items) as it:
                act.wait_ge(S("gclip_ready"), it + 1)
                nc.scalar.activation(es, eg, ACT.Sigmoid, scale=ALPHA).then_inc(S("sig_ready"), 1)
                gathered(it + 2)
                act.wait_ge(S("at_full"), it + 1)
                nc.scalar.copy(aT.rearrange("p i h c -> p (i h c)"), psum[:, 2, :]).then_inc(S("aT_ready"), 1)
                act.wait_ge(S("d_full"), it + 1)
                act.wait_ge(S("sc_full"), it + 2)
                nc.scalar.copy(ey, psum[:, 3, :]).then_inc(S("y_ready"), 1)
            for a in range(2):
                act.wait_ge(S("fin_full"), a + 1)
                nc.scalar.activation(h2TM[:, a, :].rearrange("p (b n) -> p b n", b=2), psum[:, 2 * a:2 * a + 2, :],
                                     ACT.Square, accum_out=tiny[:, 50 + a:51 + a]).then_inc(S("last_ssq"), 1)

        @block.vector
        def _(dve):
            v = nc.vector
            chain = [0]
            counts = {}

            def link(ins, done=None):
                if done is None:
                    chain[0] += 1
                    ins.then_inc(dve_chain, 1)
                    dve.wait_ge(dve_chain, chain[0])
                    return
                counts[done] = counts.get(done, 0) + 1
                ins.then_inc(S(done), 1)
                dve.wait_ge(S(done), counts[done])

            def emptied(ins, name):
                ring.mark_emptied(ins, name, "dve")
                ring.wait_emptied(dve, name)

            def add(o, a, b):
                return v.tensor_tensor(o, a, b, ALU.add)

            def sub(o, a, b):
                return v.tensor_tensor(o, a, b, ALU.subtract)

            def mul(o, a, b):
                return v.tensor_tensor(o, a, b, ALU.mult)

            v.memset(par2[:, :], 0.0)
            v.memset(a2[:, :], 0.0)
            link(v.memset(par1[:, :], 0.0))
            dve.sem_inc(par_zeroed, 1)

            ring.wait_filled(dve, "par")
            emptied(v.tensor_copy(prm[:, :], bank("par")[:, 0:NPAR]), "par")
            ring.wait_filled(dve, "s5par")
            emptied(v.tensor_copy(s5p[:, :], bank("s5par")[:, 0:NPAR2]), "s5par")
            ce_ = tiny[:, 16:32]
            dve.wait_ge(cexp_ready, 1)
            link(v.memset(cond, 0.0))
            link(mul(cond[:, :, 0:2].rearrange("p k c -> p c k"), prm[:, 0:16].rearrange("p (c k) -> p c k", c=2),
                     ce_.rearrange("p (c k) -> p c k", c=2)), "cond_silu")

            dve.wait_ge(rstd_ready, 1)
            ring.wait_filled(dve, "xraw3")
            for i in range(4):
                ins = v.tensor_scalar(staging[:, i, :], staging[:, i, :], tiny[:, 8 - 4 + i:8 - 4 + i + 1], None,
                                      ALU.mult)
            ins.then_inc(xn_ready, 1)

            def mod_out(first, last):
                for n in range(first, last):
                    ring.wait_filled(dve, f"at{n}")
                    x = bank(f"at{n}").rearrange("p (t h x) -> p t h x", h=2, x=32)
                    m = mod[:, 8 * n:8 * (n + 1), :]
                    link(v.tensor_copy(m, x[:, :, 0, 0:2]))
                    emptied(add(m, x[:, :, 1, 0:2], m), f"at{n}")
                    link(add(m, m, prm[:, R_ADAB + 8 * n:R_ADAB + 8 * (n + 1)].unsqueeze(2).to_broadcast([P, 8, 2])))

            def gain(dst, scale, g0):
                n = scale.shape[-1]
                link(v.scalar_tensor_tensor(dst, scale, 1.0, prm[:, g0:g0 + KT].unsqueeze(2).to_broadcast([P, KT, n]),
                                            ALU.add, ALU.mult))

            mod_out(0, 2)
            gA = tiny[:, 32:48].rearrange("p (k c) -> p k c", c=2)
            gain(gA, mod[:, 8:16, :], R_GMIX)
            for k in range(KT):
                ring.wait_filled(dve, f"xn{k}")
                for c, (a, b) in ((1, (0, NCTX)), (0, (NCTX, NTOK))):
                    ins = v.tensor_scalar(hT[:, k, a:b], bank(f"xn{k}")[:, a:b], gA[:, k, c:c + 1], mod[:, k, c:c + 1],
                                          ALU.mult, ALU.add)
                ring.mark_emptied(ins, f"xn{k}", "dve")

            LN2_HI, LN2_LO = 0.693145751953125, 1.42860682030941723212e-6
            PI2_A, PI2_B, PI2_C = 6.28125, 1.93500518798828125e-3, 3.0199159819567014e-7
            MAGIC = 1.5 * 2.0 ** 23
            (dt_, zr, zi, t0, t1, t2, ex, sn, cs, ar, ai, am, den, wr_, wi_, t3) = (sc5[:, j, :] for j in range(16))
            lre, lim_, ldt = s5p[:, 0:16], s5p[:, 16:32], s5p[:, 32:48]

            def nearest(o, a, scale):
                link(v.tensor_scalar(o, a, scale, MAGIC, ALU.mult, ALU.add))
                link(v.tensor_scalar(o, o, -MAGIC, None, ALU.add))

            def exponential(o, a):
                link(v.tensor_scalar(t0, a, -87.0, 88.0, ALU.max, ALU.min))
                nearest(t1, t0, 1.0 / float(np.log(2.0)))
                link(v.scalar_tensor_tensor(t0, t1, -LN2_HI, t0, ALU.mult, ALU.add))
                link(v.scalar_tensor_tensor(t0, t1, -LN2_LO, t0, ALU.mult, ALU.add))
                link(v.tensor_scalar(t2, t0, 1.0 / 5040, None, ALU.mult))
                for c in (720, 120, 24, 6, 2, 1):
                    link(v.scalar_tensor_tensor(t2, t2, 1.0 / c, t0, ALU.add, ALU.mult))
                link(v.tensor_scalar(t1.bitcast(I32), t1, 127.0, 2.0 ** 23, ALU.add, ALU.mult))
                link(v.scalar_tensor_tensor(o, t2, 1.0, t1, ALU.add, ALU.mult))

            exponential(dt_, ldt)
            link(mul(zr, lre, dt_))
            link(mul(zi, lim_, dt_))
            exponential(ex, zr)
            nearest(t1, zi, 1.0 / (2 * float(np.pi)))
            for c in (PI2_A, PI2_B, PI2_C):
                link(v.scalar_tensor_tensor(zi, t1, -c, zi, ALU.mult, ALU.add))
            link(v.tensor_scalar(t0, zi, 0.25, None, ALU.mult))
            link(mul(t1, t0, t0))
            link(v.tensor_scalar(sn, t1, 1.0 / 362880, None, ALU.mult))
            for c in (-5040.0, 120.0, -6.0):
                link(v.scalar_tensor_tensor(sn, sn, 1.0 / c, t1, ALU.add, ALU.mult))
            link(v.scalar_tensor_tensor(sn, sn, 1.0, t0, ALU.add, ALU.mult))
            link(v.tensor_scalar(cs, t1, -1.0 / 3628800, None, ALU.mult))
            for c in (40320.0, -720.0, 24.0, -2.0):
                link(v.scalar_tensor_tensor(cs, cs, 1.0 / c, t1, ALU.add, ALU.mult))
            link(v.tensor_scalar(cs, cs, 1.0, None, ALU.add))
            for _ in range(2):
                link(mul(t2, sn, sn))
                link(v.scalar_tensor_tensor(sn, sn, 2.0, cs, ALU.mult, ALU.mult))
                link(v.tensor_scalar(cs, t2, -2.0, 1.0, ALU.mult, ALU.add))
            link(mul(ar, ex, cs))
            link(mul(ai, ex, sn))
            link(v.tensor_scalar(am, ar, -1.0, None, ALU.add))
            link(mul(den, lre, lre))
            link(mul(t0, lim_, lim_))
            link(add(den, den, t0))
            link(v.reciprocal(den, den))
            link(mul(t0, am, lre))
            link(mul(t1, ai, lim_))
            link(add(t0, t0, t1))
            link(mul(wr_, t0, den))
            link(mul(t0, ai, lre))
            link(mul(t1, am, lim_))
            link(sub(t0, t0, t1))
            link(mul(wi_, t0, den))

            def cmul(orr, oi, xr, xi, yr, yi, tr):
                link(mul(orr, xr, yr))
                link(mul(tr, xi, yi))
                link(sub(orr, orr, tr))
                link(mul(oi, xr, yi))
                link(mul(tr, xi, yr))
                link(add(oi, oi, tr))

            dve.wait_ge(s5b_in, 64)

            def over(x, n):
                return x.unsqueeze(2).to_broadcast([P, 16, n])

            tb = vtmp[:, 0:256].rearrange("p (g c) -> p g c", g=16)
            cmul(bbr, bbi, over(wr_, CH), over(wi_, CH), bre, bim, tb)
            v.memset(pwr[:, 0, :], 1.0)
            v.memset(pwi[:, 0, :], 0.0)
            v.tensor_copy(pwr[:, 1, :], ar)
            link(v.tensor_copy(pwi[:, 1, :], ai))
            for n in (1, 2, 4):
                a, b = slice(1, n + 1), slice(n + 1, 2 * n + 1)

                def times(x):
                    return x[:, n:n + 1, :].to_broadcast([P, n, 16])

                cmul(pwr[:, b, :], pwi[:, b, :], pwr[:, a, :], pwi[:, a, :], times(pwr), times(pwi),
                     vtmp[:, 0:16 * n].rearrange("p (j g) -> p j g", g=16))
            for r, pw in enumerate((pwr, pwi)):
                v.tensor_copy(pV[:, r, 0:8, :], pw[:, 7::-1, 0:8].rearrange("p j g -> p g j"))
                v.tensor_copy(pV[:, r, 8:16, :], pw[:, 0:8, 8:16].rearrange("p j g -> p g j"))
                v.tensor_copy(pC[:, r, 0:8, :], pw[:, 1:9, 0:8].rearrange("p j g -> p g j"))
                link(v.tensor_copy(pC[:, r, 8:16, :], pw[:, 8:0:-1, 8:16].rearrange("p j g -> p g j")))
            def power_of(x, r):
                return x[:, r].unsqueeze(3).to_broadcast([P, 16, Q, CH])

            def channel_of(x):
                return x.unsqueeze(2).to_broadcast([P, 16, Q, CH])

            Vr, Vi = (V[:, :, r, :].rearrange("p g (m c) -> p g m c", m=Q) for r in range(2))
            vt4 = vtmp.rearrange("p (g m c) -> p g m c", g=16, m=Q)
            link(mul(Vr, power_of(pV, 0), channel_of(bbr)))
            link(mul(vt4, power_of(pV, 1), channel_of(bbi)))
            link(sub(Vr, Vr, vt4))
            link(mul(Vi, power_of(pV, 0), channel_of(bbi)))
            link(mul(vt4, power_of(pV, 1), channel_of(bbr)))
            link(add(Vi, Vi, vt4), "V_done")
            dve.sem_inc(V_ready, 1)
            dve.wait_ge(const_in, 16)
            ring.wait_emptied(dve, "cpar1")
            for h in range(2):
                hm = con("halfm")[:, h:h + 1]
                v.tensor_scalar(c0[:, h, :, 0, :], cT[:, 0], hm, None, ALU.mult)
                ins = v.tensor_scalar(c0[:, h, :, 1, :], cT[:, 1], hm, -1.0, ALU.mult, ALU.mult)
            link(ins, "C0_done")

            v.memset(pAr[:, 0, :], 1.0)
            v.memset(pAi[:, 0, :], 0.0)
            v.tensor_copy(pAr[:, 1, :], pwr[:, Q, :])
            link(v.tensor_copy(pAi[:, 1, :], pwi[:, Q, :]))
            for n in (1, 2, 4):
                a, b = slice(1, n + 1), slice(n + 1, 2 * n + 1)
                cmul(pAr[:, b, :], pAi[:, b, :], pAr[:, a, :], pAi[:, a, :],
                     pAr[:, n:n + 1, :].to_broadcast([P, n, 16]), pAi[:, n:n + 1, :].to_broadcast([P, n, 16]),
                     ptmp[:, 0:16 * n].rearrange("p (j g) -> p j g", g=16))
            for dst, j in ((cA, slice(0, SG)), (cG.unsqueeze(1), slice(SG, SG + 1))):
                v.tensor_copy(dst[:, :, 0, :, 0], pAr[:, j, :])
                v.tensor_scalar(dst[:, :, 0, :, 1], pAi[:, j, :], -1.0, None, ALU.mult)
                v.tensor_copy(dst[:, :, 1, :, 0], pAi[:, j, :])
                link(v.tensor_copy(dst[:, :, 1, :, 1], pAr[:, j, :]))

            ring.wait_emptied(dve, "C")
            n_ = PADW - 4
            for k in range(5):
                for a in range(4):
                    wc = prm[:, R_CONVW + 4 * k + a:R_CONVW + 4 * k + a + 1]
                    if k == 0:
                        ins = v.tensor_scalar(cv[:, a, 2:2 + n_], xbc[:, a, 0:n_], wc,
                                              prm[:, R_CONVB + a:R_CONVB + a + 1], ALU.mult, ALU.add)
                    else:
                        ins = v.scalar_tensor_tensor(cv[:, a, 2:2 + n_], xbc[:, a, k:k + n_], wc, cv[:, a, 2:2 + n_],
                                                     ALU.mult, ALU.add)
                if k == 0:
                    v.memset(cv[:, :, 0:2], 0.0)
                    ins = v.memset(cv[:, :, 2 + n_:], 0.0)
                link(ins)
            dve.sem_inc(S("conv_ready"), 1)
            ring.wait_filled(dve, "z")
            Cr, Ci = (Cc[:, :, r, :].rearrange("p g (m c) -> p g m c", m=Q) for r in range(2))
            cct = mix(11264, 2048).rearrange("p (g m c) -> p g m c", g=16, m=Q)
            link(mul(Cr, power_of(pC, 0), channel_of(cT[:, 0])))
            link(mul(cct, power_of(pC, 1), channel_of(cT[:, 1])))
            link(sub(Cr, Cr, cct))
            link(mul(Ci, power_of(pC, 0), channel_of(cT[:, 1])))
            link(mul(cct, power_of(pC, 1), channel_of(cT[:, 0])))
            link(add(Ci, Ci, cct))
            link(v.tensor_scalar(Ci, Ci, -1.0, None, ALU.mult), "Cc_done")

            ring.wait_emptied(dve, "D3")
            W8 = W.rearrange("p (m s) o g t -> p m s o g t", s=SG)
            SH8 = SH.rearrange("p (m s) r g -> p m s r g", s=SG)

            def flat(x):
                return x.rearrange("p m o g -> p m (o g)")

            v.memset(SH8[:, :, 0], 0.0)
            link(v.tensor_copy(flat(SH8[:, :, 1]), flat(W8[:, :, 0, :, :, 2])))
            for q in range(1, SG):
                for o in range(2):
                    ins = v.tensor_tensor(W8[:, :, q, o, :, 0:2], cA[:, 1, o].unsqueeze(1).to_broadcast([P, SG, 16, 2]),
                                          SH8[:, :, q].rearrange("p m r g -> p m g r"), ALU.mult)
                link(ins)
                dst = SH8[:, :, q + 1] if q < SG - 1 else WG[:, :, :, :, 2]
                link(v.tensor_reduce(flat(dst), W8[:, :, q].rearrange("p m o g t -> p m (o g) t"), AX.X, ALU.add))
            v.memset(SB[:, 0], 0.0)
            link(v.tensor_copy(SB[:, 1], WG[:, 0, :, :, 2]))
            for m in range(1, SG - 1):
                link(v.tensor_tensor(WG[:, m, :, :, 0:2], cG, SB[:, m].rearrange("p r g -> p g r").unsqueeze(1)
                                     .to_broadcast([P, 2, 16, 2]), ALU.mult))
                link(v.tensor_reduce(SB[:, m + 1], WG[:, m], AX.X, ALU.add))
            for m in range(SG // 2, SG):
                for o in range(2):
                    ins = v.tensor_tensor(W8[:, m, :, o, :, 0:2], cA[:, :, o], SB[:, m].rearrange("p r g -> p g r")
                                          .unsqueeze(1).to_broadcast([P, SG, 16, 2]), ALU.mult)
            link(ins)
            link(v.tensor_reduce(carried, W[:, LCH:, :, :, 0:2].rearrange("p c o g t -> p c (o g) t"), AX.X, ALU.add))
            SHl = SH[:, LCH:].rearrange("p c r g -> p c (r g)")
            link(add(SHl, SHl, carried))
            for h in range(2):
                hm = con("halfm")[:, h:h + 1]
                v.tensor_scalar(SHm[:, h, :, 0:8, :], SH[:, LCH:, :, 0:8].rearrange("p c r g -> p c g r"), hm, None, ALU.mult)
                ins = v.tensor_scalar(SHm[:, h, :, 8:16, :],
                                      SH[:, NCH - 1:LCH - 1:-1, :, 8:16].rearrange("p c r g -> p c g r"), hm, None,
                                      ALU.mult)
            link(ins, "SHm_done")
            dve.sem_inc(T_free, 1)

            ring.wait_emptied(dve, "zg1")
            link(v.scalar_tensor_tensor(gln, gz, -1.0, gz, ALU.mult, ALU.max), "gabs")
            mod_out(2, 4)
            dve.wait_ge(S("glog"), 1)
            link(v.scalar_tensor_tensor(gz, gz, 0.0, gln, ALU.min, ALU.subtract))
            link(v.tensor_scalar(gz, gz, 1.0 / GATE_TAU, None, ALU.mult))
            v.tensor_tensor_scan(gb[:, 0, :], con("scan"), gz[:, 0, :], 0.0, ALU.mult, ALU.add)
            link(v.tensor_tensor_scan(gb[:, 1, ::-1], con("scan"), gz[:, 1, ::-1], 0.0, ALU.mult, ALU.add))

            def chunks(x):
                return x.rearrange("p (n c) -> p n c", c=CSZ)

            for x in (dtR, cumR, wR):
                v.memset(x[0:ROW0, :], 0.0)
            link(v.tensor_scalar(dtR[ROW0:, :], miscT[ROW0:, :], prm[ROW0:, R_DTB:R_DTB + 1], None, ALU.add))
            link(v.scalar_tensor_tensor(tR[ROW0:, :], dtR[ROW0:, :], -1.0, dtR[ROW0:, :], ALU.mult, ALU.max), "dt_abs")
            dve.wait_ge(S("dt_log"), 1)
            link(v.scalar_tensor_tensor(dtR[ROW0:, :], dtR[ROW0:, :], 0.0, tR[ROW0:, :], ALU.max, ALU.add))
            link(v.tensor_scalar(tR[ROW0:, :], dtR[ROW0:, :], anegc[ROW0:, :], -1.0, ALU.mult, ALU.mult))
            v.tensor_tensor_scan(cumR[64:96, :], con("scan")[64:96, :], tR[64:96, :], 0.0, ALU.mult, ALU.add)
            link(v.tensor_tensor_scan(cumR[96:128, ::-1], con("scan")[96:128, :], tR[96:128, ::-1], 0.0, ALU.mult,
                                      ALU.add))
            for d in range(2):
                last = CSZ - 1 if d == 0 else 0
                a, b = ROW0 + 32 * d, ROW0 + 32 * d + 32
                ins = sub(chunks(wR[a:b, :]), chunks(cumR[a:b, :])[:, :, last:last + 1].to_broadcast([32, NCK, CSZ]),
                          chunks(cumR[a:b, :]))
            link(ins, "cum_ready")
            dve.wait_ge(S("w_exp"), 1)
            link(mul(wR[ROW0:, :], wR[ROW0:, :], dtR[ROW0:, :]), "rows_ready")
            ring.wait_filled(dve, "Yt")
            dve.wait_ge(S("conv_exp"), 1)
            mul(XC[:, :, 0:NCTX], cv[:, :, 2:2 + NCTX], ce[:, :, 2:2 + NCTX])

            def lat_rows(tile, a):
                return tile[:, a, NCTX + 4:].rearrange("p (r w) -> p r w", w=CSZ + 4)[:, :, 2:2 + CSZ]

            for a in range(4):
                ins = mul(XC[:, a, NCTX:].rearrange("p (r w) -> p r w", w=CSZ), lat_rows(cv, a), lat_rows(ce, a))
            link(ins, "XC_ready")
            for d in range(2):
                last = CSZ - 1 if d == 0 else 0
                ins = sub(chunks(gln[:, d, :]),
                          chunks(gb[:, d, :])[:, :, last:last + 1].to_broadcast([P, NCK, CSZ]), chunks(gb[:, d, :]))
            link(ins, "gscan")
            dve.wait_ge(S("gexp"), 1)
            for d in range(2):
                for h in range(4):
                    ins = v.scalar_tensor_tensor(qm[:, d, h, :], qT, con("headm")[:, h:h + 1], qin[:, d, :], ALU.mult,
                                                 ALU.mult)
            link(ins)
            link(mul(qin, qin, qT.unsqueeze(1).to_broadcast([P, 2, NLAT])))
            mul(kin, kin, kTt[:, NCTX:].unsqueeze(1).to_broadcast([P, 2, NLAT]))
            link(mul(gln, gln, kTt.unsqueeze(1).to_broadcast([P, 2, NTOK])), "gla_ready")
            dve.wait_ge(S("y_in"), 16)
            y5, e5, g5, _ = fin5
            for a in range(2):
                ins = v.scalar_tensor_tensor(y5[:, a, :].rearrange("p (c i) -> p i c", i=Q),
                                             uT[:, a, :].rearrange("p (j c) -> p j c", j=Q)[:, :, NCH - LCH:],
                                             prm[:, R_S5D + a:R_S5D + a + 1], ychunks[:, a], ALU.mult, ALU.add)
            link(ins)
            link(mul(e5, y5, y5))
            link(v.tensor_scalar(e5, e5, 0.044715, 1.0, ALU.mult, ALU.add))
            link(mul(e5, e5, y5), "gelu_in")
            dve.wait_ge(S("gelu_exp"), 1)
            link(mul(y5, y5, e5), "gelu_ready")
            ring.wait_emptied(dve, "glu")
            link(mul(mixT[:, 2:4, :], y5, g5))

            mod_out(4, 6)
            for d in range(2):
                ring.wait_filled(dve, f"kd{d}")
                for h in range(2):
                    ins = v.tensor_scalar(kdM[:, d, :, h, :], bank(f"kd{d}").rearrange("p (a n) -> p a n", a=4),
                                          con("halfm")[:, h:h + 1], None, ALU.mult)
                ring.mark_emptied(ins, f"kd{d}", "dve")
            for i in range(4):
                d, a = divmod(i, 2)
                ring.wait_filled(dve, f"att{i}")
                ring.mark_emptied(v.tensor_tensor(
                    att[:, d, a], bank(f"att{i}").rearrange("p (h t) -> p h t", h=4),
                    con("tri")[:, P * d:P * (d + 1)].unsqueeze(1).to_broadcast([P, 4, P]), ALU.mult), f"att{i}", "dve")
            hmask = con("headm").unsqueeze(2).to_broadcast([P, 4, 64])
            for n in range(NCK - 1):
                ring.wait_filled(dve, f"ds{n}")
                for d in range(2):
                    b_ = bank(f"ds{n}")[:, 256 * d:256 * (d + 1)]
                    chunk_ = n if d == 0 else (3 - n if n < 4 else 11 - n)
                    if n == 0:
                        ins = v.tensor_copy(Srun[:, d, :], b_)
                    else:
                        ins = v.scalar_tensor_tensor(Srun[:, d, :], Srun[:, d, :], gdec[:, d, chunk_:chunk_ + 1], b_,
                                                     ALU.mult, ALU.add)
                emptied(ins, f"ds{n}")
                if n >= 3:
                    for d in range(2):
                        ins = mul(SM[:, d, n - 3, :].rearrange("p (h n) -> p h n", h=4),
                                  Srun[:, d, :].rearrange("p (h n) -> p h n", h=4), hmask)
                    link(ins)
            dve.sem_inc(S("SM_ready"), 1)
            ring.wait_filled(dve, "og")
            emptied(v.tensor_copy(go.rearrange("p a t -> p (a t)"), bank("og")), "og")
            dve.sem_inc(S("go_ready"), 1)
            dve.wait_ge(S("gsl_ready"), 1)
            link(mul(gsl, gsl, rT))
            ring.wait_emptied(dve, "gss")
            link(v.reciprocal(grs, grs))
            link(mul(go, go, grs))
            link(v.scalar_tensor_tensor(mixT[:, 4:6, :], go, prm[:, R_GLAG:R_GLAG + 1], gsl, ALU.mult, ALU.mult))

            for g in range(2):
                ins = v.tensor_scalar(Cg[:, g, :], XC[:, 3, NCTX:], con("halfm")[:, g:g + 1], None, ALU.mult)
            link(ins, "Cg_ready")
            for i in range(3):
                ring.wait_filled(dve, f"rT{i}")
                src = bank(f"rT{i}").rearrange("p (a m x) -> p a m x", a=4, m=4)[:, :, 2:4, 0:4]
                emptied(v.tensor_copy(cols[:, i], src), f"rT{i}")

            def heads(x):
                return x.rearrange("p (h n) -> p h n", h=4)

            for a in range(4):
                ring.wait_filled(dve, f"xt{a}")
                xb = heads(bank(f"xt{a}")[:, 0:256])
                for d in range(2):
                    mul(heads(xdec[:, a, d, :]), xb, cols[:, 2, a, d, :].unsqueeze(2).to_broadcast([P, 4, 64]))
                    if a >= 2:
                        mul(heads(xdt[:, a - 2, d, :]), xb, cols[:, 0, a, d, :].unsqueeze(2).to_broadcast([P, 4, 64]))
                for h in range(2):
                    ins = v.tensor_scalar(BTM[:, a, h, :], bank(f"xt{a}")[:, 256:384], con("halfm")[:, h:h + 1], None,
                                          ALU.mult)
                ring.mark_emptied(ins, f"xt{a}", "dve")
            for i in range(4):
                dve.wait_ge(S("ecr_ready"), i + 1)
                for r in (2 * i, 2 * i + 1):
                    d, h = divmod(r, 4)
                    for a in range(2):
                        o = NLAT * (r % 2) + P * a
                        ins = v.scalar_tensor_tensor(SEG[:, r, a, :], bank(f"rb{i}")[:, o:o + P],
                                                     cols[:, 1, 2 + a, d, h:h + 1], con("neg")[:, P * d:P * (d + 1)],
                                                     ALU.subtract, ALU.add)
                ring.mark_emptied(ins, f"rb{i}", "dve")
            ring.wait_emptied(dve, "rb3")
            dve.sem_inc(S("seg_ready"), 1)
            for d in range(2):
                e4 = ECR[:, 4 * d:4 * d + 4, :].rearrange("p (g h) t -> p g h t", g=2)
                ins = mul(e4, e4, Cg.unsqueeze(2).to_broadcast([P, 2, 2, NLAT]))
            link(ins)
            dve.wait_ge(S("seg_exp"), 1)
            for a in range(2):
                ring.wait_filled(dve, f"bc{a}")
                bc_ = bank(f"bc{a}")[:, 0:256].rearrange("p (g t) -> p g t", g=2).unsqueeze(2).to_broadcast([P, 2, 2, P])
                for d in range(2):
                    s4 = SEG[:, 4 * d:4 * d + 4, a, :].rearrange("p (g h) t -> p g h t", g=2)
                    ins = mul(s4, s4, bc_)
                ring.mark_emptied(ins, f"bc{a}", "dve")
            for n in range(NCK - 1):
                ring.wait_filled(dve, f"sds{n}")
                for d in range(2):
                    b_ = bank(f"sds{n}")[:, 256 * d:256 * (d + 1)]
                    chunk_ = n if d == 0 else (3 - n if n < 4 else 11 - n)
                    dst = SSrun[:, d, :] if n < 3 else SE[:, d, n - 3, :]
                    if n == 0:
                        ins = v.tensor_copy(dst, b_)
                    else:
                        prev = SSrun[:, d, :] if n <= 3 else SE[:, d, n - 4, :]
                        link(mul(heads(dst), heads(prev),
                                 DEC[:, 4 * d:4 * d + 4, chunk_].unsqueeze(2).to_broadcast([P, 4, 64])))
                        ins = add(dst, dst, b_)
                emptied(ins, f"sds{n}")
            dve.sem_inc(S("SE_ready"), 1)
            sy, ssq_, srt, ssl = fin5
            dve.wait_ge(S("sz_exp"), 1)
            link(mul(ssl, ssl, zT))
            ring.wait_filled(dve, "oy")
            for a in range(2):
                ins = v.scalar_tensor_tensor(sy[:, a, :], XC[:, a, NCTX:], s5p[:, PAIR_D + a:PAIR_D + a + 1],
                                             bank("oy")[:, NLAT * a:NLAT * (a + 1)], ALU.mult, ALU.add)
            emptied(ins, "oy")
            link(mul(sy, sy, ssl), "yz_ready")
            ring.wait_emptied(dve, "yss")
            link(v.reciprocal(srt[:, 0, :], srt[:, 0, :]))
            for a in range(2):
                ins = v.scalar_tensor_tensor(mixT[:, 6 + a, :], sy[:, a, :], prm[:, R_SSDG + a:R_SSDG + a + 1],
                                             srt[:, 0, :], ALU.mult, ALU.mult)
            link(ins, "mixers_done")
            v.memset(bgu, 0.0).then_inc(S("bgu_zeroed"), 1)

            for i in range(4):
                ring.wait_filled(dve, f"wo{i}")
                for o in (2 * i, 2 * i + 1):
                    ins = v.scalar_tensor_tensor(xT[:, o, :], bank(f"wo{i}")[:, NLAT * (o % 2):NLAT * (o % 2) + NLAT],
                                                 mod[:, 16 + o, 0:1], xT[:, o, :], ALU.mult, ALU.add)
                    if o % 2 == 0:
                        link(ins, "x2_ready")
                emptied(ins, f"wo{i}")
                dve.sem_inc(S("x2_ready"), 1)
                counts["x2_ready"] += 1
            g2 = tiny[:, 60:68].unsqueeze(2)
            gain(g2, mod[:, 32:40, 0:1], R_GFFN)
            ring.wait_emptied(dve, "ss2")
            link(v.reciprocal(mixT[:, 0, :], mixT[:, 0, :]))
            link(mul(h2T, xT, mixT[:, 0:1, :].to_broadcast([P, KT, NLAT])))
            for k in range(KT):
                ins = v.tensor_scalar(h2T[:, k, :], h2T[:, k, :], g2[:, k, :], mod[:, 24 + k, 0:1], ALU.mult, ALU.add)
            link(ins, "h2T_ready")
            v.memset(Em, 0.0)
            v.memset(ey, 0.0).then_inc(S("y_ready"), 1)

            ring.wait_filled(dve, "lg")
            dve.wait_ge(S("router_in"), 32)
            emptied(v.tensor_tensor(lg, bank("lg")[:, 0:64].rearrange("p (a e) -> p a e", a=2),
                                    rbias.unsqueeze(1).to_broadcast([P, 2, NE]), ALU.add), "lg")
            for a in range(2):
                ins = v.max(top[:, a, :], lg[:, a, :])
            link(ins)
            link(v.tensor_scalar(nmax, top[:, :, 0], -1.0, None, ALU.mult), "lmax_ready")
            for a in range(2):
                th = top[:, a, TOPK - 1:TOPK]
                v.tensor_scalar(gt[:, a, :], lg[:, a, :], th, None, ALU.is_gt)
                ins = v.tensor_scalar(eq[:, a, :], lg[:, a, :], th, None, ALU.is_equal)
            link(ins)
            link(v.tensor_reduce(need[:, :, 0], gt, AX.X, ALU.add))
            link(v.tensor_scalar(need[:, :, 0], need[:, :, 0], -1.0, float(TOPK), ALU.mult, ALU.add))
            for a in range(2):
                ins = v.tensor_tensor_scan(rank[:, a, :], con("ones")[:, 0:NE], eq[:, a, :], 0.0, ALU.mult, ALU.add)
            link(ins)
            for a in range(2):
                ins = v.scalar_tensor_tensor(eq[:, a, :], rank[:, a, :], need[:, a, 0:1], eq[:, a, :], ALU.is_le,
                                             ALU.mult)
            link(ins)
            link(add(sel, gt, eq), "sel_ready")
            dve.wait_ge(S("gate_exp"), 1)
            link(mul(gate, gate, sel))
            link(v.tensor_reduce(zsum, gate, AX.X, ALU.add))
            link(v.reciprocal(zsum, zsum))
            link(mul(gate, gate, zsum.unsqueeze(2).to_broadcast([P, 2, NE])))
            ring.wait_filled(dve, "pos")
            emptied(v.tensor_tensor(posm, bank("pos")[:, 0:64].rearrange("p (a e) -> p a e", a=2), sel, ALU.mult),
                    "pos")
            dve.sem_inc(S("posm_ready"), 1)
            ring.wait_filled(dve, "pgT")
            v.tensor_copy(posT[0:NE, :], bank("pgT")[0:NE, 0:256])
            emptied(v.tensor_copy(gatT[0:NE, :], bank("pgT")[0:NE, 256:512]), "pgT")
            ring.wait_filled(dve, "cnt")
            ne = slice(0, NE)
            emptied(v.tensor_copy(nb[ne, 1:2], bank("cnt")[ne, 0:1]), "cnt")
            link(v.tensor_scalar(nb[ne, 0:1], nb[ne, 1:2], 0.0, con("first", NE), ALU.is_gt, ALU.max))
            for b_ in range(1, -(-NLAT // CAP)):
                link(v.scalar_tensor_tensor(nb[ne, 0:1], nb[ne, 1:2], float(CAP * b_), nb[ne, 0:1], ALU.is_gt, ALU.add))
            dve.sem_inc(S("nb_ready"), 1)
            ring.wait_filled(dve, "start")
            emptied(v.tensor_copy(nb[ne, 2:3], bank("start")[ne, 0:1]), "start")
            link(v.tensor_scalar(Et[ne, :], con("items", NE), nb[ne, 2:3], None, ALU.subtract))
            link(v.tensor_scalar(Em[ne, :], Et[ne, :], 0.0, None, ALU.is_ge))
            link(v.scalar_tensor_tensor(Em[ne, :], Et[ne, :], nb[ne, 0:1], Em[ne, :], ALU.is_lt, ALU.mult))
            link(v.tensor_scalar(Et[ne, :], Et[ne, :], -float(CAP), None, ALU.mult))
            link(mul(Eb[ne, :], Et[ne, :], Em[ne, :]), "E_ready")
            ring.wait_filled(dve, "it0")
            i4 = bank("it0")[:, 0:4 * NI].rearrange("p (w i) -> p w i", w=4)
            v.tensor_copy(posI, i4[:, 0:2, :])
            emptied(v.tensor_copy(gatI, i4[:, 2:4, :]), "it0")
            ring.wait_filled(dve, "ids")
            emptied(v.tensor_copy(ids[0:1, :], bank("ids")[0:1, 0:NI + 1]), "ids")
            dve.sem_inc(S("ids_ready"), 1)

            def select(col):
                for a in range(2):
                    ins = v.tensor_tensor(Ssel[:, a, :], con("iota")[:, 0:CAP],
                                          posI[:, a, bass.ds(col, 1)].to_broadcast([P, CAP]), ALU.is_equal)
                return ins

            def gates(col):
                for a in range(2):
                    ins = v.tensor_tensor(Sgat[:, a, :], con("iota"),
                                          posI[:, a, bass.ds(col, 1)].to_broadcast([P, 2 * CAP]), ALU.is_equal)
                ins.then_inc(S("sgat_chain"), 1)

            def scale_gates(col):
                v.tensor_tensor(Sgat, Sgat, gatI[:, :, bass.ds(col, 1)].to_broadcast([P, 2, 2 * CAP]),
                                ALU.mult).then_inc(S("sgat_ready"), 1)

            def gt_out(n):
                dve.wait_ge(S("gt_full"), n)
                dve.wait_ge(S("sc_full"), n)
                v.tensor_copy(GT, psum[:, 2, 0:NLAT]).then_inc(S("gt_ready"), 1)

            select(1).then_inc(S("s_ready"), 1)
            n_items = dve.value_load(ids[0:1, NI:NI + 1], min_val=2, max_val=NI - 2)

            dve.sem_inc(S("gu_emptied"), 1)
            gates(0)
            dve.wait_ge(S("sgat_chain"), 1)
            scale_gates(0)
            with dve.Fori(0, n_items) as it:
                dve.wait_ge(S("g_full"), it + 1)
                v.tensor_copy(Ecol, Em[:, bass.ds(it + 1, 1)].to_broadcast([P, CAP])).then_inc(S("Ecol_ready"), 1)
                select(it + 2).then_inc(S("s_ready"), 1)
                gt_out(it + 1)
                gates(it + 1)
                dve.wait_ge(S("sgat_chain"), it + 2)
                scale_gates(it + 1)
                dve.wait_ge(S("gu_full"), it + 1)
                gu = psum[:, 0:2, :].rearrange("p b (f w) -> p b f w", w=2)
                eg2, eu2 = (x.rearrange("p (b f) -> p b f", b=2) for x in (eg, eu))
                v.tensor_scalar(eg2, gu[:, :, :, 0], LIMIT, None, ALU.min).then_inc(S("gclip_ready"), 1)
                v.tensor_scalar(eu2, gu[:, :, :, 1], LIMIT, -LIMIT, ALU.min, ALU.max).then_inc(S("gu_emptied"), 1)
                dve.wait_ge(S("gclip_ready"), it + 1)
                dve.wait_ge(S("gu_emptied"), it + 2)
                v.scalar_tensor_tensor(eu, eu, 1.0, eg, ALU.add, ALU.mult).then_inc(S("ug_ready"), 1)
                dve.wait_ge(S("ug_ready"), it + 1)
                dve.wait_ge(S("sig_ready"), it + 1)
                v.tensor_tensor(eu, eu, es, ALU.mult).then_inc(S("act_ready"), 1)
                dve.wait_ge(S("at_full"), it + 1)
            gt_out(n_items + 1)
            dve.wait_ge(S("sc_full"), n_items + 2)
            for k in range(KT):
                v.scalar_tensor_tensor(xT[:, k, :], facc[:, k, :], mod[:, 40 + k, 0:1], xT[:, k, :], ALU.mult,
                                       ALU.add).then_inc(S("x3_ready"), 1)
            dve.wait_ge(S("last_root"), 1)
            dve.wait_ge(S("gfin_in"), 16)
            for a in range(2):
                v.scalar_tensor_tensor(h2TM[:, a, :].rearrange("p (b n) -> p b n", b=2), psum[:, 2 * a:2 * a + 2, :],
                                       tiny[:, 52 + a:53 + a], gfin.rearrange("p (b n) -> p b n", b=2),
                                       ALU.mult, ALU.mult).then_inc(S("out_ready"), 1)

        @block.tensor
        def _(pe):
            mm = nc.tensor.matmul

            def start(name):
                ring.wait_free(pe, name)
                return bank(name)

            def transposed(o, x):
                n = x.shape[0]
                return nc.tensor.transpose(o, x, ident[0:n, 0:n])

            pe.wait_ge(S("ident_in"), 16)
            pe.wait_ge(par_in, 16 * NPAR_IN)
            ring.mark_filled(transposed(start("par")[:, 0:NPAR], par1[0:NPAR, :]))
            pe.wait_ge(S("pairs_spread"), 4)
            ring.mark_filled(transposed(start("s5par")[:, 0:NPAR2], par2[0:NPAR2, :]))
            pe.wait_ge(x_in, 64)
            for i in range(4):
                b = start(f"xraw{i}")
                for j in range(4):
                    k = 2 * i + j // 2
                    ins = transposed(b[:, P * j:P * (j + 1)], staging[:, 2 + j % 2, P * k:P * (k + 1)])
                ring.mark_filled(ins)

            def wait_slot(n):
                pe.wait_ge(loaded[n % FR], 16 * (n // FR + 1))

            def both(ins):
                ring.mark_filled(ins)
                pe.wait_ge(filled, ring.done["pe"])
                pe.sem_inc(slot_read, 1)

            def ada_rows(i):
                b = start(f"ar{i}")
                for blk in range(4):
                    n = AT[("ada", 4 * i + blk)]
                    wait_slot(n)
                    for k in range(KT // 2):
                        for o in range(2):
                            for h in range(2):
                                q = 32 * (2 * o + h)
                                kk = KT // 2 * h + k
                                ins = mm(b[q:q + 32, P * blk:P * (blk + 1)], cond[:, kk, :],
                                         sview(n)[:, kk, P * o:P * (o + 1)], start=(k == 0),
                                         stop=(k == KT // 2 - 1), skip_group_check=True)
                    if blk < 3:
                        ins.then_inc(slot_read, 1)
                both(ins)

            def ada_turn(i):
                ring.wait_emptied(pe, f"ar{i}")
                b = start(f"at{i}")
                for j in range(4):
                    ins = transposed(b[:, P * j:P * (j + 1)], ada_sb[i][:, P * j:P * (j + 1)])
                ring.mark_filled(ins)

            pe.wait_ge(S("cond_silu"), 1)
            for i in range(2):
                ada_rows(i)
            for i in range(2):
                ada_turn(i)

            pe.wait_ge(xn_ready, 1)
            for k in range(KT):
                b = start(f"xn{k}")
                for i in range(4):
                    ins = transposed(b[:, P * i:P * (i + 1)], staging[:, i, P * k:P * (k + 1)])
                ring.mark_filled(ins)

            pe.wait_ge(S("s5c_in"), 16 * 4)
            for r in range(2):
                b = start(f"cpar{r}")
                for i in range(4):
                    ins = transposed(b[:, P * i:P * (i + 1)], crow[:, r, i, :])
                ring.mark_filled(ins)
            pe.wait_ge(const_in, 16)
            ring.wait_emptied(pe, f"xn{KT - 1}")

            def feature_major(o, n, c0_, toks):
                for k in range(KT):
                    ins = mm(o, sview(n)[:, k, c0_:c0_ + P], hT[:, k, toks], start=(k == 0), stop=(k == KT - 1))
                return ins

            every, lat = slice(0, NTOK), slice(NCTX, NTOK)

            def two_lat(name, blk):
                n = AT[("win", blk)]
                wait_slot(n)
                b = start(name)
                for o in range(2):
                    ins = feature_major(b[:, NLAT * o:NLAT * (o + 1)], n, P * o, lat)
                return ins

            both(two_lat("four", W_FOUR))
            n = AT[("win", W_U)]
            wait_slot(n)
            ring.mark_filled(feature_major(start("u0"), n, 0, every))
            both(feature_major(start("u1"), n, P, every))
            n = AT[("win", W_X)]
            wait_slot(n)
            ring.mark_filled(feature_major(start("x0"), n, 0, every))
            both(feature_major(start("x1"), n, P, every))
            n = AT[("win", W_BC)]
            wait_slot(n)
            ring.mark_filled(feature_major(start("B"), n, 0, every))
            both(feature_major(start("C")[:, 0:NLAT], n, P, lat))

            n = AT[("win", W_QK)]
            wait_slot(n)
            ring.mark_filled(feature_major(start("q")[:, 0:NLAT], n, 0, lat))
            both(feature_major(start("k"), n, P, every))
            n = AT[("win", W_V)]
            wait_slot(n)
            for i in range(2):
                b = start(f"v{i}")
                for a in (2 * i, 2 * i + 1):
                    for k in range(KT):
                        ins = mm(b[:, 256 * (a % 2):256 * (a % 2 + 1)], hT[:, k, P * a:P * (a + 1)], sview(n)[:, k, :],
                                 start=(k == 0), stop=(k == KT - 1))
                if i == 0:
                    ring.mark_filled(ins)
            both(ins)
            both(two_lat("r", W_R))
            pe.wait_ge(V_ready, 1)
            for i in range(8):
                b = start(f"VT{i}")
                for j in range(4):
                    g, r = divmod(4 * i + j, 2)
                    ins = transposed(b[:, P * j:P * (j + 1)], V[:, g, r, :])
                ring.mark_filled(ins)
            pe.wait_ge(S("C0_done"), 1)
            for d in range(2):
                b = start(f"Kr{d}")
                for r4 in range(4):
                    for r in range(2):
                        for q in range(4):
                            g = 4 * r4 + q
                            dg = 8 * d + g // 2
                            at_ = CH * (2 * (16 * (g % 2) + dg) + r)
                            ins = mm(b[32 * q:32 * (q + 1), P * r4:P * (r4 + 1)],
                                     c0f[:, at_:at_ + 2 * CH], V[:, dg, r, :],
                                     start=(r == 0), stop=(r == 1), skip_group_check=True)
                ring.mark_filled(ins)
            for d in range(2):
                ring.wait_emptied(pe, f"Kr{d}")
                b = start(f"Kq{d}")
                for r4 in range(4):
                    ins = transposed(b[:, P * r4:P * (r4 + 1)], kr[:, d, P * r4:P * (r4 + 1)])
                ring.mark_filled(ins)

            n = AT[("win", W_MISC)]
            pe.wait_ge(S("misc_in"), 32)
            wait_slot(n)
            both(feature_major(start("misc"), n, 0, every))
            both(two_lat("z", W_Z))
            ring.wait_emptied(pe, "four")
            for i in range(2):
                b = start(f"fA{i}")
                for f in range(2):
                    ins = mm(b[:, 256 * f:256 * (f + 1)], fourT[:, f, P * i:P * (i + 1)], con("cbd"), start=True,
                             stop=True)
                ring.mark_filled(ins)
            ring.wait_emptied(pe, "fA1")
            b = start("fB")
            for f in range(2):
                for i in range(2):
                    for w, tab in enumerate(("cseq", "sseq")):
                        ins = mm(b[:, NLAT * f:NLAT * (f + 1)], fA[:, i, f, P * w:P * (w + 1)],
                                 con(tab)[:, NLAT * i:NLAT * (i + 1)], start=(i + w == 0), stop=(i + w == 2))
            ring.mark_filled(ins)
            pe.wait_ge(fw_in, 16)
            ring.wait_emptied(pe, "fB")
            b = start("fW")
            for o in range(2):
                for k in range(2):
                    ins = mm(b[:, NLAT * o:NLAT * (o + 1)], fourw[:, k, P * o:P * (o + 1)], fourT[:, k, :],
                             start=(k == 0), stop=(k == 1))
            ring.mark_filled(ins)

            pe.wait_ge(S("U_in"), 16 * Q)
            for i in range(4):
                b = start(f"D{i}")
                for r in range(2):
                    for j in range(4):
                        dg = 4 * i + j
                        for h in range(2):
                            o = NCH * (4 * r + j)
                            ins = mm(b[64 * h:64 * h + 64, o:o + NCH], VT[:, dg, r, 64 * h:64 * h + 64],
                                     U[:, 2 * (dg % 8) + h, :], start=True, stop=True)
                ring.mark_filled(ins)

            pe.wait_ge(a2_in, 32)
            for d in range(2):
                ring.mark_filled(mm(start(f"zg{d}"), a2[0:32, P * d:P * (d + 1)], miscT[0:32, :], start=True, stop=True))
            for i in (2, 3):
                ada_rows(i)
            for i in (2, 3):
                ada_turn(i)

            pe.wait_ge(T_in, 16 * Q)
            pe.wait_ge(S("T1_in"), 16 * Q)
            pe.wait_ge(S("SHm_done"), 1)
            b = start("Yt")
            for r4 in range(4):
                def product(q, stat, mov, first, last):
                    return mm(b[LCH * q:LCH * (q + 1), P * r4:P * (r4 + 1)], stat, mov, start=first, stop=last,
                              skip_group_check=True)

                for d in range(2):
                    for q in range(4):
                        g = 4 * r4 + q
                        product(q, U[:, g, LCH:], T5[:, g, d, :], d == 0, False)
                for d in range(2):
                    for r in range(2):
                        for q in range(4):
                            g = 4 * r4 + q
                            dg = 8 * d + g // 2
                            ins = product(q, SHm[:, g % 2, :, dg, r], Cc[:, dg, r, :], False, d + r == 2)
            ring.mark_filled(ins)
            ring.wait_emptied(pe, "Yt")
            b = start("Y")
            for r4 in range(4):
                ins = transposed(b[:, P * r4:P * (r4 + 1)], YT[:, P * r4:P * (r4 + 1)])
            ring.mark_filled(ins)
            for i in (4, 5):
                ada_rows(i)
            pe.wait_ge(glu_in, 16)
            pe.wait_ge(S("gelu_ready"), 1)
            b = start("glu")
            for o in range(2):
                for k in range(2):
                    ins = mm(b[:, NLAT * o:NLAT * (o + 1)], gluw[:, k, P * o:P * (o + 1)], fin5[0][:, k, :],
                             start=(k == 0), stop=(k == 1))
            ring.mark_filled(ins)

            for i in (4, 5):
                ada_turn(i)

            pe.wait_ge(S("gla_ready"), 1)
            for d in range(2):
                b = start(f"kd{d}")
                for a in range(4):
                    ins = transposed(b[:, P * a:P * (a + 1)], gln[:, d, P * a:P * (a + 1)])
                ring.mark_filled(ins)
            for i in range(4):
                d, a = divmod(i, 2)
                ring.mark_filled(mm(start(f"att{i}").rearrange("p (h t) -> p h t", h=4), kin[:, d, P * a:P * (a + 1)],
                                    qm[:, d, :, P * a:P * (a + 1)], start=True, stop=True))

            def chunk_at(n, d):
                return divmod(n if d == 0 else (3 - n if n < 4 else 11 - n), 2)

            ring.wait_emptied(pe, "kd1")
            for n in range(NCK - 1):
                b = start(f"ds{n}")
                for d in range(2):
                    a, h = chunk_at(n, d)
                    ins = mm(b[:, 256 * d:256 * (d + 1)], kdM[:, d, a, h, :], vTM[:, a, :], start=True, stop=True)
                ring.mark_filled(ins)
            pe.wait_ge(S("SM_ready"), 1)
            ring.wait_emptied(pe, "att3")
            b = start("og")
            for vt in range(2):
                for a in range(2):
                    o = NLAT * vt + P * a
                    for d in range(2):
                        for h in (2 * vt, 2 * vt + 1):
                            q0 = 64 * (h % 2)
                            mm(b[q0:q0 + 64, o:o + P], vTM[:, 2 + a, 64 * h:64 * h + 64], att[:, d, a, h, :],
                               start=(d == 0), stop=False, skip_group_check=True)
                    for d in range(2):
                        for c in (2 * a, 2 * a + 1):
                            step = c if d == 0 else 3 - c
                            ins = mm(b[:, NLAT * vt + CSZ * c:NLAT * vt + CSZ * (c + 1)], SM[:, d, step, P * vt:P * (vt + 1)],
                                     qin[:, d, CSZ * c:CSZ * (c + 1)], start=False, stop=(d == 1),
                                     skip_group_check=True)
            ring.mark_filled(ins)
            pe.wait_ge(S("gsq_ready"), 1)
            ring.mark_filled(mm(start("gss"), con("blk64"), gsq.rearrange("p a t -> p (a t)"), start=True, stop=True))

            pe.wait_ge(S("rows_ready"), 1)
            for i, x in enumerate((dtR, cumR, wR)):
                b = start(f"rT{i}")
                for a in range(4):
                    ins = transposed(b[:, P * a:P * (a + 1)], x[:, P * a:P * (a + 1)])
                ring.mark_filled(ins)
            pe.wait_ge(S("XC_ready"), 1)
            for a in range(4):
                b = start(f"xt{a}")
                for j in range(3):
                    ins = transposed(b[:, P * j:P * (j + 1)], XC[:, j, P * a:P * (a + 1)])
                ring.mark_filled(ins)
            rowsel = con("rows").rearrange("p (r n) -> p r n", r=8)
            b = start("decl")
            for r in range(8):
                last = CSZ - 1 if r < 4 else 0
                ins = mm(b[:, 8 * r:8 * r + 8], rowsel[:, r, :], cumR[:, last::CSZ], start=True, stop=True)
            ring.mark_filled(ins)
            for i in range(4):
                b = start(f"rb{i}")
                for r in (2 * i, 2 * i + 1):
                    ins = mm(b[:, NLAT * (r % 2):NLAT * (r % 2 + 1)], rowsel[:, r, :], cumR[:, NCTX:], start=True,
                             stop=True)
                ring.mark_filled(ins)
            pe.wait_ge(S("Cg_ready"), 1)
            for a in range(2):
                b = start(f"bc{a}")
                ring.mark_filled(mm(b[:, 0:256].rearrange("p (g t) -> p g t", g=2),
                                    XC[:, 2, NCTX + P * a:NCTX + P * (a + 1)], Cg[:, :, P * a:P * (a + 1)],
                                    start=True, stop=True))
            ring.wait_emptied(pe, "xt3")
            for n in range(NCK - 1):
                b = start(f"sds{n}")
                for d in range(2):
                    a, h = chunk_at(n, d)
                    ins = mm(b[:, 256 * d:256 * (d + 1)], BTM[:, a, h, :], xdec[:, a, d, :], start=True, stop=True)
                ring.mark_filled(ins)
            pe.wait_ge(S("SE_ready"), 1)
            b = start("oy")
            for h in range(4):
                q0, o0 = 64 * (h % 2), NLAT * (h // 2)
                hs = slice(64 * h, 64 * h + 64)
                for a in range(2):
                    for d in range(2):
                        mm(b[q0:q0 + 64, o0 + P * a:o0 + P * (a + 1)], xdt[:, a, d, hs], SEG[:, 4 * d + h, a, :],
                           start=(d == 0), stop=False, skip_group_check=True)
                    for d in range(2):
                        for c in (2 * a, 2 * a + 1):
                            step = c if d == 0 else 3 - c
                            ins = mm(b[q0:q0 + 64, o0 + CSZ * c:o0 + CSZ * (c + 1)], SE[:, d, step, hs],
                                     ECR[:, 4 * d + h, CSZ * c:CSZ * (c + 1)], start=False, stop=(d == 1),
                                     skip_group_check=True)
            ring.mark_filled(ins)
            pe.wait_ge(S("ysq_ready"), 1)
            b = start("yss")
            for a in range(2):
                ins = mm(b[:, 0:NLAT], con("ones"), fin5[1][:, a, :], start=(a == 0), stop=(a == 1))
            ring.mark_filled(ins)

            pe.wait_ge(S("mixers_done"), 1)
            for i in range(4):
                n = AT[("wout", i)]
                wait_slot(n)
                b = start(f"wo{i}")
                for o in range(2):
                    for k in range(KT):
                        ins = mm(b[:, NLAT * o:NLAT * (o + 1)], sview(n)[:, k, P * o:P * (o + 1)], mixT[:, k, :],
                                 start=(k == 0), stop=(k == KT - 1))
                both(ins)
            b = start("ss2")
            for k in range(KT):
                pe.wait_ge(S("xsq_ready"), k // 2 + 1)
                ins = mm(b[:, 0:NLAT], con("ones"), xsq[:, k, :], start=(k == 0), stop=(k == KT - 1))
            ring.mark_filled(ins)
            pe.wait_ge(S("h2T_ready"), 1)
            for i in range(4):
                b = start(f"h2{i}")
                for j in range(4):
                    a, k = j // 2, 2 * i + j % 2
                    ins = transposed(b[:, P * j:P * (j + 1)], h2T[:, k, P * a:P * (a + 1)])
                ring.mark_filled(ins)

            pe.wait_ge(S("router_in"), 32)
            b = start("lg")
            for a in range(2):
                for k in range(KT):
                    ins = mm(b[:, NE * a:NE * (a + 1)], h2T[:, k, P * a:P * (a + 1)], rw[:, k, :], start=(k == 0),
                             stop=(k == KT - 1))
            ring.mark_filled(ins)
            pe.wait_ge(S("sel_ready"), 1)
            b = start("pos")
            mm(b[:, 0:NE], con("incl"), sel[:, 0, :], start=True, stop=True)
            mm(b[:, NE:2 * NE], con("incl"), sel[:, 1, :], start=True, stop=False)
            ring.mark_filled(mm(b[:, NE:2 * NE], con("ones"), sel[:, 0, :], start=False, stop=True))
            pe.wait_ge(S("posm_ready"), 1)
            b = start("pgT")
            for j, x in enumerate((posm, gate)):
                for a in range(2):
                    o = 256 * j + P * a
                    ins = transposed(b[0:NE, o:o + P], x[:, a, :])
            ring.mark_filled(ins)
            b = start("cnt")
            for a in range(2):
                ins = mm(b[0:NE, 0:1], sel[:, a, :], con("ones")[:, 0:1], start=(a == 0), stop=(a == 1))
            ring.mark_filled(ins)
            pe.wait_ge(S("nb_ready"), 1)
            ne = slice(0, NE)
            ring.mark_filled(mm(start("start")[0:NE, 0:1], con("strict", NE), nb[ne, 0:1], start=True, stop=True))
            pe.wait_ge(S("E_ready"), 1)
            b = start("it0")
            for a in range(2):
                mm(b[:, NI * a:NI * (a + 1)], posT[ne, P * a:P * (a + 1)], Em[ne, :], start=True, stop=False)
                mm(b[:, NI * a:NI * (a + 1)], con("ones", NE), Eb[ne, :], start=False, stop=True)
            for a in range(2):
                ins = mm(b[:, NI * (2 + a):NI * (3 + a)], gatT[ne, P * a:P * (a + 1)], Em[ne, :], start=True, stop=True)
            ring.mark_filled(ins)
            b = start("ids")
            mm(b[0:1, 0:NI], con("evec", NE), Em[ne, :], start=True, stop=True)
            ring.mark_filled(mm(b[0:1, NI:NI + 1], nb[ne, 0:1], con("ones", NE)[:, 0:1], start=True, stop=True))
            pe.wait_ge(S("bias_in"), 32)
            for name in ring.names[-8:]:
                ring.wait_emptied(pe, name)
            n_items = pe.value_load(ids[0:1, NI:NI + 1], min_val=2, max_val=NI - 2)
            halves = [slice(CAP * h, CAP * (h + 1)) for h in range(2)]

            def gather(count):
                pe.wait_ge(S("s_ready"), count)
                for j in range(KT):
                    for a in range(2):
                        ins = mm(psum[:, 3, CAP * j:CAP * (j + 1)], h2TM[:, a, P * j:P * (j + 1)], Ssel[:, a, :],
                                 start=(a == 0), stop=(a == 1))
                ins.then_inc(S("g_full"), 1)

            def turn_gates(count):
                pe.wait_ge(S("sgat_ready"), count)
                for a in range(2):
                    ins = transposed(psum[:, 2, P * a:P * (a + 1)], Sgat[:, a, :])
                ins.then_inc(S("gt_full"), 1)

            def scatter(count):
                pe.wait_ge(S("y_ready"), count)
                pe.wait_ge(S("gt_ready"), count)
                for k in range(KT // 2):
                    for h, q in enumerate(halves):
                        ins = mm(facc[:, 4 * h + k, :], ey[q, P * k:P * (k + 1)], GT[q, :], start=False, stop=False,
                                 skip_group_check=True)
                ins.then_inc(S("sc_full"), 1)

            pe.sem_inc(S("sc_full"), 1)
            gather(1)
            for k in range(KT):
                mm(facc[:, k, :], bdn[:, P * k:P * (k + 1)], gatT[ne, :], start=(k % 2 == 0), stop=False,
                   skip_group_check=True)

            with pe.Fori(0, n_items) as it:
                turn_gates(it + 1)
                pe.wait_ge(S("Ecol_ready"), it + 1)
                pe.wait_ge(S("hg_ready"), it + 1)
                pe.wait_ge(S("gu_emptied"), it + 1)
                for b_ in range(2):
                    for h, q in enumerate(halves):
                        mm(psum[q, b_, :], Ecol,
                           bgu[:, 1024 * h + 512 * b_:1024 * h + 512 * (b_ + 1)], start=True, stop=False,
                           skip_group_check=True)
                for c in range(KT):
                    pe.wait_ge(loaded[c], 16 * it + 16 * (uses[c] + 1))
                    for b_ in range(2):
                        for h, q in enumerate(halves):
                            ins = mm(psum[q, b_, :], hg[:, c, :],
                                     slot(c)[:, 1024 * h + 512 * b_:1024 * h + 512 * (b_ + 1)], start=False,
                                     stop=(c == KT - 1), skip_group_check=True)
                    ins.then_inc(slot_read if c < KT - 1 else S("gu_full"), 1)
                pe.wait_ge(S("y_ready"), it + 1)
                gather(it + 2)
                scatter(it + 1)
                pe.wait_ge(S("act_ready"), it + 1)
                for i in range(4):
                    ins = transposed(psum[:, 2, P * i:P * (i + 1)], eu[:, P * i:P * (i + 1)])
                ins.then_inc(S("at_full"), 1)
                pe.wait_ge(S("aT_ready"), it + 1)
                pe.wait_ge(S("hg_ready"), it + 2)
                for c in range(4):
                    pe.wait_ge(loaded[8 + c], 16 * it + 16)
                    for a in range(2):
                        j = 2 * c + a
                        for h, q in enumerate(halves):
                            ins = mm(psum[q, 3, :], aT[:, j % 4, j // 4, :],
                                     slot(8 + c)[:, 1024 * a + 512 * h:1024 * a + 512 * (h + 1)], start=(j == 0),
                                     stop=(j == KT - 1), skip_group_check=True)
                    ins.then_inc(slot_read if c < 3 else S("d_full"), 1)
            turn_gates(n_items + 1)
            scatter(n_items + 1)

            for k in range(KT):
                pe.wait_ge(S("x3_ready"), k + 1)
                for a in range(2):
                    ins = transposed(psum[:, 2 * a + k // 4, P * (k % 4):P * (k % 4 + 1)], xT[:, k, P * a:P * (a + 1)])
                    if k == KT - 1:
                        ins.then_inc(S("fin_full"), 1)


_INS = ['x', 'c', 'ctx', 'c_ctx', 'ada_w', 'ada_b', 'norm_mix_g', 'norm_ffn_g', 'w_in', 'w_out', 'four_w', 's5_lam_re',
        's5_lam_im', 's5_log_dt', 's5_b_re', 's5_b_im', 's5_c_re', 's5_c_im', 's5_d', 's5_w_glu', 'gla_a2', 'gla_a_b',
        'gla_norm_g', 'ssd_conv_w', 'ssd_conv_b', 'ssd_a_log', 'ssd_dt_bias', 'ssd_d', 'ssd_norm_g', 'router_w',
        'router_b', 'exp_w_gu', 'exp_b_gu', 'exp_w_dn', 'exp_b_dn', 'final_g']


def kernel(**inputs):
    import numpy as _np
    import concourse.bacc as _bacc
    from concourse import mybir as _mybir
    from concourse.bass_utils import run_bass_kernel_spmd as _run

    nc = _bacc.Bacc("TRN2", target_bir_lowering=False, num_devices=1)
    arrays, handles = {}, {}
    for name in _INS:
        a = _np.ascontiguousarray(inputs[name])
        arrays[f"in_{name}_dram"] = a
        handles[name] = nc.dram_tensor(f"in_{name}_dram", a.shape, _mybir.dt.from_np(a.dtype),
                                       kind="ExternalInput").ap()
    arrays["const_dram"] = shape_constants()
    handles["const"] = nc.dram_tensor("const_dram", (P, NCONST), F32, kind="ExternalInput").ap()
    out = nc.dram_tensor("out_dram", (1, NLAT, D), F32, kind="ExternalOutput").ap()
    backbone(nc, handles, out)
    r = _run(nc, [arrays], core_ids=[0])
    return r.results[0]["out_dram"]
```
